# Optimizing a Trainium2 kernel written in Bass

```python
import jax, jax.numpy as jnp
from jax import lax
import numpy as np

D_MODEL = 1024
BATCH = 1
SEQ = 1024
DEPTH = 2

D_PLE = 256
N_MIXERS = 2
GDN_HEADS = 8
GDN_DK = 128
GDN_DV = 128
GDN_CONV = 4
GDN_CHUNK = 64
GDN_QK = GDN_HEADS * GDN_DK
GDN_V = GDN_HEADS * GDN_DV
GDN_IN = 2 * GDN_QK + 2 * GDN_V + 2 * GDN_HEADS
FOX_HEADS = 16
FOX_DH = 64
FOX_BLOCK = 128
FOX_W = FOX_HEADS * FOX_DH
FOX_IN = 4 * FOX_W + FOX_HEADS
N_GDN = (DEPTH + 1) // 2
N_FOX = DEPTH // 2
DN_ALPHA = (2 * DEPTH) ** 0.25
DN_BETA = (8 * DEPTH) ** -0.25
LN_EPS = 1e-5
RMS_EPS = 1e-6

kernel_name = 'hybrid_gdn_fox_deepnorm_ple'

F32 = jnp.float32

def layer_norm(x, g, b):
    xf = x.astype(F32)
    mu = jnp.mean(xf, -1, keepdims=True)
    var = jnp.mean(jnp.square(xf - mu), -1, keepdims=True)
    return ((xf - mu) * lax.rsqrt(var + LN_EPS) * g + b).astype(x.dtype)

def rms_norm(x, g):
    xf = x.astype(F32)
    return (xf * lax.rsqrt(jnp.mean(xf * xf, -1, keepdims=True) + RMS_EPS) * g).astype(x.dtype)

def l2_normalize(x):
    xf = x.astype(F32)
    return xf * lax.rsqrt(jnp.sum(xf * xf, -1, keepdims=True) + RMS_EPS)

def causal_depthwise_conv(x, w):
    K, C = w.shape
    return lax.conv_general_dilated(x, w[:, None, :].astype(x.dtype), window_strides=(1,),
                                    padding=[(K - 1, 0)], dimension_numbers=('NWC', 'WIO', 'NWC'),
                                    feature_group_count=C)

def gated_delta_rule(q, k, v, beta, g):
    B, S, H, dk = q.shape
    dv = v.shape[-1]
    C = GDN_CHUNK
    N = S // C

    def to_chunks(t):
        return t.astype(F32).reshape(B, N, C, H, *t.shape[3:]).swapaxes(2, 3)

    q = to_chunks(q) * (dk ** -0.5)
    k = to_chunks(k)
    v = to_chunks(v)
    beta = to_chunks(beta)
    g = jnp.cumsum(to_chunks(g), axis=-1)
    causal = jnp.tril(jnp.ones((C, C), bool))
    strict = jnp.tril(jnp.ones((C, C), bool), -1)
    decay = jnp.exp(jnp.where(causal, g[..., :, None] - g[..., None, :], -jnp.inf))
    kb = k * beta[..., None]
    L = jnp.where(strict, jnp.einsum('bnhid,bnhjd->bnhij', kb, k) * decay, 0.0)
    eye = jnp.eye(C, dtype=F32)
    rhs = jnp.concatenate([v * beta[..., None], kb * jnp.exp(g)[..., None]], axis=-1)
    sol = lax.linalg.triangular_solve(eye + L, rhs, left_side=True, lower=True, unit_diagonal=True)
    u, w = sol[..., :dv], sol[..., dv:]
    a_qk = jnp.where(causal, jnp.einsum('bnhid,bnhjd->bnhij', q, k) * decay, 0.0)
    q_dec = q * jnp.exp(g)[..., None]
    k_dec = k * jnp.exp(g[..., -1:] - g)[..., None]
    g_last = jnp.exp(g[..., -1])

    def step(state, xs):
        q_c, k_c, u_c, w_c, a_c, gl = xs
        v_new = u_c - jnp.einsum('bhcd,bhde->bhce', w_c, state)
        o_c = jnp.einsum('bhcd,bhde->bhce', q_c, state) + jnp.einsum('bhij,bhje->bhie', a_c, v_new)
        state = state * gl[..., None, None] + jnp.einsum('bhcd,bhce->bhde', k_c, v_new)
        return state, o_c

    xs = tuple(jnp.moveaxis(t, 1, 0) for t in (q_dec, k_dec, u, w, a_qk, g_last))
    s0 = jnp.zeros((B, H, dk, dv), F32)
    _, o = lax.scan(step, s0, xs)
    return o.transpose(1, 0, 3, 2, 4).reshape(B, S, H, dv)

def gdn_mixer(x, w_in, conv_w, a_log, dt_bias, norm_g, w_out):
    B, S, _ = x.shape
    h = x @ w_in
    qkv, z, b_raw, a_raw = jnp.split(h, [2 * GDN_QK + GDN_V, 2 * GDN_QK + 2 * GDN_V,
                                         2 * GDN_QK + 2 * GDN_V + GDN_HEADS], axis=-1)
    qkv = jax.nn.silu(causal_depthwise_conv(qkv, conv_w))
    q, k, v = jnp.split(qkv, [GDN_QK, 2 * GDN_QK], axis=-1)
    q = l2_normalize(q.reshape(B, S, GDN_HEADS, GDN_DK))
    k = l2_normalize(k.reshape(B, S, GDN_HEADS, GDN_DK))
    v = v.reshape(B, S, GDN_HEADS, GDN_DV)
    beta = jax.nn.sigmoid(b_raw.astype(F32))
    g = -jnp.exp(a_log.astype(F32)) * jax.nn.softplus(a_raw.astype(F32) + dt_bias.astype(F32))
    o = gated_delta_rule(q, k, v, beta, g)
    o = rms_norm(o, norm_g) * jax.nn.silu(z.reshape(B, S, GDN_HEADS, GDN_DV).astype(F32))
    return o.reshape(B, S, GDN_V).astype(x.dtype) @ w_out

def forgetting_attention(q, k, v, c):
    B, S, H, Dh = q.shape
    nb = S // FOX_BLOCK
    kf = k.astype(F32)
    vf = v.astype(F32)
    c_t = c.transpose(0, 2, 1)
    q_blocks = (q.astype(F32) * (Dh ** -0.5)).reshape(B, nb, FOX_BLOCK, H, Dh).transpose(1, 0, 3, 2, 4)
    c_blocks = c_t.reshape(B, H, nb, FOX_BLOCK).transpose(2, 0, 1, 3)
    key_pos = jnp.arange(S)

    def one_block(args):
        qb, cb, blk = args
        logits = jnp.einsum('bhtd,bshd->bhts', qb, kf) + cb[..., None] - c_t[:, :, None, :]
        q_pos = blk * FOX_BLOCK + jnp.arange(FOX_BLOCK)
        logits = jnp.where(key_pos[None, :] <= q_pos[:, None], logits, -jnp.inf)
        probs = jax.nn.softmax(logits, axis=-1)
        return jnp.einsum('bhts,bshd->bthd', probs, vf)

    o = lax.map(one_block, (q_blocks, c_blocks, jnp.arange(nb)))
    return o.transpose(1, 0, 2, 3, 4).reshape(B, S, H, Dh)

def fox_mixer(x, w_in, b_f, q_norm_g, k_norm_g, w_out):
    B, S, _ = x.shape
    h = x @ w_in
    q, k, v, z, f_raw = jnp.split(h, [FOX_W, 2 * FOX_W, 3 * FOX_W, 4 * FOX_W], axis=-1)
    q = rms_norm(q.reshape(B, S, FOX_HEADS, FOX_DH), q_norm_g)
    k = rms_norm(k.reshape(B, S, FOX_HEADS, FOX_DH), k_norm_g)
    v = v.reshape(B, S, FOX_HEADS, FOX_DH)
    log_f = jax.nn.log_sigmoid(f_raw.astype(F32) + b_f.astype(F32))
    c = jnp.cumsum(log_f, axis=1)
    o = forgetting_attention(q, k, v, c)
    o = o * jax.nn.silu(z.reshape(B, S, FOX_HEADS, FOX_DH).astype(F32))
    return o.reshape(B, S, FOX_W).astype(x.dtype) @ w_out

def setup_inputs(seed: int = 0) -> dict:
    key = jax.random.key(seed)
    ks = jax.random.split(key, 20)
    nrm = jax.random.normal
    x = nrm(ks[0], (BATCH, SEQ, D_MODEL), F32)
    p = nrm(ks[1], (DEPTH, BATCH, SEQ, D_PLE), F32)
    ln_g = 1.0 + 0.02 * nrm(ks[2], (DEPTH, D_MODEL), F32)
    ln_b = 0.02 * nrm(ks[3], (DEPTH, D_MODEL), F32)
    ple_w_gate = nrm(ks[4], (DEPTH, D_MODEL, D_MODEL), F32) * D_MODEL ** -0.5
    ple_w_proj = nrm(ks[5], (DEPTH, D_PLE, D_MODEL), F32) * D_PLE ** -0.5
    gdn_w_in = nrm(ks[6], (N_GDN, D_MODEL, GDN_IN), F32) * D_MODEL ** -0.5
    gdn_conv_w = nrm(ks[7], (N_GDN, GDN_CONV, 2 * GDN_QK + GDN_V), F32) * GDN_CONV ** -0.5
    gdn_a_log = jnp.log(jax.random.uniform(ks[8], (N_GDN, GDN_HEADS), F32, 1.0, 16.0))
    dt = jnp.exp(jax.random.uniform(ks[9], (N_GDN, GDN_HEADS), F32, np.log(1e-3), np.log(1e-1)))
    gdn_dt_bias = dt + jnp.log(-jnp.expm1(-dt))
    gdn_norm_g = 1.0 + 0.02 * nrm(ks[10], (N_GDN, GDN_DV), F32)
    gdn_w_out = nrm(ks[11], (N_GDN, GDN_V, D_MODEL), F32) * (GDN_V ** -0.5) * DN_BETA
    fox_w_in = nrm(ks[12], (N_FOX, D_MODEL, FOX_IN), F32) * D_MODEL ** -0.5
    fox_b_f = jax.random.uniform(ks[13], (N_FOX, FOX_HEADS), F32, 1.0, 5.0)
    fox_q_norm_g = 1.0 + 0.02 * nrm(ks[14], (N_FOX, FOX_DH), F32)
    fox_k_norm_g = 1.0 + 0.02 * nrm(ks[15], (N_FOX, FOX_DH), F32)
    fox_w_out = nrm(ks[16], (N_FOX, FOX_W, D_MODEL), F32) * (FOX_W ** -0.5) * DN_BETA
    return {'x': x, 'p': p, 'ln_g': ln_g, 'ln_b': ln_b, 'ple_w_gate': ple_w_gate,
            'ple_w_proj': ple_w_proj, 'gdn_w_in': gdn_w_in, 'gdn_conv_w': gdn_conv_w,
            'gdn_a_log': gdn_a_log, 'gdn_dt_bias': gdn_dt_bias, 'gdn_norm_g': gdn_norm_g,
            'gdn_w_out': gdn_w_out, 'fox_w_in': fox_w_in, 'fox_b_f': fox_b_f,
            'fox_q_norm_g': fox_q_norm_g, 'fox_k_norm_g': fox_k_norm_g, 'fox_w_out': fox_w_out}

def reference(x, p, ln_g, ln_b, ple_w_gate, ple_w_proj, gdn_w_in, gdn_conv_w, gdn_a_log,
              gdn_dt_bias, gdn_norm_g, gdn_w_out, fox_w_in, fox_b_f, fox_q_norm_g,
              fox_k_norm_g, fox_w_out):
    for i in range(DEPTH):
        j = i // N_MIXERS
        if i % N_MIXERS == 0:
            y = gdn_mixer(x, gdn_w_in[j], gdn_conv_w[j], gdn_a_log[j], gdn_dt_bias[j],
                          gdn_norm_g[j], gdn_w_out[j])
        else:
            y = fox_mixer(x, fox_w_in[j], fox_b_f[j], fox_q_norm_g[j], fox_k_norm_g[j],
                          fox_w_out[j])
        x = layer_norm(DN_ALPHA * x + y, ln_g[i], ln_b[i])
        gate = jax.nn.sigmoid((x @ ple_w_gate[i]).astype(F32))
        x = x + (gate * (p[i] @ ple_w_proj[i]).astype(F32)).astype(x.dtype)
    return x


_drawn_inputs = setup_inputs


def setup_inputs(seed=0):
    import zlib

    import numpy as np

    out = dict(_drawn_inputs(seed))
    spreads = {}
    factors = {'gdn_norm_g': 8.0, 'fox_q_norm_g': 8.0, 'fox_k_norm_g': 8.0}
    for name, (base, spread) in spreads.items():
        noise = np.random.default_rng([zlib.crc32(name.encode()), seed]).standard_normal(out[name].shape)
        drawn = base * np.exp(spread * noise) if base else spread * noise
        out[name] = __import__('jax').numpy.asarray(drawn.astype(out[name].dtype))
    for name, factor in factors.items():
        out[name] = (out[name] * factor).astype(out[name].dtype)
    return out
```

```python
import numpy as np
from contextlib import ExitStack

import concourse.bass as bass
from concourse import mybir

F32 = mybir.dt.float32
F32R = mybir.dt.float32r
ALU = mybir.AluOpType
ACT = mybir.ActivationFunctionType

P = 128
D = 1024
T = 1024
KT = D // P
NT = T // P
HALF = 512
H = 8
DK = 128
TAPS = 4
BIG = 1e30
RMS_EPS = 1e-6
LN_EPS = 1e-5
ALPHA = float((2 * 2) ** 0.25)
LEVELS = 6


class Phase(ExitStack):

    def __init__(self, nc, name):
        super().__init__()
        self.nc, self.name, self.semaphores = nc, name, []
        self.callback(self.clear)

    def sb(self, name, shape, dtype=F32):
        return self.enter_context(self.nc.sbuf_tensor(f"{self.name}_{name}", shape, dtype))

    def ps(self, name, shape):
        return self.enter_context(self.nc.psum_tensor(f"{self.name}_{name}", shape, F32))

    def sem(self, name):
        self.semaphores.append(self.nc.alloc_semaphore(f"{self.name}_{name}"))
        return self.semaphores[-1]

    def clear(self):
        self.nc.clear_and_free_semaphores(self.semaphores)
        self.nc.all_engine_barrier()


class Step:

    def __init__(self, engine, own):
        self.engine, self.own, self.value = engine, own, {}

    def __call__(self, instruction, signal=None):
        sem = self.own if signal is None else signal
        self.value[sem] = self.value.get(sem, 0) + 1
        instruction.then_inc(sem, 1)
        self.engine.wait_ge(sem, self.value[sem])


def constants_program(pool, step, c):
    def select(ap, compare, fill, base, pattern, multiplier):
        step(pool.affine_select(out=ap, in_=ap, compare_op=compare, fill=fill, base=base,
                                pattern=pattern, channel_multiplier=multiplier))

    step(pool.memset(c["ident"][:], 0.0))
    select(c["ident"][:], ALU.not_equal, 1.0, 0, [[-1, P]], 1)
    step(pool.memset(c["tri"][:], 1.0))
    select(c["tri"][:], ALU.is_ge, 0.0, 0, [[1, P]], -1)
    step(pool.memset(c["ones"][:], 1.0))
    step(pool.memset(c["above_big"][:], 0.0))
    select(c["above_big"][:], ALU.is_ge, BIG, 0, [[-1, P]], 1)
    step(pool.memset(c["below_neg"][:], 0.0))
    select(c["below_neg"][:], ALU.is_ge, -BIG, 0, [[1, P]], -1)
    step(pool.memset(c["odd_below"][:], 0.0))
    view = c["odd_below"][:].rearrange("p (n two) -> p n two", two=2)[:, :, 0]
    step(pool.affine_select(out=view, in_=view, compare_op=ALU.not_equal, fill=-1.0, base=-1,
                            pattern=[[-2, P // 2]], channel_multiplier=1))
    for level in range(LEVELS):
        s = 2 << level
        nb = P // (2 * s)
        m = c["level_mask"][:, level, :]
        step(pool.memset(m, -1.0))
        select(m, ALU.is_ge, 0.0, 0, [[-2 * s, nb], [0, s]], 1)
        select(m, ALU.is_ge, 0.0, s - 1, [[2 * s, nb], [0, s]], -1)


def right_halves(ap, level):
    return ap.rearrange("p (n two s) -> p n two s", two=2, s=2 << level)[:, :, 1, :]


def as_blocks(ap, level):
    return ap.rearrange("p (n s) -> p n s", s=2 << level)


def transpose_input(nc, x, c, xh, xl, w_gate, gates, g_rows_dram):
    with Phase(nc, "in") as ph:
        sb, ps, sem = ph.sb, ph.ps, ph.sem
        x_tile = sb("x_tile", [P, 2, D])
        ab_raw = sb("ab_raw", [P, KT, 2 * H])
        ab_hi = sb("ab_hi", [P, KT, 2 * H], F32R)
        ab_lo = sb("ab_lo", [P, KT, 2 * H], F32R)
        dt_bias = sb("dt_bias", [P, H])
        a_log = sb("a_log", [P, H])
        work = [sb(f"gate_work{n}", [P, NT, H]) for n in range(6)]
        g_rows = sb("g_rows", [NT * H, P])
        turned = [ps(f"turned{n}", [P, HALF]) for n in range(2)]
        ab = ps("ab", [P, NT, 2 * H])
        cums = ps("cums", [P, HALF])
        totals = ps("totals", [P, HALF])
        rows = ps("rows", [P, HALF])

        x_loaded = [sem(f"x_loaded{n}") for n in range(2)]
        small_loaded = sem("small_loaded")
        pool_step, act_step, dve_step = sem("in_pool_step"), sem("in_act_step"), sem("in_dve_step")
        constants_made = sem("constants_made")
        x_turned, high_made, low_made = sem("x_turned"), sem("high_made"), sem("low_made")
        gate_high, gate_low, ab_made = sem("gate_high"), sem("gate_low"), sem("ab_made")
        exp_beta, exp_alpha, g_made = sem("exp_beta"), sem("exp_alpha"), sem("g_made")
        g_summed, g_copied, g_turned, g_out = sem("g_summed"), sem("g_copied"), sem("g_turned"), sem("g_out")
        rows_made = sem("rows_made")
        decays_made, e_made = sem("decays_made"), sem("e_made")
        block = ph.enter_context(nc.Block())

        @block.sync
        def _(sp):
            for t in range(NT):
                if t >= 2:
                    sp.wait_ge(x_turned, 2 * (t - 1))
                sp.dma_start(x_tile[:, t % 2, :], x[0, t * P:(t + 1) * P, :]).then_inc(x_loaded[t % 2], 16)
                if t == 1:
                    sp.dma_start(ab_raw[:], w_gate["ab"].rearrange("(k p) n -> p k n", p=P)).then_inc(small_loaded, 16)
                    sp.dma_start(dt_bias[:], w_gate["dt_bias"].partition_broadcast(P)).then_inc(small_loaded, 16)
                    sp.dma_start(a_log[:], w_gate["a_log"].partition_broadcast(P)).then_inc(small_loaded, 16)
            sp.wait_ge(rows_made, 1)
            sp.dma_start(g_rows_dram, g_rows[:]).then_inc(g_out, 16)
            sp.wait_ge(g_out, 16)

        @block.gpsimd
        def _(pool):
            step = Step(pool, pool_step)
            constants_program(pool, step, c)
            step(pool.memset(c["ones"][:], 1.0), constants_made)

        @block.tensor
        def _(pe):
            pe.wait_ge(constants_made, 1)
            for t in range(NT):
                pe.wait_ge(x_loaded[t % 2], 16 * (t // 2 + 1))
                for half in range(2):
                    n = 2 * t + half
                    if n >= 2:
                        pe.wait_ge(low_made, n - 1)
                    for j in range(4):
                        k = 4 * half + j
                        mm = pe.transpose(turned[half][:, j * P:(j + 1) * P],
                                          x_tile[:, t % 2, k * P:(k + 1) * P], c["ident"][:])
                    mm.then_inc(x_turned, 1)
            pe.wait_ge(gate_low, 1)
            pe.wait_ge(low_made, 2 * NT)
            for t in range(NT):
                for k in range(KT):
                    ts = slice(t * P, (t + 1) * P)
                    pe.matmul(ab[:, t, :], xh[:, k, ts], ab_hi[:, k, :], start=(k == 0), stop=False)
                    pe.matmul(ab[:, t, :], xh[:, k, ts], ab_lo[:, k, :], start=False, stop=False)
                    mm = pe.matmul(ab[:, t, :], xl[:, k, ts], ab_hi[:, k, :], start=False, stop=(k == KT - 1))
            mm.then_inc(ab_made, 1)
            pe.wait_ge(g_made, 1)
            g = work[5][:].rearrange("p c h -> p (c h)")
            pe.matmul(cums[:, 0:NT * H], c["tri"][:], g, start=True, stop=True)
            pe.matmul(totals[:, 0:NT * H], c["ones"][:], g, start=True, stop=True).then_inc(g_summed, 1)
            pe.wait_ge(g_copied, 1)
            pe.transpose(rows[0:NT * H, 0:P], gates["g"][:].rearrange("p c h -> p (c h)"),
                         c["ident"][:]).then_inc(g_turned, 1)

        @block.scalar
        def _(act):
            step = Step(act, act_step)
            for n in range(2 * NT):
                t, half = n // 2, n % 2
                act.wait_ge(x_turned, n + 1)
                src = turned[half][:].rearrange("p (j t) -> p j t", j=4)
                step(act.activation(xh[:, 4 * half:4 * half + 4, t * P:(t + 1) * P], src, ACT.Copy), high_made)
                if n == 4:
                    act.wait_ge(small_loaded, 48)
                    step(act.activation(ab_hi[:], ab_raw[:], ACT.Copy), gate_high)
            act.wait_ge(ab_made, 1)
            step(act.activation(work[0][:], ab[:, :, 0:H], ACT.Exp, scale=-1.0), exp_beta)
            act.wait_ge(decays_made, 1)
            step(act.activation(work[2][:], work[1][:], ACT.Exp))
            step(act.activation(a_log[:], a_log[:], ACT.Exp), exp_alpha)
            act.wait_ge(g_copied, 2)
            step(act.activation(gates["neg_beta_eg"][:], gates["g"][:], ACT.Exp))
            step(act.activation(gates["k_decay"][:], work[0][:], ACT.Exp))
            step(act.activation(gates["last"][:], totals[:, 0:NT * H].rearrange("p (c h) -> p c h", h=H), ACT.Exp))
            act.wait_ge(g_turned, 1)
            step(act.activation(g_rows[:], rows[0:NT * H, 0:P], ACT.Copy), rows_made)
            step(act.activation(work[4][:], work[0][:], ACT.Copy), e_made)

        @block.vector
        def _(dve):
            step = Step(dve, dve_step)
            for n in range(2 * NT):
                t, half = n // 2, n % 2
                dve.wait_ge(high_made, n + 1)
                src = turned[half][:].rearrange("p (j t) -> p j t", j=4)
                where = (slice(None), slice(4 * half, 4 * half + 4), slice(t * P, (t + 1) * P))
                step(dve.tensor_tensor(xl[where], src, xh[where].bitcast(F32), ALU.subtract), low_made)
                if n == 5:
                    dve.wait_ge(gate_high, 1)
                    step(dve.tensor_tensor(ab_lo[:], ab_raw[:], ab_hi[:].bitcast(F32), ALU.subtract), gate_low)
            bias = dt_bias[:].unsqueeze(1).to_broadcast([P, NT, H])
            dve.wait_ge(exp_beta, 1)
            step(dve.tensor_scalar(work[0][:], work[0][:], 1.0, None, ALU.add))
            step(dve.reciprocal(gates["beta"][:], work[0][:]))
            step(dve.tensor_tensor(work[3][:], ab[:, :, H:2 * H], bias, ALU.add))
            step(dve.scalar_tensor_tensor(work[1][:], work[3][:], -1.0, work[3][:], ALU.mult, ALU.min), decays_made)
            dve.wait_ge(exp_alpha, 1)
            log_one_plus(dve, step, work[2], work[1], work[4], work[0])
            step(dve.scalar_tensor_tensor(work[0][:], work[3][:], 0.0, work[1][:], ALU.max, ALU.add))
            step(dve.scalar_tensor_tensor(work[5][:], work[0][:], -1.0,
                                          a_log[:].unsqueeze(1).to_broadcast([P, NT, H]),
                                          ALU.mult, ALU.mult), g_made)
            dve.wait_ge(g_summed, 1)
            summed = cums[:, 0:NT * H].rearrange("p (c h) -> p c h", h=H)
            total = totals[:, 0:NT * H].rearrange("p (c h) -> p c h", h=H)
            step(dve.tensor_copy(gates["g"][:], summed), g_copied)
            step(dve.tensor_tensor(work[0][:], total, gates["g"][:], ALU.subtract), g_copied)
            dve.wait_ge(e_made, 1)
            step(dve.scalar_tensor_tensor(gates["neg_beta_eg"][:], gates["neg_beta_eg"][:], -1.0,
                                          gates["beta"][:], ALU.mult, ALU.mult))


def log_one_plus(dve, step, y, out, z2, series):
    step(dve.tensor_scalar(z2[:], y[:], 2.0, None, ALU.add))
    step(dve.reciprocal(out[:], z2[:]))
    step(dve.tensor_tensor(y[:], y[:], out[:], ALU.mult))
    step(dve.tensor_tensor(z2[:], y[:], y[:], ALU.mult))
    step(dve.tensor_scalar(series[:], z2[:], 2.0 / 17, None, ALU.mult))
    for odd in (15, 13, 11, 9, 7, 5, 3):
        step(dve.scalar_tensor_tensor(series[:], series[:], 2.0 / odd, z2[:], ALU.add, ALU.mult))
    step(dve.scalar_tensor_tensor(out[:], series[:], 2.0, y[:], ALU.add, ALU.mult))


STEPS = 8 * KT
AT_VALUES = 3
AT_NORMS = 6
AT_KEYS = 14
AT_KK = 15
AT_QK = 17
AT_FIRST = 20
AT_LEVELS = 22
AT_CHUNKS = 40


def delta_net(nc, c, xh, xl, gates, w_in, conv_w, norm_g, g_rows_dram, qkvz_space, o_t):
    with Phase(nc, "gdn") as ph:
        sb, ps, sem = ph.sb, ph.ps, ph.sem
        w_raw = sb("w_raw", [P, 2, KT, P])
        w_hi = sb("w_hi", [P, 2, KT, P], F32R)
        w_lo = sb("w_lo", [P, 2, KT, P], F32R)
        raw = sb("raw", [P, 2, TAPS - 1 + T])
        qkvz = qkvz_space[:].rearrange("p (b n) t -> p b n t", b=2)
        g_rows = sb("g_bc", [P, 2, T])
        lower = sb("lower", [P, T])
        inv = sb("inv", [P, T])
        inv_t = sb("inv_t", [P, T])
        att_t = sb("att_t", [P, T])
        y = sb("y", [P, 2, T // 4])
        k_rows = sb("k_rows", [P, T])
        v_rows = sb("v_rows", [P, T])
        eg = sb("eg", [P, T])
        rest = sb("rest", [P, P])
        v_new = sb("v_new", [P, P])
        state = sb("state", [P, 2, P])
        taps = sb("taps", [P, TAPS, 3 * H])
        gain = sb("gain", [P, 1])
        eps = sb("gdn_eps", [P, 1])
        unit = [ps(f"unit{n}", [P, HALF]) for n in range(2)]
        w0, w1, w2 = ps("w0", [P, T]), ps("w1", [P, T]), ps("w2", [P, T])

        w_loaded = [sem(f"w_loaded{n}") for n in range(2)]
        g_loaded = [sem(f"g_loaded{n}") for n in range(2)]
        small = sem("taps_loaded")
        pool_step, act_step, dve_step = sem("gdn_pool_step"), sem("gdn_act_step"), sem("gdn_dve_step")
        w_high, w_low = sem("w_high"), sem("w_low")
        unit_made, unit_taken, conv_made = sem("unit_made"), sem("unit_taken"), sem("conv_made")
        z_ready, v_ready, squared = sem("z_ready"), sem("v_ready"), sem("squared")
        v_turned, bv_made = sem("v_turned"), sem("bv_made")
        o_squared, o_summed, o_rms, o_done = sem("o_squared"), sem("o_summed"), sem("o_rms"), sem("o_done")
        q_summed, k_summed, norms, normed = sem("q_summed"), sem("k_summed"), sem("norms"), sem("normed")
        exponents, decays, eg_made = sem("exponents"), sem("decays"), sem("eg_made")
        k_turned, kd_made = sem("k_turned"), sem("kd_made")
        kk_made, lower_made, qk_made, att_made = sem("kk_made"), sem("lower_made"), sem("qk_made"), sem("att_made")
        q_decayed, inv2_made, inv2_turned, inv2_copied = sem("q_decayed"), sem("inv2_made"), sem("inv2_turned"), sem("inv2_copied")
        y_product, y_made, x_product, x_made = sem("y_product"), sem("y_made"), sem("x_product"), sem("x_made")
        t_turned, t_copied = sem("t_turned"), sem("t_copied")
        ks_made, rest_made, tr_made, vn_made = sem("ks_made"), sem("rest_made"), sem("tr_made"), sem("vn_made")
        ds_made, s_made, o_made, o_taken = sem("ds_made"), sem("s_made"), sem("o_made"), sem("o_taken")
        block = ph.enter_context(nc.Block())

        def columns(j):
            head, kind = j // 4, j % 4
            return slice(kind * H * DK + head * DK, kind * H * DK + (head + 1) * DK)

        def chunk(n):
            return slice(n * P, (n + 1) * P)

        @block.sync
        def _(sp):
            def load(j):
                if j >= 2:
                    sp.wait_ge(w_low, j - 1)
                sp.dma_start(w_raw[:, j % 2], w_in[:, columns(j)].rearrange("(k p) n -> p k n", p=P)
                             ).then_inc(w_loaded[j % 2], 16)

            load(0)
            with nc.allow_non_contiguous_dma(reason="the taps of a channel on its partition"):
                for tap in range(TAPS):
                    sp.dma_start(taps[:, tap], conv_w[tap].rearrange("(b p) -> p b", p=P)).then_inc(small, 16)
                sp.dma_start(gain[:], norm_g.rearrange("(p n) -> p n", n=1)).then_inc(small, 16)
            load(1)
            for it in range(H + 1):
                p = it - 1
                if p >= 0:
                    if p >= 2:
                        sp.wait_ge(eg_made, p - 1)
                    rows = g_rows_dram.rearrange("(c h) t -> h c t", h=H)[p]
                    sp.dma_start(g_rows[:, p % 2].rearrange("p (c t) -> p c t", c=NT),
                                 rows.partition_broadcast(P)).then_inc(g_loaded[p % 2], 16)
                for b in range(4):
                    j = 4 * it + b + 2
                    if it < H and j < 4 * H:
                        load(j)

        @block.gpsimd
        def _(pool):
            step = Step(pool, pool_step)

            def low_part(j):
                pool.wait_ge(w_high, j + 1)
                step(pool.tensor_tensor(w_lo[:, j % 2], w_raw[:, j % 2], w_hi[:, j % 2].bitcast(F32),
                                        ALU.subtract), w_low)

            low_part(0)
            for it in range(H + 2):
                p = it - 1
                for s in range(STEPS):
                    if it < H and s % 16 == 4 and 4 * it + s // 16 + 1 < 4 * H:
                        low_part(4 * it + s // 16 + 1)
                    if 0 <= p < H and s == AT_QK:
                        pool.wait_ge(qk_made, p + 1)
                        pool.wait_ge(eg_made, p + 1)
                        q = qkvz[:, p % 2, 0]
                        step(pool.tensor_tensor(q, q, eg[:], ALU.mult), q_decayed)

        @block.tensor
        def _(pe):
            def project(it, s):
                u, k = s // KT, s % KT
                n, j, half = 8 * it + u, 4 * it + u // 2, u % 2
                if k == 0:
                    pe.wait_ge(w_low, j + 1)
                    if n >= 2:
                        pe.wait_ge(unit_taken, n - 1)
                out, ts = unit[n % 2][:], slice(half * HALF, (half + 1) * HALF)
                pe.matmul(out, w_hi[:, j % 2, k, :], xh[:, k, ts], start=(k == 0), stop=False)
                pe.matmul(out, w_hi[:, j % 2, k, :], xl[:, k, ts], start=False, stop=False)
                mm = pe.matmul(out, w_lo[:, j % 2, k, :], xh[:, k, ts], start=False, stop=(k == KT - 1))
                if k == KT - 1:
                    mm.then_inc(unit_made, 1)

            def column_sums(out, src, signal):
                for half in range(2):
                    ts = slice(half * HALF, (half + 1) * HALF)
                    mm = pe.matmul(out[:, ts], c["ones"][:], src[:, ts], start=True, stop=True)
                mm.then_inc(signal, 1)

            def turn(out, src, signal, chunks):
                for n in chunks:
                    mm = pe.transpose(out[:, chunk(n)], src[:, chunk(n)], c["ident"][:])
                mm.then_inc(signal, 1)

            def head_work(p, s):
                q, k, v = (qkvz[:, p % 2, n] for n in range(3))
                if s == AT_VALUES:
                    pe.wait_ge(v_ready, p + 1)
                    if p:
                        pe.wait_ge(s_made, 9 * p)
                    turn(w1, v, v_turned, range(NT))
                if s == AT_NORMS:
                    pe.wait_ge(squared, 2 * p + 2)
                    pe.wait_ge(bv_made, p + 1)
                    column_sums(w1, lower, q_summed)
                    column_sums(w2, inv, k_summed)
                if s == AT_KEYS:
                    pe.wait_ge(normed, p + 1)
                    if p:
                        pe.wait_ge(o_rms, p)
                    turn(w0, k, k_turned, range(NT))
                if s == AT_KK:
                    for n in range(NT):
                        mm = pe.matmul(w2[:, chunk(n)], k[:, chunk(n)], k[:, chunk(n)], start=True, stop=True)
                    mm.then_inc(kk_made, 1)
                if s == AT_QK:
                    for n in range(NT):
                        mm = pe.matmul(w1[:, chunk(n)], k[:, chunk(n)], q[:, chunk(n)], start=True, stop=True)
                    mm.then_inc(qk_made, 1)
                if s == AT_FIRST:
                    pe.wait_ge(kd_made, p + 1)
                    for g in range(2):
                        pe.wait_ge(inv2_made, 2 * p + g + 1)
                        turn(w0, inv, inv2_turned, range(4 * g, 4 * g + 4))
                level, what = (s - AT_LEVELS) // 3, (s - AT_LEVELS) % 3
                if 0 <= level < LEVELS:
                    for g in range(2):
                        if what == 0:
                            if level == 0:
                                pe.wait_ge(inv2_copied, 2 * p + g + 1)
                            else:
                                pe.wait_ge(x_made, 12 * p + 2 * level - 1 + g)
                            for n in range(4):
                                mm = pe.matmul(as_blocks(w2[:, g * HALF + 64 * n:g * HALF + 64 * n + 64], level),
                                               lower[:, chunk(4 * g + n)],
                                               right_halves(inv_t[:, chunk(4 * g + n)], level), start=True, stop=True)
                            mm.then_inc(y_product, 1)
                        if what == 1:
                            pe.wait_ge(y_made, 12 * p + 2 * level + g + 1)
                            if level == 0:
                                pe.wait_ge(att_made, p + 1)
                            else:
                                pe.wait_ge(t_copied, 10 * p + 2 * level - 1 + g)
                            for n in range(4):
                                mm = pe.matmul(w1[:, g * HALF + 64 * n:g * HALF + 64 * n + 64],
                                               inv[:, chunk(4 * g + n)], y[:, g, 64 * n:64 * n + 64],
                                               start=True, stop=True)
                            mm.then_inc(x_product, 1)
                        if what == 2 and level < LEVELS - 1:
                            pe.wait_ge(x_made, 12 * p + 2 * level + g + 1)
                            turn(w0, inv_t, t_turned, range(4 * g, 4 * g + 4))
                n, what = (s - AT_CHUNKS) // 3, (s - AT_CHUNKS) % 3
                if 0 <= n < NT and s >= AT_CHUNKS:
                    if what == 0:
                        pe.wait_ge(s_made, 9 * p + n + 1)
                        pe.wait_ge(q_decayed, p + 1)
                        pe.matmul(w2[:, 0:P], k[:, chunk(n)], state[:, n % 2], start=True, stop=True).then_inc(ks_made, 1)
                        pe.matmul(w0[:, chunk(n)], state[:, n % 2], q[:, chunk(n)], start=True, stop=False)
                    if what == 1:
                        pe.wait_ge(x_made, 12 * p + 12)
                        pe.wait_ge(rest_made, NT * p + n + 1)
                        pe.matmul(w2[:, HALF:HALF + P], inv_t[:, chunk(n)], rest[:], start=True, stop=True
                                  ).then_inc(tr_made, 1)
                    if what == 2:
                        pe.wait_ge(vn_made, NT * p + n + 1)
                        pe.matmul(w1[:, 0:P], k_rows[:, chunk(n)], v_new[:], start=True, stop=True).then_inc(ds_made, 1)
                        pe.matmul(w0[:, chunk(n)], v_new[:], att_t[:, chunk(n)], start=False, stop=True
                                  ).then_inc(o_made, 1)

            for it in range(H + 2):
                for s in range(STEPS):
                    if it < H:
                        project(it, s)
                    if it >= 2 and s == AT_NORMS:
                        pe.wait_ge(o_squared, it - 1)
                        column_sums(w0, eg, o_summed)
                    if 1 <= it <= H:
                        head_work(it - 1, s)

        @block.scalar
        def _(act):
            step = Step(act, act_step)

            def high_part(j):
                act.wait_ge(w_loaded[j % 2], 16 * (j // 2 + 1))
                if j >= 2:
                    act.wait_ge(unit_made, 2 * j - 2)
                step(act.activation(w_hi[:, j % 2], w_raw[:, j % 2], ACT.Copy), w_high)

            def take_unit(it, u):
                n, block_n, half = 8 * it + u, 3 * it + u // 2, u % 2
                act.wait_ge(unit_made, n + 1)
                if u >= 6:
                    if it >= 2:
                        act.wait_ge(o_done, it - 1)
                    step(act.activation(qkvz[:, it % 2, 3, half * HALF:(half + 1) * HALF], unit[n % 2][:], ACT.Copy),
                         unit_taken)
                    return
                if block_n >= 2:
                    act.wait_ge(conv_made, 2 * block_n - 2)
                at = TAPS - 1 + half * HALF
                step(act.activation(raw[:, block_n % 2, at:at + HALF], unit[n % 2][:], ACT.Copy), unit_taken)

            def root(out, sums, signal, scale):
                step(act.activation(out, sums[:], ACT.Ln, bias=eps[:, 0:1], scale=scale))
                step(act.activation(out, out, ACT.Exp, scale=-0.5), signal)

            high_part(0)
            act.wait_ge(small, 16 * (TAPS + 1))
            for it in range(H + 2):
                p = it - 1
                for s in range(STEPS):
                    if it < H and s % 16 == 4 and 4 * it + s // 16 + 1 < 4 * H:
                        high_part(4 * it + s // 16 + 1)
                    if it < H and s % 8 == 0 and s:
                        take_unit(it, s // 8 - 1)
                    if it >= 2 and s == AT_NORMS:
                        act.wait_ge(o_summed, it - 1)
                        root(eg[:], w0, o_rms, 1.0 / DK)
                    if not 1 <= it <= H:
                        continue
                    if s == AT_NORMS:
                        act.wait_ge(q_summed, p + 1)
                        root(inv_t[:], w1, norms, 1.0)
                        act.wait_ge(k_summed, p + 1)
                        root(att_t[:], w2, norms, 1.0)
                        act.wait_ge(exponents, 2 * p + 1)
                        step(act.activation(lower[:], lower[:], ACT.Exp, scale=-1.0), decays)
                        act.wait_ge(exponents, 2 * p + 2)
                        step(act.activation(att_t[:], att_t[:], ACT.Exp), decays)
                        if p:
                            act.wait_ge(o_done, p)
                        step(act.activation(eg[:], g_rows[:, p % 2], ACT.Exp), eg_made)
                    if s == AT_KEYS:
                        act.wait_ge(k_turned, p + 1)
                        for n in range(NT):
                            step(act.activation(k_rows[:, chunk(n)], w0[:, chunk(n)], ACT.Copy,
                                                scale=gates["k_decay"][:, n, p:p + 1]),
                                 kd_made if n == NT - 1 else None)
                    if s == AT_FIRST:
                        for g in range(2):
                            act.wait_ge(inv2_turned, 2 * p + g + 1)
                            step(act.activation(inv_t[:, g * HALF:(g + 1) * HALF], w0[:, g * HALF:(g + 1) * HALF],
                                                ACT.Copy), inv2_copied)
                    level, what = (s - AT_LEVELS) // 3, (s - AT_LEVELS) % 3
                    if 0 <= level < LEVELS - 1 and what == 2:
                        for g in range(2):
                            act.wait_ge(t_turned, 10 * p + 2 * level + g + 1)
                            step(act.activation(inv[:, g * HALF:(g + 1) * HALF], w0[:, g * HALF:(g + 1) * HALF],
                                                ACT.Copy), t_copied)
                    if s == AT_CHUNKS + 3 * 4:
                        act.wait_ge(o_made, NT * p + 4)
                        step(act.activation(o_t[:, p, 0:HALF], w0[:, 0:HALF], ACT.Copy), o_taken)
                if 1 <= it <= H:
                    act.wait_ge(o_made, NT * p + NT)
                    step(act.activation(o_t[:, p, HALF:T], w0[:, HALF:T], ACT.Copy), o_taken)
                    step(act.activation(eg[:], o_t[:, p], ACT.Square), o_squared)
                if it < H:
                    take_unit(it, 7)
                    q, k, v, z = (qkvz[:, it % 2, n] for n in range(4))
                    act.wait_ge(conv_made, 6 * it + 6)
                    step(act.activation(v, v, ACT.Silu), v_ready)
                    step(act.activation(q, q, ACT.Silu))
                    step(act.activation(lower[:], q, ACT.Square), squared)
                    step(act.activation(k, k, ACT.Silu))
                    step(act.activation(inv[:], k, ACT.Square), squared)
                    step(act.activation(z, z, ACT.Silu), z_ready)

        @block.vector
        def _(dve):
            step = Step(dve, dve_step)
            step(dve.memset(raw[:, :, 0:TAPS - 1], 0.0))
            step(dve.memset(eps[:], RMS_EPS))
            dve.wait_ge(small, 16 * (TAPS + 1))

            def convolve(it, u, part):
                kind, half = u // 2, u % 2
                if part == 0:
                    dve.wait_ge(unit_taken, 8 * it + u + 1)
                src = raw[:, (3 * it + kind) % 2]
                out = qkvz[:, it % 2, kind, half * HALF:(half + 1) * HALF]
                tap = TAPS - 1 - part
                shifted = src[:, half * HALF + tap:half * HALF + tap + HALF]
                weight = taps[:, tap, kind * H + it:kind * H + it + 1]
                if part == 0:
                    step(dve.tensor_scalar(out, shifted, weight, None, ALU.mult))
                else:
                    step(dve.scalar_tensor_tensor(out, shifted, weight, out, ALU.mult, ALU.add),
                         conv_made if part == TAPS - 1 else None)

            def head_work(p, s):
                q, k = qkvz[:, p % 2, 0], qkvz[:, p % 2, 1]
                if s == AT_VALUES:
                    dve.wait_ge(v_turned, p + 1)
                    for n in range(NT):
                        step(dve.tensor_scalar(v_rows[:, chunk(n)], w1[:, chunk(n)], gates["beta"][:, n, p:p + 1], None,
                                               ALU.mult), bv_made if n == NT - 1 else None)
                    step(dve.memset(state[:, 0], 0.0), s_made)
                if s == AT_NORMS:
                    dve.wait_ge(norms, 2 * p + 1)
                    step(dve.scalar_tensor_tensor(q, q, DK ** -0.5, inv_t[:], ALU.mult, ALU.mult))
                    dve.wait_ge(norms, 2 * p + 2)
                    step(dve.tensor_tensor(k, k, att_t[:], ALU.mult), normed)
                    dve.wait_ge(g_loaded[p % 2], 16 * (p // 2 + 1))
                    for n in range(NT):
                        step(dve.scalar_tensor_tensor(lower[:, chunk(n)], g_rows[:, p % 2, chunk(n)],
                                                      gates["g"][:, n, p:p + 1], c["above_big"][:],
                                                      ALU.subtract, ALU.max), exponents if n == NT - 1 else None)
                    for n in range(NT):
                        step(dve.scalar_tensor_tensor(att_t[:, chunk(n)], g_rows[:, p % 2, chunk(n)],
                                                      gates["g"][:, n, p:p + 1], c["below_neg"][:],
                                                      ALU.subtract, ALU.min), exponents if n == NT - 1 else None)
                if s == AT_KK:
                    dve.wait_ge(kk_made, p + 1)
                    dve.wait_ge(decays, 2 * p + 1)
                    for n in range(NT):
                        step(dve.scalar_tensor_tensor(lower[:, chunk(n)], w2[:, chunk(n)], gates["beta"][:, n, p:p + 1],
                                                      lower[:, chunk(n)], ALU.mult, ALU.mult),
                             lower_made if n % 4 == 3 else None)
                    for g in range(2):
                        four = slice(g * HALF, (g + 1) * HALF)
                        view = lambda ap: ap[:, four].rearrange("p (n t) -> p n t", n=4)
                        step(dve.tensor_tensor(view(inv), view(lower), c["odd_below"][:].unsqueeze(1).to_broadcast(
                            [P, 4, P]), ALU.mult))
                        step(dve.tensor_tensor(view(inv), view(inv), c["ident"][:].unsqueeze(1).to_broadcast(
                            [P, 4, P]), ALU.add), inv2_made)
                if s == AT_QK:
                    dve.wait_ge(qk_made, p + 1)
                    dve.wait_ge(decays, 2 * p + 2)
                    step(dve.tensor_tensor(att_t[:, 0:HALF], w1[:, 0:HALF], att_t[:, 0:HALF], ALU.mult))
                    step(dve.tensor_tensor(att_t[:, HALF:T], w1[:, HALF:T], att_t[:, HALF:T], ALU.mult), att_made)
                level, what = (s - AT_LEVELS) // 3, (s - AT_LEVELS) % 3
                if 0 <= level < LEVELS:
                    for g in range(2):
                        four = slice(g * HALF, g * HALF + 256)
                        if what == 0:
                            dve.wait_ge(y_product, 12 * p + 2 * level + g + 1)
                            mask = c["level_mask"][:, level].unsqueeze(1).to_broadcast([P, 4, P // 2])
                            step(dve.tensor_tensor(y[:, g].rearrange("p (n t) -> p n t", n=4),
                                                   w2[:, four].rearrange("p (n t) -> p n t", n=4), mask, ALU.mult),
                                 y_made)
                        if what == 1:
                            dve.wait_ge(x_product, 12 * p + 2 * level + g + 1)
                            x = right_halves(inv_t[:, g * HALF:(g + 1) * HALF], level)
                            step(dve.tensor_tensor(x, x, as_blocks(w1[:, four], level), ALU.add), x_made)
                n, what = (s - AT_CHUNKS) // 3, (s - AT_CHUNKS) % 3
                if 0 <= n < NT and s >= AT_CHUNKS:
                    if what == 0:
                        dve.wait_ge(ks_made, NT * p + n + 1)
                        step(dve.scalar_tensor_tensor(rest[:], w2[:, 0:P], gates["neg_beta_eg"][:, n, p:p + 1],
                                                      v_rows[:, chunk(n)], ALU.mult, ALU.add), rest_made)
                    if what == 1:
                        dve.wait_ge(tr_made, NT * p + n + 1)
                        step(dve.tensor_copy(v_new[:], w2[:, HALF:HALF + P]), vn_made)
                    if what == 2:
                        dve.wait_ge(ds_made, NT * p + n + 1)
                        step(dve.scalar_tensor_tensor(state[:, (n + 1) % 2], state[:, n % 2],
                                                      gates["last"][:, n, p:p + 1], w1[:, 0:P], ALU.mult, ALU.add),
                             s_made)

            for it in range(H + 2):
                for s in range(STEPS):
                    if it >= 2 and s == AT_NORMS:
                        q = it - 2
                        dve.wait_ge(o_rms, q + 1)
                        dve.wait_ge(z_ready, q + 1)
                        step(dve.scalar_tensor_tensor(o_t[:, q], o_t[:, q], gain[:, 0:1], eg[:], ALU.mult, ALU.mult))
                        step(dve.tensor_tensor(o_t[:, q], o_t[:, q], qkvz[:, q % 2, 3], ALU.mult), o_done)
                    if 1 <= it <= H:
                        head_work(it - 1, s)
                    u, part = s // 8 - 1, (s % 8 - 1) // 2
                    if it < H and 0 <= u < 6 and s % 2 == 1:
                        convolve(it, u, part)


def mixer_out(nc, c, o, turned, residual, w_out, ln_g, ln_b, w_hi, w_lo, x1, name):
    with Phase(nc, name) as ph:
        sb, ps, sem = ph.sb, ph.ps, ph.sem
        RAW = 3
        w_raw = sb("w_raw", [P, RAW, D])
        o_hi, o_lo = sb("o_hi", [P, 2, KT, P], F32R), sb("o_lo", [P, 2, KT, P], F32R)
        old = sb("old", [P, 2, D])
        mixed = sb("mixed", [P, 2, D])
        gain, shift = sb("gain", [P, D]), sb("shift", [P, D])
        stats, moments = sb("stats", [P, 2, 2, 6]), sb("moments", [P, 2, 2])
        rstd, eps = sb("rstd", [P, 2]), sb("eps", [P, 1])
        out = [ps(f"y{n}", [P, D]) for n in range(3)]
        flip = [ps(f"flip{n}", [P, HALF]) for n in range(2)]
        w_loaded = [sem(f"w_loaded{n}") for n in range(RAW)]
        x_loaded = [sem(f"x_loaded{n}") for n in range(2)]
        ln_loaded = sem("ln_loaded")
        act_step, dve_step, pool_step = sem("act_step"), sem("dve_step"), sem("pool_step")
        w_high, w_low, o_high, o_low = sem("w_high"), sem("w_low"), sem("o_high"), sem("o_low")
        flipped, y_made, mixed_made = sem("flipped"), sem("y_made"), sem("mixed_made")
        var_made, rstd_made, scaled, x_made = sem("var_made"), sem("rstd_made"), sem("scaled"), sem("x_made")
        eps_made = sem("eps_made")
        block = ph.enter_context(nc.Block())

        @block.sync
        def _(sp):
            def load_x(t):
                if t >= 2:
                    sp.wait_ge(mixed_made, t - 1)
                sp.dma_start(old[:, t % 2], residual[t * P:(t + 1) * P, :]).then_inc(x_loaded[t % 2], 16)

            for k in range(KT):
                if k >= RAW:
                    sp.wait_ge(w_low, k - RAW + 1)
                sp.dma_start(w_raw[:, k % RAW], w_out[k * P:(k + 1) * P, :]).then_inc(w_loaded[k % RAW], 16)
            load_x(0)
            load_x(1)
            sp.dma_start(gain[:], ln_g.partition_broadcast(P)).then_inc(ln_loaded, 16)
            sp.dma_start(shift[:], ln_b.partition_broadcast(P)).then_inc(ln_loaded, 16)
            for t in range(2, NT):
                load_x(t)

        @block.tensor
        def _(pe):
            def flip_tile(t):
                for half in range(2):
                    n = 2 * t + half
                    if n >= 2:
                        pe.wait_ge(o_low, n - 1)
                    for j in range(4):
                        k = 4 * half + j
                        mm = pe.transpose(flip[half][:, j * P:(j + 1) * P], o[:, t, k * P:(k + 1) * P], c["ident"][:])
                    mm.then_inc(flipped, 1)

            def multiply(t, k):
                if k == 0 and t >= 3:
                    pe.wait_ge(mixed_made, t - 2)
                y = out[t % 3]
                for half in range(2):
                    cols = slice(half * HALF, (half + 1) * HALF)
                    pe.matmul(y[:, cols], o_hi[:, t % 2, k, :], w_hi[:, k, cols], start=(k == 0), stop=False)
                    pe.matmul(y[:, cols], o_hi[:, t % 2, k, :], w_lo[:, k, cols], start=False, stop=False)
                    mm = pe.matmul(y[:, cols], o_lo[:, t % 2, k, :], w_hi[:, k, cols], start=False,
                                   stop=(k == KT - 1))
                if k == KT - 1:
                    mm.then_inc(y_made, 1)

            if turned:
                flip_tile(0)
                flip_tile(1)
            pe.wait_ge(o_low, 4)
            for k in range(KT):
                pe.wait_ge(w_low, k + 1)
                multiply(0, k)
                multiply(1, k)
                if turned and k == KT // 2:
                    flip_tile(2)
            for t in range(2, NT):
                pe.wait_ge(o_low, 2 * t + 2)
                for k in range(KT):
                    multiply(t, k)
                    if turned and k == KT // 2 and t + 1 < NT:
                        flip_tile(t + 1)

        def halves(t):
            for half in range(2):
                ks = slice(4 * half, 4 * half + 4)
                src = flip[half][:].rearrange("p (k t) -> p k t", k=4) if turned else o[:, ks, t * P:(t + 1) * P]
                yield 2 * t + half, ks, src

        @block.scalar
        def _(act):
            step = Step(act, act_step)

            def o_part(t):
                if t >= 2:
                    act.wait_ge(y_made, t - 1)
                for n, ks, src in halves(t):
                    if turned:
                        act.wait_ge(flipped, n + 1)
                    step(act.activation(o_hi[:, t % 2, ks], src, ACT.Copy), o_high)

            o_part(0)
            o_part(1)
            for k in range(KT):
                act.wait_ge(w_loaded[k % RAW], 16 * (k // RAW + 1))
                step(act.activation(w_hi[:, k], w_raw[:, k % RAW], ACT.Copy), w_high)
            act.wait_ge(eps_made, 1)
            for t in range(NT):
                if t + 2 < NT:
                    o_part(t + 2)
                act.wait_ge(var_made, t + 1)
                r = rstd[:, t % 2:t % 2 + 1]
                step(act.activation(r, moments[:, t % 2, 1:2], ACT.Ln, bias=eps[:, 0:1]))
                step(act.activation(r, r, ACT.Exp, scale=-0.5), rstd_made)

        @block.vector
        def _(dve):
            step = Step(dve, dve_step)
            step(dve.memset(eps[:], LN_EPS), eps_made)

            def o_part(t):
                for n, ks, src in halves(t):
                    dve.wait_ge(o_high, n + 1)
                    step(dve.tensor_tensor(o_lo[:, t % 2, ks], src, o_hi[:, t % 2, ks].bitcast(F32),
                                           ALU.subtract), o_low)

            o_part(0)
            o_part(1)
            for k in range(KT):
                dve.wait_ge(w_high, k + 1)
                step(dve.tensor_tensor(w_lo[:, k], w_raw[:, k % RAW], w_hi[:, k].bitcast(F32), ALU.subtract), w_low)
            for t in range(NT):
                b = t % 2
                dve.wait_ge(x_loaded[b], 16 * (t // 2 + 1))
                dve.wait_ge(y_made, t + 1)
                if t >= 2:
                    dve.wait_ge(x_made, t - 1)
                step(dve.scalar_tensor_tensor(mixed[:, b], old[:, b], ALPHA, out[t % 3][:], ALU.mult, ALU.add),
                     mixed_made)
                for half in range(2):
                    step(dve.bn_stats(stats[:, b, half], mixed[:, b, half * HALF:(half + 1) * HALF]))
                step(dve.bn_aggr(moments[:, b], stats[:, b]), var_made)
                if t + 2 < NT:
                    o_part(t + 2)
                dve.wait_ge(rstd_made, t + 1)
                step(dve.tensor_scalar(mixed[:, b], mixed[:, b], moments[:, b, 0:1], rstd[:, b:b + 1],
                                       ALU.subtract, ALU.mult))
                if t == 0:
                    dve.wait_ge(ln_loaded, 32)
                step(dve.tensor_tensor(mixed[:, b], mixed[:, b], gain[:], ALU.mult), scaled)

        @block.gpsimd
        def _(pool):
            step = Step(pool, pool_step)
            pool.wait_ge(ln_loaded, 32)
            for t in range(NT):
                pool.wait_ge(scaled, t + 1)
                step(pool.tensor_tensor(x1[:, t], mixed[:, t % 2], shift[:], ALU.add), x_made)


def gated_embedding(nc, c, x1, p_emb, w_gate, w_proj, out_dram, xh, xl, stored, name):
    KP = p_emb.shape[1] // P
    with Phase(nc, name) as ph:
        sb, ps, sem = ph.sb, ph.ps, ph.sem
        RAW, KW = 2, KP + KT
        w_raw = sb("w_raw", [P, RAW, D])
        w_hi, w_lo = sb("w_hi", [P, KW, D], F32R), sb("w_lo", [P, KW, D], F32R)
        p_hi, p_lo = sb("p_hi", [P, KP, P], F32R), sb("p_lo", [P, KP, P], F32R)
        a_hi, a_lo = sb("a_hi", [P, 2, KT, P], F32R), sb("a_lo", [P, 2, KT, P], F32R)
        p_tile = sb("p_tile", [P, 2, KP * P])
        tanh = sb("tanh", [P, HALF])
        flip = [ps(f"flip{n}", [P, HALF]) for n in range(2)]
        gate = [ps(f"gate{n}", [P, D]) for n in range(2)]
        proj = ps("proj", [P, D])
        w_loaded = [sem(f"w_loaded{n}") for n in range(RAW)]
        p_loaded = [sem(f"p_loaded{n}") for n in range(2)]
        act_step, dve_step = sem("act_step"), sem("dve_step")
        w_high, w_low = sem("w_high"), sem("w_low")
        flipped, high, low = sem("flipped"), sem("high"), sem("low")
        proj_made, gate_made, tanh_made, proj_used, half_used = (
            sem("proj_made"), sem("gate_made"), sem("tanh_made"), sem("proj_used"), sem("half_used"))
        block = ph.enter_context(nc.Block())
        last = xh is None

        pieces = []
        for t in range(NT + 1):
            if t < NT:
                pieces += [("p", t, 0), ("x1", t, 0), ("x1", t, 1)]
            if t >= 1 and not last:
                pieces += [("x2", t - 1, 0), ("x2", t - 1, 1)]
        order = {piece: n for n, piece in enumerate(pieces)}

        def source(piece):
            kind, t, half = piece
            if kind == "p":
                return [p_tile[:, t % 2, k * P:(k + 1) * P] for k in range(KP)]
            return [x1[:, t, (4 * half + j) * P:(4 * half + j + 1) * P] for j in range(4)]

        def targets(piece):
            kind, t, half = piece
            if kind == "p":
                return [p_hi[:], p_lo[:]]
            if kind == "x1":
                return [a[:, t % 2, 4 * half:4 * half + 4] for a in (a_hi, a_lo)]
            return [a[:, 4 * half:4 * half + 4, t * P:(t + 1) * P] for a in (xh, xl)]

        @block.sync
        def _(sp):
            def load_w(k):
                if k >= RAW:
                    sp.wait_ge(w_low, k - RAW + 1)
                src = w_proj[k * P:(k + 1) * P, :] if k < KP else w_gate[(k - KP) * P:(k - KP + 1) * P, :]
                sp.dma_start(w_raw[:, k % RAW], src).then_inc(w_loaded[k % RAW], 16)

            def load_p(t):
                sp.dma_start(p_tile[:, t % 2], p_emb[t * P:(t + 1) * P, :]).then_inc(p_loaded[t % 2], 16)

            load_p(0)
            load_p(1)
            for k in range(KW):
                load_w(k)
            for t in range(NT):
                if t + 2 < NT:
                    sp.wait_ge(low, order[("p", t, 0)] + 1)
                    load_p(t + 2)
                sp.wait_ge(half_used, 2 * t + 2)
                sp.dma_start(out_dram[t * P:(t + 1) * P, :], x1[:, t]).then_inc(stored, 16)
            sp.wait_ge(stored, 16 * NT)

        @block.tensor
        def _(pe):
            def flip_piece(piece):
                n = order[piece]
                if n >= 2:
                    pe.wait_ge(low, n - 1)
                if piece[0] == "x2":
                    pe.wait_ge(half_used, 2 * piece[1] + 2)
                if piece[0] == "p":
                    pe.wait_ge(p_loaded[piece[1] % 2], 16 * (piece[1] // 2 + 1))
                for j, src in enumerate(source(piece)):
                    mm = pe.transpose(flip[n % 2][:, j * P:(j + 1) * P], src, c["ident"][:])
                mm.then_inc(flipped, 1)

            def flip_tile(t):
                for piece in pieces:
                    if piece[0] != "x2" and piece[1] == t:
                        flip_piece(piece)

            def multiply(out, hi, lo, k, first, end):
                for half in range(2):
                    cols = slice(half * HALF, (half + 1) * HALF)
                    pe.matmul(out[:, cols], hi, w_hi[:, k, cols], start=first, stop=False)
                    pe.matmul(out[:, cols], hi, w_lo[:, k, cols], start=False, stop=False)
                    mm = pe.matmul(out[:, cols], lo, w_hi[:, k, cols], start=False, stop=end)
                return mm

            def project(t):
                if t >= 1:
                    pe.wait_ge(proj_used, 2 * t)
                for k in range(KP):
                    mm = multiply(proj, p_hi[:, k], p_lo[:, k], k, k == 0, k == KP - 1)
                mm.then_inc(proj_made, 1)

            def gates(t, k):
                if k == 0 and t >= 2:
                    pe.wait_ge(tanh_made, 2 * t - 2)
                mm = multiply(gate[t % 2], a_hi[:, t % 2, k], a_lo[:, t % 2, k], KP + k, k == 0, k == KT - 1)
                if k == KT - 1:
                    mm.then_inc(gate_made, 1)

            flip_tile(0)
            for t in range(NT):
                pe.wait_ge(low, order[("x1", t, 1)] + 1)
                if t == 0:
                    pe.wait_ge(w_low, KP)
                project(t)
                for k in range(KT):
                    if t == 0:
                        pe.wait_ge(w_low, KP + k + 1)
                    gates(t, k)
                    if k == 3 and t >= 1 and not last:
                        for half in range(2):
                            flip_piece(("x2", t - 1, half))
                    if k == 5 and t + 1 < NT:
                        flip_tile(t + 1)
            if not last:
                for half in range(2):
                    flip_piece(("x2", NT - 1, half))

        @block.scalar
        def _(act):
            step = Step(act, act_step)

            def high_part(piece):
                n = order[piece]
                if piece[0] == "x1" and piece[1] >= 2:
                    act.wait_ge(gate_made, piece[1] - 1)
                if piece[0] == "p" and piece[1] >= 1:
                    act.wait_ge(proj_made, piece[1])
                act.wait_ge(flipped, n + 1)
                width = len(source(piece))
                step(act.activation(targets(piece)[0], flip[n % 2][:, 0:width * P].rearrange("p (k t) -> p k t", t=P),
                                    ACT.Copy), high)

            def tile_parts(t):
                for piece in pieces:
                    if piece[0] != "x2" and piece[1] == t:
                        high_part(piece)

            tile_parts(0)
            for k in range(KW):
                act.wait_ge(w_loaded[k % RAW], 16 * (k // RAW + 1))
                step(act.activation(w_hi[:, k], w_raw[:, k % RAW], ACT.Copy), w_high)
            for t in range(NT):
                if t + 1 < NT:
                    tile_parts(t + 1)
                act.wait_ge(gate_made, t + 1)
                for half in range(2):
                    if 2 * t + half:
                        act.wait_ge(half_used, 2 * t + half)
                    step(act.activation(tanh[:], gate[t % 2][:, half * HALF:(half + 1) * HALF], ACT.Tanh, scale=0.5),
                         tanh_made)
                if not last:
                    for half in range(2):
                        high_part(("x2", t, half))

        @block.vector
        def _(dve):
            step = Step(dve, dve_step)

            def low_part(piece):
                n = order[piece]
                dve.wait_ge(high, n + 1)
                hi, lo = targets(piece)
                width = len(source(piece))
                step(dve.tensor_tensor(lo, flip[n % 2][:, 0:width * P].rearrange("p (k t) -> p k t", t=P),
                                       hi.bitcast(F32), ALU.subtract), low)

            def tile_parts(t):
                for piece in pieces:
                    if piece[0] != "x2" and piece[1] == t:
                        low_part(piece)

            tile_parts(0)
            for k in range(KW):
                dve.wait_ge(w_high, k + 1)
                step(dve.tensor_tensor(w_lo[:, k], w_raw[:, k % RAW], w_hi[:, k].bitcast(F32), ALU.subtract), w_low)
            for t in range(NT):
                if t + 1 < NT:
                    tile_parts(t + 1)
                dve.wait_ge(proj_made, t + 1)
                for half in range(2):
                    cols = slice(half * HALF, (half + 1) * HALF)
                    dve.wait_ge(tanh_made, 2 * t + half + 1)
                    step(dve.scalar_tensor_tensor(tanh[:], tanh[:], 1.0, proj[:, cols], ALU.add, ALU.mult), proj_used)
                    step(dve.scalar_tensor_tensor(x1[:, t, cols], tanh[:], 0.5, x1[:, t, cols], ALU.mult, ALU.add),
                         half_used)
                if not last:
                    for half in range(2):
                        low_part(("x2", t, half))


BF16 = mybir.dt.bfloat16
FH = 16
DH = 64
PAIRS = FH // 2
WIDTH = FH * DH


def fox_values(nc, c, xh, xl, w_in, b_f, c_rows, values, gate_z):
    with Phase(nc, "fv") as ph:
        sb, ps, sem = ph.sb, ph.ps, ph.sem
        RAW, PANELS = 3, 4
        w_raw = sb("w_raw", [P, RAW, HALF])
        w_hi, w_lo = sb("w_hi", [P, 2, KT, HALF], F32R), sb("w_lo", [P, 2, KT, HALF], F32R)
        f_raw, f_hi, f_lo = (sb("f_raw", [P, KT, FH]), sb("f_hi", [P, KT, FH], F32R), sb("f_lo", [P, KT, FH], F32R))
        bias = sb("bias", [P, FH])
        work = [sb(f"work{n}", [P, NT, FH]) for n in range(5)]
        rows = sb("rows", [P, P])
        bank = [ps(f"bank{n}", [P, HALF]) for n in range(8)]
        w_loaded = [sem(f"w_loaded{n}") for n in range(RAW)]
        small = sem("small")
        act_step, dve_step = sem("act_step"), sem("dve_step")
        w_high, w_low, f_high, f_low = sem("w_high"), sem("w_low"), sem("f_high"), sem("f_low")
        made, taken, f_made, f_log, c_summed, c_ready, c_turned = (
            sem("made"), sem("taken"), sem("f_made"), sem("f_log"), sem("c_summed"), sem("c_ready"), sem("c_turned"))
        abs_made, exp_made, rows_made, stored = sem("abs_made"), sem("exp_made"), sem("rows_made"), sem("stored")
        block = ph.enter_context(nc.Block())
        F = NT * FH

        @block.sync
        def _(sp):
            for n in range(PANELS):
                for k in range(KT):
                    m = n * KT + k
                    if m >= RAW:
                        sp.wait_ge(w_low, m - RAW + 1)
                    sp.dma_start(w_raw[:, m % RAW], w_in[k * P:(k + 1) * P, 2 * WIDTH + n * HALF:2 * WIDTH + (n + 1) * HALF]
                                 ).then_inc(w_loaded[m % RAW], 16)
                    if m == 0:
                        sp.dma_start(f_raw[:], w_in[:, 4 * WIDTH:4 * WIDTH + FH].rearrange("(k p) n -> p k n", p=P)
                                     ).then_inc(small, 16)
                        sp.dma_start(bias[:], b_f.partition_broadcast(P)).then_inc(small, 16)
            sp.wait_ge(rows_made, 1)
            sp.dma_start(c_rows, rows[:]).then_inc(stored, 16)
            sp.wait_ge(stored, 16)

        @block.tensor
        def _(pe):
            def multiply(n, t, k):
                ts, b = slice(t * P, (t + 1) * P), n % 2
                if k == 0 and n >= 1:
                    pe.wait_ge(taken, (n - 1) * NT + t + 1)
                pe.matmul(bank[t][:], xh[:, k, ts], w_hi[:, b, k], start=(k == 0), stop=False)
                pe.matmul(bank[t][:], xh[:, k, ts], w_lo[:, b, k], start=False, stop=False)
                mm = pe.matmul(bank[t][:], xl[:, k, ts], w_hi[:, b, k], start=False, stop=(k == KT - 1))
                if k == KT - 1:
                    mm.then_inc(made, 1)

            for k in range(KT):
                pe.wait_ge(w_low, k + 1)
                for t in range(NT):
                    multiply(0, t, k)
            for n in range(1, PANELS):
                pe.wait_ge(w_low, (n + 1) * KT)
                for t in range(NT):
                    for k in range(KT):
                        multiply(n, t, k)
            pe.wait_ge(taken, PANELS * NT)
            pe.wait_ge(f_low, 1)
            f = bank[0][:, 0:F].rearrange("p (t h) -> p t h", h=FH)
            for t in range(NT):
                for k in range(KT):
                    ts = slice(t * P, (t + 1) * P)
                    pe.matmul(f[:, t], xh[:, k, ts], f_hi[:, k], start=(k == 0), stop=False)
                    pe.matmul(f[:, t], xh[:, k, ts], f_lo[:, k], start=False, stop=False)
                    mm = pe.matmul(f[:, t], xl[:, k, ts], f_hi[:, k], start=False, stop=(k == KT - 1))
            mm.then_inc(f_made, 1)
            pe.wait_ge(f_log, 1)
            for t in range(NT):
                out = bank[1][:, t * FH:(t + 1) * FH]
                for before in range(t):
                    pe.matmul(out, c["ones"][:], work[3][:, before], start=(before == 0), stop=False)
                mm = pe.matmul(out, c["tri"][:], work[3][:, t], start=(t == 0), stop=True)
            mm.then_inc(c_summed, 1)
            pe.wait_ge(c_ready, 1)
            pe.transpose(bank[2][:, 0:P], work[4][:].rearrange("p t h -> p (t h)"), c["ident"][:]).then_inc(c_turned, 1)

        @block.scalar
        def _(act):
            step = Step(act, act_step)

            def high(m):
                n, k = m // KT, m % KT
                act.wait_ge(w_loaded[m % RAW], 16 * (m // RAW + 1))
                if n >= 2:
                    act.wait_ge(made, (n - 1) * NT)
                step(act.activation(w_hi[:, n % 2, k], w_raw[:, m % RAW], ACT.Copy), w_high)

            for m in range(2 * KT):
                high(m)
            act.wait_ge(small, 32)
            step(act.activation(f_hi[:], f_raw[:], ACT.Copy), f_high)
            for n in range(PANELS):
                for t in range(NT):
                    act.wait_ge(made, n * NT + t + 1)
                    half = n % 2
                    cols = slice(half * HALF, (half + 1) * HALF)
                    if n < 2:
                        step(act.activation(values[:, t, cols], bank[t][:], ACT.Copy), taken)
                    else:
                        step(act.activation(gate_z[:, t, cols], bank[t][:], ACT.Silu), taken)
                if n + 2 < PANELS:
                    for k in range(KT):
                        high((n + 2) * KT + k)
            act.wait_ge(abs_made, 1)
            step(act.activation(work[1][:], work[1][:], ACT.Exp), exp_made)
            act.wait_ge(c_turned, 1)
            step(act.activation(rows[:], bank[2][:, 0:P], ACT.Copy), rows_made)

        @block.vector
        def _(dve):
            step = Step(dve, dve_step)
            for m in range(PANELS * KT):
                n, k = m // KT, m % KT
                dve.wait_ge(w_high, m + 1)
                step(dve.tensor_tensor(w_lo[:, n % 2, k], w_raw[:, m % RAW], w_hi[:, n % 2, k].bitcast(F32),
                                       ALU.subtract), w_low)
            dve.wait_ge(f_high, 1)
            step(dve.tensor_tensor(f_lo[:], f_raw[:], f_hi[:].bitcast(F32), ALU.subtract), f_low)
            dve.wait_ge(f_made, 1)
            f = bank[0][:, 0:F].rearrange("p (t h) -> p t h", h=FH)
            step(dve.tensor_tensor(work[0][:], f, bias[:].unsqueeze(1).to_broadcast([P, NT, FH]), ALU.add))
            step(dve.scalar_tensor_tensor(work[1][:], work[0][:], -1.0, work[0][:], ALU.mult, ALU.min), abs_made)
            dve.wait_ge(exp_made, 1)
            log_one_plus(dve, step, work[1], work[2], work[4], work[3])
            step(dve.scalar_tensor_tensor(work[3][:], work[0][:], 0.0, work[2][:], ALU.min, ALU.subtract), f_log)
            dve.wait_ge(c_summed, 1)
            step(dve.tensor_scalar(work[4][:], bank[1][:, 0:F].rearrange("p (t h) -> p t h", h=FH), -1.0, None,
                                   ALU.mult), c_ready)


F_STEPS = 32
AT_SUMS = 1
AT_ITEMS = 7
ITEMS = 2 * NT
LAG_TURN, LAG_OUT = 2, 3


def fox_attention(nc, c, xh, xl, w_in, q_gain, k_gain, c_rows, values, gate_z):
    with Phase(nc, "fa") as ph:
        sb, ps, sem = ph.sb, ph.ps, ph.sem
        w_raw = sb("w_raw", [P, 2, KT, P])
        w_hi, w_lo = sb("w_hi", [P, 2, KT, P], F32R), sb("w_lo", [P, 2, KT, P], F32R)
        qk = sb("qk", [P, 2, 2, T])
        root = sb("root", [P, 2, T])
        decay = sb("decay", [P, 2, T])
        probs = sb("probs", [P, 3, T])
        probs_t = sb("probs_t", [P, 2, T])
        halves = sb("halves", [P, P])
        ident_b, mask_b = sb("ident_b", [P, P], BF16), sb("mask_b", [P, P], BF16)
        gains = sb("gains", [P, 2])
        top, total, share = sb("top", [P, 4]), sb("total", [P, 4]), sb("share", [P, 4])
        eps = sb("eps", [P, 1])
        unit = [ps(f"unit{n}", [P, HALF]) for n in range(2)]
        scores, turned = ps("scores", [P, T]), ps("turned", [P, T])
        result, spare = ps("result", [P, HALF]), ps("spare", [P, HALF])
        w_loaded = [sem(f"w_loaded{n}") for n in range(2)]
        d_loaded = [sem(f"d_loaded{n}") for n in range(2)]
        small = sem("small")
        act_step, dve_step, pool_step = sem("act_step"), sem("dve_step"), sem("pool_step")
        ready = sem("constants")
        w_high, w_low, unit_made, unit_taken = sem("w_high"), sem("w_low"), sem("unit_made"), sem("unit_taken")
        squared, summed, normed = sem("squared"), sem("summed"), sem("normed")
        rooted, roots = sem("rooted"), sem("roots")
        scored, biased, topped, exped = sem("scored"), sem("biased"), sem("topped"), sem("exped")
        flipped, flip_a, flip_d, result_made, result_used = (
            sem("flipped"), sem("flip_a"), sem("flip_d"), sem("result_made"), sem("result_used"))
        block = ph.enter_context(nc.Block())

        def items_of(step):
            lo, hi = step - AT_ITEMS, step - AT_ITEMS + 1
            span, n = F_STEPS - AT_ITEMS, ITEMS + LAG_OUT
            if lo < 0:
                return range(0)
            return range(lo * n // span, hi * n // span)

        def by_scalar(m):
            return m // NT * (NT // 2) + max(0, m % NT - NT // 2)

        def columns(j):
            pair, kind = j // 2, j % 2
            return slice(kind * WIDTH + pair * P, kind * WIDTH + (pair + 1) * P)

        def blocks(i):
            return slice(0, (i + 1) * P)

        @block.sync
        def _(sp):
            def load(j):
                if j >= 2:
                    sp.wait_ge(w_low, j - 1)
                sp.dma_start(w_raw[:, j % 2], w_in[:, columns(j)].rearrange("(k p) n -> p k n", p=P)
                             ).then_inc(w_loaded[j % 2], 16)

            load(0)
            for n, g in enumerate((q_gain, k_gain)):
                for head in range(2):
                    sp.dma_start(gains[head * DH:(head + 1) * DH, n:n + 1], g.rearrange("(p n) -> p n", n=1)
                                 ).then_inc(small, 16)
            load(1)
            for it in range(PAIRS + 1):
                if it >= 1:
                    for head in range(2):
                        p = it - 1
                        if p:
                            sp.wait_ge(biased, ITEMS * (p - 1) + NT * (head + 1))
                        rows = c_rows.rearrange("(t h) s -> h t s", h=FH)[2 * p + head]
                        sp.dma_start(decay[:, head].rearrange("p (t s) -> p t s", t=NT), rows.partition_broadcast(P)
                                     ).then_inc(d_loaded[head], 16)
                        if it < PAIRS and 2 * it + head + 2 < 2 * PAIRS:
                            load(2 * it + head + 2)
                else:
                    load(2)
                    load(3)

        @block.gpsimd
        def _(pool):
            step = Step(pool, pool_step)
            step(pool.memset(eps[:], RMS_EPS))
            step(pool.memset(halves[:], 0.0))
            step(pool.memset(halves[0:DH, 0:DH], 1.0))
            step(pool.memset(halves[DH:P, DH:P], 1.0))
            step(pool.memset(mask_b[:], 0.0))
            step(pool.affine_select(out=mask_b[:], in_=mask_b[:], compare_op=ALU.is_ge, fill=-BIG, base=0,
                                    pattern=[[-1, P]], channel_multiplier=1))
            step(pool.tensor_copy(ident_b[:], c["ident"][:]), ready)
            for j in range(2 * PAIRS):
                pool.wait_ge(w_high, j + 1)
                step(pool.tensor_tensor(w_lo[:, j % 2], w_raw[:, j % 2], w_hi[:, j % 2].bitcast(F32),
                                        ALU.subtract), w_low)

        @block.tensor
        def _(pe):
            def project(it, s):
                u, k = s // KT, s % KT
                n, j, half = 4 * it + u, 2 * it + u // 2, u % 2
                if k == 0:
                    pe.wait_ge(w_low, j + 1)
                    if n >= 2:
                        pe.wait_ge(unit_taken, n - 1)
                out, ts = unit[n % 2][:], slice(half * HALF, (half + 1) * HALF)
                pe.matmul(out, w_hi[:, j % 2, k, :], xh[:, k, ts], start=(k == 0), stop=False)
                pe.matmul(out, w_hi[:, j % 2, k, :], xl[:, k, ts], start=False, stop=False)
                mm = pe.matmul(out, w_lo[:, j % 2, k, :], xh[:, k, ts], start=False, stop=(k == KT - 1))
                if k == KT - 1:
                    mm.then_inc(unit_made, 1)

            def score(p, n):
                head, i = n // NT, n % NT
                m = ITEMS * p + n
                if n == 0:
                    pe.wait_ge(normed, p + 1)
                if m:
                    pe.wait_ge(biased, m)
                rows = slice(head * DH, (head + 1) * DH)
                q, k = qk[rows, p % 2, 0, i * P:(i + 1) * P], qk[rows, p % 2, 1]
                width = (i + 1) * P
                for at in range(0, width, HALF):
                    end = min(width, at + HALF)
                    pe.matmul(scores[:, at:end], q, k[:, at:end], start=True, stop=(end < width))
                pe.matmul(scores[:, width - P:width], ident_b[:], mask_b[:], start=False, stop=True
                          ).then_inc(scored, 1)

            def turn(p, n):
                i, m = n % NT, ITEMS * p + n
                pe.wait_ge(exped, m + 1)
                if m:
                    pe.wait_ge(flip_d, m)
                if by_scalar(m):
                    pe.wait_ge(flip_a, by_scalar(m))
                for b in range(i + 1):
                    mm = pe.transpose(turned[:, b * P:(b + 1) * P], probs[:, m % 3, b * P:(b + 1) * P], c["ident"][:])
                mm.then_inc(flipped, 1)

            def weigh(p, n):
                head, i, m = n // NT, n % NT, ITEMS * p + n
                pe.wait_ge(flip_d, m + 1)
                if by_scalar(m + 1):
                    pe.wait_ge(flip_a, by_scalar(m + 1))
                if m:
                    pe.wait_ge(result_used, m)
                col = (2 * p + head) * DH
                for b in range(i + 1):
                    mm = pe.matmul(result[:, 0:DH], probs_t[:, m % 2, b * P:(b + 1) * P], values[:, b, col:col + DH],
                                   start=(b == 0), stop=(b == i))
                mm.then_inc(result_made, 1)

            pe.wait_ge(ready, 1)
            for it in range(PAIRS + 1):
                p = it - 1
                for s in range(F_STEPS):
                    if it < PAIRS:
                        project(it, s)
                    if p < 0:
                        continue
                    if s == AT_SUMS:
                        for kind in range(2):
                            pe.wait_ge(squared, 2 * p + kind + 1)
                            if kind == 0 and p:
                                pe.wait_ge(biased, ITEMS * p)
                            if kind == 1:
                                pe.wait_ge(rooted, 2 * p + 1)
                            for half in range(2):
                                ts = slice(half * HALF, (half + 1) * HALF)
                                mm = pe.matmul(scores[:, ts], halves[:], root[:, kind, ts], start=True, stop=True)
                            mm.then_inc(summed, 1)
                    for e in items_of(s):
                        if e < ITEMS:
                            score(p, e)
                        if 0 <= e - LAG_TURN < ITEMS:
                            turn(p, e - LAG_TURN)
                        if 0 <= e - LAG_OUT < ITEMS:
                            weigh(p, e - LAG_OUT)

        @block.scalar
        def _(act):
            step = Step(act, act_step)

            def high_part(j):
                act.wait_ge(w_loaded[j % 2], 16 * (j // 2 + 1))
                if j >= 2:
                    act.wait_ge(unit_made, 2 * j - 2)
                step(act.activation(w_hi[:, j % 2], w_raw[:, j % 2], ACT.Copy), w_high)

            def take_unit(it, u):
                n = 4 * it + u
                act.wait_ge(unit_made, n + 1)
                step(act.activation(qk[:, it % 2, u // 2, u % 2 * HALF:(u % 2 + 1) * HALF], unit[n % 2][:], ACT.Copy),
                     unit_taken)

            high_part(0)
            act.wait_ge(ready, 1)
            for it in range(PAIRS + 1):
                p = it - 1
                for s in range(F_STEPS):
                    if it < PAIRS and s % 16 == 4 and 2 * it + s // 16 + 1 < 2 * PAIRS:
                        high_part(2 * it + s // 16 + 1)
                    if it < PAIRS and s % 8 == 0 and s:
                        take_unit(it, s // 8 - 1)
                    if p < 0:
                        continue
                    if s == AT_SUMS:
                        for kind in range(2):
                            act.wait_ge(summed, 2 * p + kind + 1)
                            step(act.activation(root[:, kind], scores[:], ACT.Ln, bias=eps[:, 0:1], scale=1.0 / DH),
                                 rooted)
                        for kind in range(2):
                            step(act.activation(root[:, kind], root[:, kind], ACT.Exp, scale=-0.5), roots)
                    for e in items_of(s):
                        if e < ITEMS:
                            m, i = ITEMS * p + e, e % NT
                            act.wait_ge(topped, m + 1)
                            row = probs[:, m % 3, blocks(i)]
                            step(act.activation(row, row, ACT.Exp, bias=top[:, m % 4:m % 4 + 1],
                                                accum_out=total[:, m % 4:m % 4 + 1]), exped)
                        n = e - LAG_TURN
                        if 0 <= n < ITEMS:
                            m, i = ITEMS * p + n, n % NT
                            act.wait_ge(flipped, m + 1)
                            if m >= 2:
                                act.wait_ge(result_made, m - 1)
                            if i >= NT // 2:
                                step(act.activation(probs_t[:, m % 2, 0:HALF], turned[:, 0:HALF], ACT.Copy), flip_a)
                if it < PAIRS:
                    take_unit(it, 3)
                    for kind in range(2):
                        step(act.activation(root[:, kind], qk[:, it % 2, kind], ACT.Square), squared)

        @block.vector
        def _(dve):
            step = Step(dve, dve_step)
            dve.wait_ge(small, 64)
            step(dve.tensor_scalar(gains[:, 0:1], gains[:, 0:1], DH ** -0.5, None, ALU.mult))
            for it in range(1, PAIRS + 1):
                p = it - 1
                for s in range(F_STEPS):
                    if s == AT_SUMS:
                        for kind in range(2):
                            dve.wait_ge(roots, 2 * p + kind + 1)
                            step(dve.scalar_tensor_tensor(qk[:, p % 2, kind], qk[:, p % 2, kind], gains[:, kind:kind + 1],
                                                          root[:, kind], ALU.mult, ALU.mult), normed if kind else None)
                    for e in items_of(s):
                        if e < ITEMS:
                            head, i, m = e // NT, e % NT, ITEMS * p + e
                            if i == 0:
                                dve.wait_ge(d_loaded[head], 16 * (p + 1))
                            dve.wait_ge(scored, m + 1)
                            if m >= 3:
                                dve.wait_ge(flipped, m - 2)
                            peak = top[:, m % 4:m % 4 + 1]
                            step(dve.tensor_tensor_reduce(probs[:, m % 3, blocks(i)], scores[:, blocks(i)],
                                                          decay[:, head, blocks(i)], 1.0, -3e38, ALU.add, ALU.max,
                                                          peak), biased)
                            step(dve.tensor_scalar(peak, peak, -1.0, None, ALU.mult), topped)
                        n = e - LAG_TURN
                        if 0 <= n < ITEMS:
                            m, i = ITEMS * p + n, n % NT
                            dve.wait_ge(flipped, m + 1)
                            if m >= 2:
                                dve.wait_ge(result_made, m - 1)
                            at = HALF if i >= NT // 2 else 0
                            there = slice(at, (i + 1) * P)
                            step(dve.tensor_copy(probs_t[:, m % 2, there], turned[:, there]), flip_d)
                        n = e - LAG_OUT
                        if 0 <= n < ITEMS:
                            head, i, m = n // NT, n % NT, ITEMS * p + n
                            sums, inverse = total[:, m % 4:m % 4 + 1], share[:, m % 4:m % 4 + 1]
                            dve.wait_ge(exped, m + 1)
                            step(dve.reciprocal(inverse, sums))
                            dve.wait_ge(result_made, m + 1)
                            col = (2 * p + head) * DH
                            z = gate_z[:, i, col:col + DH]
                            step(dve.scalar_tensor_tensor(z, result[:, 0:DH], inverse, z, ALU.mult, ALU.mult),
                                 result_used)


def build_program(nc, a, out):
    g_rows = nc.dram_tensor("g_rows_scratch", (NT * H, P), F32, kind="Internal").ap()
    c_rows = nc.dram_tensor("c_rows_scratch", (NT * FH, P), F32, kind="Internal").ap()
    x2 = nc.dram_tensor("x2_scratch", (T, D), F32, kind="Internal").ap()
    with ExitStack() as ctx:
        x2_stored = ctx.enter_context(nc.semaphore("x2_stored"))
        output_stored = ctx.enter_context(nc.semaphore("output_stored"))
        sb = lambda n, s, d=F32: ctx.enter_context(nc.sbuf_tensor(n, s, d))
        c = {n: sb(n, [P, P]) for n in ("ident", "tri", "ones")}
        part_hi, part_lo = sb("part_hi", [P, KT, T], F32R), sb("part_lo", [P, KT, T], F32R)
        x1 = sb("x1", [P, NT, D])
        with ExitStack() as gdn:
            sb1 = lambda n, s, d=F32: gdn.enter_context(nc.sbuf_tensor(n, s, d))
            o_t = sb1("o_t", [P, H, T])
            with ExitStack() as masks:
                sb2 = lambda n, s, d=F32: masks.enter_context(nc.sbuf_tensor(n, s, d))
                for n in ("odd_below", "above_big", "below_neg"):
                    c[n] = sb2(n, [P, P])
                c["level_mask"] = sb2("level_mask", [P, LEVELS, P // 2])
                gates = {n: sb2(f"gates_{n}", [P, NT, H]) for n in ("beta", "g", "neg_beta_eg", "k_decay", "last")}
                w_in = a["gdn_w_in"][0]
                small = {"ab": w_in[:, 4 * H * DK:4 * H * DK + 2 * H], "dt_bias": a["gdn_dt_bias"][0],
                         "a_log": a["gdn_a_log"][0]}
                transpose_input(nc, a["x"], c, part_hi, part_lo, small, gates, g_rows)
                delta_net(nc, c, part_hi, part_lo, gates, w_in, a["gdn_conv_w"][0], a["gdn_norm_g"][0], g_rows,
                          x1, o_t)
            mixer_out(nc, c, o_t, False, a["x"][0], a["gdn_w_out"][0], a["ln_g"][0], a["ln_b"][0],
                      part_hi, part_lo, x1, "m0")
        gated_embedding(nc, c, x1, a["p"][0, 0], a["ple_w_gate"][0], a["ple_w_proj"][0], x2, part_hi, part_lo,
                        x2_stored, "e0")
        with ExitStack() as fox:
            gate_z = fox.enter_context(nc.sbuf_tensor("gate_z", [P, NT, WIDTH], F32))
            w_in = a["fox_w_in"][0]
            fox_values(nc, c, part_hi, part_lo, w_in, a["fox_b_f"][0], c_rows, x1, gate_z)
            fox_attention(nc, c, part_hi, part_lo, w_in, a["fox_q_norm_g"][0], a["fox_k_norm_g"][0], c_rows, x1,
                          gate_z)
            mixer_out(nc, c, gate_z, True, x2, a["fox_w_out"][0], a["ln_g"][1], a["ln_b"][1],
                      part_hi, part_lo, x1, "m1")
        gated_embedding(nc, c, x1, a["p"][1, 0], a["ple_w_gate"][1], a["ple_w_proj"][1], out[0], None, None,
                        output_stored, "e1")


_INS = ["x", "p", "ln_g", "ln_b", "ple_w_gate", "ple_w_proj", "gdn_w_in", "gdn_conv_w", "gdn_a_log", "gdn_dt_bias",
        "gdn_norm_g", "gdn_w_out", "fox_w_in", "fox_b_f", "fox_q_norm_g", "fox_k_norm_g", "fox_w_out"]


def kernel(**inputs):
    import numpy as _np
    import concourse.bacc as _bacc
    from concourse import mybir as _mybir
    from concourse.bass_utils import run_bass_kernel_spmd as _run

    nc = _bacc.Bacc("TRN2", target_bir_lowering=False, num_devices=1)
    arrays, args = {}, {}
    for name in _INS:
        a = _np.ascontiguousarray(inputs[name])
        arrays[f"in_{name}_dram"] = a
        args[name] = nc.dram_tensor(f"in_{name}_dram", a.shape, _mybir.dt.from_np(a.dtype), kind="ExternalInput").ap()
    out = nc.dram_tensor("out_0_dram", (1, T, D), F32, kind="ExternalOutput").ap()
    build_program(nc, args, out)
    r = _run(nc, [arrays], core_ids=[0])
    return r.results[0]["out_0_dram"]
```

```python
import numpy as np
from contextlib import ExitStack

import concourse.bass as bass
from concourse import mybir

F32 = mybir.dt.float32
F32R = mybir.dt.float32r
ALU = mybir.AluOpType
ACT = mybir.ActivationFunctionType

P = 128
D = 1024
T = 1024
KT = D // P
NT = T // P
HALF = 512
H = 8
DK = 128
TAPS = 4
BIG = 1e30
RMS_EPS = 1e-6
LN_EPS = 1e-5
ALPHA = float((2 * 2) ** 0.25)
LEVELS = 6


class Phase(ExitStack):

    def __init__(self, nc, name):
        super().__init__()
        self.nc, self.name, self.semaphores = nc, name, []
        self.callback(self.clear)

    def sb(self, name, shape, dtype=F32):
        return self.enter_context(self.nc.sbuf_tensor(f"{self.name}_{name}", shape, dtype))

    def ps(self, name, shape):
        return self.enter_context(self.nc.psum_tensor(f"{self.name}_{name}", shape, F32))

    def sem(self, name):
        self.semaphores.append(self.nc.alloc_semaphore(f"{self.name}_{name}"))
        return self.semaphores[-1]

    def clear(self):
        self.nc.clear_and_free_semaphores(self.semaphores)
        self.nc.all_engine_barrier()


class Step:

    def __init__(self, engine, own):
        self.engine, self.own, self.value = engine, own, {}

    def __call__(self, instruction, signal=None):
        sem = self.own if signal is None else signal
        self.value[sem] = self.value.get(sem, 0) + 1
        instruction.then_inc(sem, 1)
        self.engine.wait_ge(sem, self.value[sem])


def constants_program(pool, step, c):
    def select(ap, compare, fill, base, pattern, multiplier):
        step(pool.affine_select(out=ap, in_=ap, compare_op=compare, fill=fill, base=base,
                                pattern=pattern, channel_multiplier=multiplier))

    step(pool.memset(c["ident"][:], 0.0))
    select(c["ident"][:], ALU.not_equal, 1.0, 0, [[-1, P]], 1)
    step(pool.memset(c["tri"][:], 1.0))
    select(c["tri"][:], ALU.is_ge, 0.0, 0, [[1, P]], -1)
    step(pool.memset(c["ones"][:], 1.0))
    step(pool.memset(c["above_big"][:], 0.0))
    select(c["above_big"][:], ALU.is_ge, BIG, 0, [[-1, P]], 1)
    step(pool.memset(c["below_neg"][:], 0.0))
    select(c["below_neg"][:], ALU.is_ge, -BIG, 0, [[1, P]], -1)
    step(pool.memset(c["odd_below"][:], 0.0))
    view = c["odd_below"][:].rearrange("p (n two) -> p n two", two=2)[:, :, 0]
    step(pool.affine_select(out=view, in_=view, compare_op=ALU.not_equal, fill=-1.0, base=-1,
                            pattern=[[-2, P // 2]], channel_multiplier=1))
    for level in range(LEVELS):
        s = 2 << level
        nb = P // (2 * s)
        m = c["level_mask"][:, level, :]
        step(pool.memset(m, -1.0))
        select(m, ALU.is_ge, 0.0, 0, [[-2 * s, nb], [0, s]], 1)
        select(m, ALU.is_ge, 0.0, s - 1, [[2 * s, nb], [0, s]], -1)


def right_halves(ap, level):
    return ap.rearrange("p (n two s) -> p n two s", two=2, s=2 << level)[:, :, 1, :]


def as_blocks(ap, level):
    return ap.rearrange("p (n s) -> p n s", s=2 << level)


def transpose_input(nc, x, c, xh, xl, w_gate, gates, g_rows_dram):
    with Phase(nc, "in") as ph:
        sb, ps, sem = ph.sb, ph.ps, ph.sem
        x_tile = sb("x_tile", [P, 2, D])
        ab_raw = sb("ab_raw", [P, KT, 2 * H])
        ab_hi = sb("ab_hi", [P, KT, 2 * H], F32R)
        ab_lo = sb("ab_lo", [P, KT, 2 * H], F32R)
        dt_bias = sb("dt_bias", [P, H])
        a_log = sb("a_log", [P, H])
        work = [sb(f"gate_work{n}", [P, NT, H]) for n in range(6)]
        g_rows = sb("g_rows", [NT * H, P])
        ab_sb = sb("ab_sb", [2 * H, T])
        turned = [ps(f"turned{n}", [P, HALF]) for n in range(2)]
        ab_rows = ps("ab_rows", [2 * H, T])
        ab = ps("ab", [P, NT, 2 * H])
        cums = ps("cums", [P, HALF])
        totals = ps("totals", [P, HALF])
        rows = ps("rows", [P, HALF])

        x_loaded = [sem(f"x_loaded{n}") for n in range(2)]
        small_loaded = sem("small_loaded")
        pool_step, act_step, dve_step = sem("in_pool_step"), sem("in_act_step"), sem("in_dve_step")
        constants_made = sem("constants_made")
        x_turned, high_made, low_made = sem("x_turned"), sem("high_made"), sem("low_made")
        gate_high, gate_low, ab_made = sem("gate_high"), sem("gate_low"), sem("ab_made")
        ab_product, ab_copied = sem("ab_product"), sem("ab_copied")
        exp_beta, exp_alpha, g_made = sem("exp_beta"), sem("exp_alpha"), sem("g_made")
        g_summed, g_copied, g_turned, g_out = sem("g_summed"), sem("g_copied"), sem("g_turned"), sem("g_out")
        rows_made = sem("rows_made")
        decays_made, e_made = sem("decays_made"), sem("e_made")
        block = ph.enter_context(nc.Block())

        @block.sync
        def _(sp):
            for t in range(NT):
                if t >= 2:
                    sp.wait_ge(x_turned, 2 * (t - 1))
                sp.dma_start(x_tile[:, t % 2, :], x[0, t * P:(t + 1) * P, :]).then_inc(x_loaded[t % 2], 16)
                if t == 1:
                    sp.dma_start(ab_raw[:], w_gate["ab"].rearrange("(k p) n -> p k n", p=P)).then_inc(small_loaded, 16)
                    sp.dma_start(dt_bias[:], w_gate["dt_bias"].partition_broadcast(P)).then_inc(small_loaded, 16)
                    sp.dma_start(a_log[:], w_gate["a_log"].partition_broadcast(P)).then_inc(small_loaded, 16)
            sp.wait_ge(rows_made, 1)
            sp.dma_start(g_rows_dram, g_rows[:]).then_inc(g_out, 16)
            sp.wait_ge(g_out, 16)

        @block.gpsimd
        def _(pool):
            step = Step(pool, pool_step)
            constants_program(pool, step, c)
            step(pool.memset(c["ones"][:], 1.0), constants_made)

        @block.tensor
        def _(pe):
            def multiply_gates(half):
                pe.wait_ge(gate_low, 1)
                pe.wait_ge(low_made, NT * (half + 1))
                out, ts = ab_rows[:, half * HALF:(half + 1) * HALF], slice(half * HALF, (half + 1) * HALF)
                for k in range(KT):
                    pe.matmul(out, ab_hi[:, k, :], xh[:, k, ts], start=(k == 0), stop=False)
                    pe.matmul(out, ab_hi[:, k, :], xl[:, k, ts], start=False, stop=False)
                    mm = pe.matmul(out, ab_lo[:, k, :], xh[:, k, ts], start=False, stop=(k == KT - 1))
                mm.then_inc(ab_product, 1)

            pe.wait_ge(constants_made, 1)
            for t in range(NT):
                pe.wait_ge(x_loaded[t % 2], 16 * (t // 2 + 1))
                for half in range(2):
                    n = 2 * t + half
                    if n >= 2:
                        pe.wait_ge(low_made, n - 1)
                    for j in range(4):
                        k = 4 * half + j
                        mm = pe.transpose(turned[half][:, j * P:(j + 1) * P],
                                          x_tile[:, t % 2, k * P:(k + 1) * P], c["ident"][:])
                    mm.then_inc(x_turned, 1)
                if t == NT // 2 + 1:
                    multiply_gates(0)
            multiply_gates(1)
            pe.wait_ge(ab_copied, 2)
            for t in range(NT):
                mm = pe.transpose(ab[:, t, :], ab_sb[:, t * P:(t + 1) * P], c["ident"][0:2 * H, 0:2 * H])
            mm.then_inc(ab_made, 1)
            pe.wait_ge(g_made, 1)
            g = work[5][:].rearrange("p c h -> p (c h)")
            pe.matmul(cums[:, 0:NT * H], c["tri"][:], g, start=True, stop=True)
            pe.matmul(totals[:, 0:NT * H], c["ones"][:], g, start=True, stop=True).then_inc(g_summed, 1)
            pe.wait_ge(g_copied, 1)
            pe.transpose(rows[0:NT * H, 0:P], gates["g"][:].rearrange("p c h -> p (c h)"),
                         c["ident"][:]).then_inc(g_turned, 1)

        @block.scalar
        def _(act):
            step = Step(act, act_step)
            for n in range(2 * NT):
                t, half = n // 2, n % 2
                act.wait_ge(x_turned, n + 1)
                src = turned[half][:].rearrange("p (j t) -> p j t", j=4)
                step(act.activation(xh[:, 4 * half:4 * half + 4, t * P:(t + 1) * P], src, ACT.Copy), high_made)
                if n == 4:
                    act.wait_ge(small_loaded, 48)
                    step(act.activation(ab_hi[:], ab_raw[:], ACT.Copy), gate_high)
            for half in range(2):
                ts = slice(half * HALF, (half + 1) * HALF)
                act.wait_ge(ab_product, half + 1)
                step(act.activation(ab_sb[:, ts], ab_rows[:, ts], ACT.Copy), ab_copied)
            act.wait_ge(ab_made, 1)
            step(act.activation(work[0][:], ab[:, :, 0:H], ACT.Exp, scale=-1.0), exp_beta)
            act.wait_ge(decays_made, 1)
            step(act.activation(work[2][:], work[1][:], ACT.Exp))
            step(act.activation(a_log[:], a_log[:], ACT.Exp), exp_alpha)
            act.wait_ge(g_copied, 2)
            step(act.activation(gates["neg_beta_eg"][:], gates["g"][:], ACT.Exp))
            step(act.activation(gates["k_decay"][:], work[0][:], ACT.Exp))
            step(act.activation(gates["last"][:], totals[:, 0:NT * H].rearrange("p (c h) -> p c h", h=H), ACT.Exp))
            act.wait_ge(g_turned, 1)
            step(act.activation(g_rows[:], rows[0:NT * H, 0:P], ACT.Copy), rows_made)
            step(act.activation(work[4][:], work[0][:], ACT.Copy), e_made)

        @block.vector
        def _(dve):
            step = Step(dve, dve_step)
            for n in range(2 * NT):
                t, half = n // 2, n % 2
                dve.wait_ge(high_made, n + 1)
                src = turned[half][:].rearrange("p (j t) -> p j t", j=4)
                where = (slice(None), slice(4 * half, 4 * half + 4), slice(t * P, (t + 1) * P))
                step(dve.tensor_tensor(xl[where], src, xh[where].bitcast(F32), ALU.subtract), low_made)
                if n == 5:
                    dve.wait_ge(gate_high, 1)
                    step(dve.tensor_tensor(ab_lo[:], ab_raw[:], ab_hi[:].bitcast(F32), ALU.subtract), gate_low)
            bias = dt_bias[:].unsqueeze(1).to_broadcast([P, NT, H])
            dve.wait_ge(exp_beta, 1)
            step(dve.tensor_scalar(work[0][:], work[0][:], 1.0, None, ALU.add))
            step(dve.reciprocal(gates["beta"][:], work[0][:]))
            step(dve.tensor_tensor(work[3][:], ab[:, :, H:2 * H], bias, ALU.add))
            step(dve.scalar_tensor_tensor(work[1][:], work[3][:], -1.0, work[3][:], ALU.mult, ALU.min), decays_made)
            dve.wait_ge(exp_alpha, 1)
            log_one_plus(dve, step, work[2], work[1], work[4], work[0])
            step(dve.scalar_tensor_tensor(work[0][:], work[3][:], 0.0, work[1][:], ALU.max, ALU.add))
            step(dve.scalar_tensor_tensor(work[5][:], work[0][:], -1.0,
                                          a_log[:].unsqueeze(1).to_broadcast([P, NT, H]),
                                          ALU.mult, ALU.mult), g_made)
            dve.wait_ge(g_summed, 1)
            summed = cums[:, 0:NT * H].rearrange("p (c h) -> p c h", h=H)
            total = totals[:, 0:NT * H].rearrange("p (c h) -> p c h", h=H)
            step(dve.tensor_copy(gates["g"][:], summed), g_copied)
            step(dve.tensor_tensor(work[0][:], total, gates["g"][:], ALU.subtract), g_copied)
            dve.wait_ge(e_made, 1)
            step(dve.scalar_tensor_tensor(gates["neg_beta_eg"][:], gates["neg_beta_eg"][:], -1.0,
                                          gates["beta"][:], ALU.mult, ALU.mult))


def log_one_plus(dve, step, y, out, z2, series):
    step(dve.tensor_scalar(z2[:], y[:], 2.0, None, ALU.add))
    step(dve.reciprocal(out[:], z2[:]))
    step(dve.tensor_tensor(y[:], y[:], out[:], ALU.mult))
    step(dve.tensor_tensor(z2[:], y[:], y[:], ALU.mult))
    step(dve.tensor_scalar(series[:], z2[:], 2.0 / 17, None, ALU.mult))
    for odd in (15, 13, 11, 9, 7, 5, 3):
        step(dve.scalar_tensor_tensor(series[:], series[:], 2.0 / odd, z2[:], ALU.add, ALU.mult))
    step(dve.scalar_tensor_tensor(out[:], series[:], 2.0, y[:], ALU.add, ALU.mult))


STEPS = 8 * KT
AT_KK = 1
AT_QK = 2
AT_KEYS = 3
AT_FIRST = 7
AT_VALUES = 8
AT_LEVELS = 10
AT_CHUNKS = 28
AT_O_TAKE = 40
AT_SILU = 42
AT_Q_SUMS = 45
AT_Q_NORM = 49
AT_K_SQUARES = 50
AT_O_SQUARES = 52
AT_K_SUMS = 53
AT_DECAYS = 54
AT_O_SUMS = 55
AT_K_NORM = 57
AT_EXP = 58
AT_O_NORM = 59
AT_EG = 61


def delta_net(nc, c, xh, xl, gates, w_in, conv_w, norm_g, g_rows_dram, qkvz_space, o_t):
    with Phase(nc, "gdn") as ph:
        sb, ps, sem = ph.sb, ph.ps, ph.sem
        w_raw = sb("w_raw", [P, 2, KT, P])
        w_hi = sb("w_hi", [P, 2, KT, P], F32R)
        w_lo = sb("w_lo", [P, 2, KT, P], F32R)
        raw = sb("raw", [P, 2, TAPS - 1 + T])
        qkvz = qkvz_space[:].rearrange("p (b n) t -> p b n t", b=2)
        g_rows = sb("g_bc", [P, T])
        lower = sb("lower", [P, T])
        inv = sb("inv", [P, T])
        inv_t = sb("inv_t", [P, T])
        att_t = sb("att_t", [P, T])
        y = sb("y", [P, 2, T // 4])
        k_rows = sb("k_rows", [P, T])
        v_rows = sb("v_rows", [P, T])
        eg = sb("eg", [P, T])
        squares = sb("squares", [P, T])
        rest = sb("rest", [P, P])
        v_new = sb("v_new", [P, P])
        state = sb("state", [P, 2, P])
        taps = sb("taps", [P, TAPS, 3 * H])
        gain = sb("gain", [P, 1])
        eps = sb("gdn_eps", [P, 1])
        unit = [ps(f"unit{n}", [P, HALF]) for n in range(2)]
        w0, w1, w2 = ps("w0", [P, T]), ps("w1", [P, T]), ps("w2", [P, T])

        w_loaded = [sem(f"w_loaded{n}") for n in range(2)]
        g_loaded = sem("g_loaded")
        small = sem("taps_loaded")
        pool_step, act_step, dve_step = sem("gdn_pool_step"), sem("gdn_act_step"), sem("gdn_dve_step")
        w_high, w_low = sem("w_high"), sem("w_low")
        unit_made, unit_taken, conv_made = sem("unit_made"), sem("unit_taken"), sem("conv_made")
        z_ready, v_ready, squared = sem("z_ready"), sem("v_ready"), sem("squared")
        v_turned, bv_made = sem("v_turned"), sem("bv_made")
        o_squared, o_summed, o_rms, o_done = sem("o_squared"), sem("o_summed"), sem("o_rms"), sem("o_done")
        summed, norms, normed = sem("summed"), sem("norms"), sem("normed")
        exponents, decays, eg_made = sem("exponents"), sem("decays"), sem("eg_made")
        k_turned, kd_made = sem("k_turned"), sem("kd_made")
        kk_made, qk_made, att_made = sem("kk_made"), sem("qk_made"), sem("att_made")
        q_decayed, inv2_made, inv2_turned, inv2_copied = sem("q_decayed"), sem("inv2_made"), sem("inv2_turned"), sem("inv2_copied")
        y_product, y_made, x_product, x_made = sem("y_product"), sem("y_made"), sem("x_product"), sem("x_made")
        t_turned, t_copied = sem("t_turned"), sem("t_copied")
        ks_made, rest_made, tr_made, vn_made = sem("ks_made"), sem("rest_made"), sem("tr_made"), sem("vn_made")
        ds_made, s_made, o_made, o_taken = sem("ds_made"), sem("s_made"), sem("o_made"), sem("o_taken")
        block = ph.enter_context(nc.Block())

        def columns(j):
            head, kind = j // 4, j % 4
            return slice(kind * H * DK + head * DK, kind * H * DK + (head + 1) * DK)

        def chunk(n):
            return slice(n * P, (n + 1) * P)

        @block.sync
        def _(sp):
            def load(j):
                if j >= 2:
                    sp.wait_ge(w_low, j - 1)
                sp.dma_start(w_raw[:, j % 2], w_in[:, columns(j)].rearrange("(k p) n -> p k n", p=P)
                             ).then_inc(w_loaded[j % 2], 16)

            load(0)
            with nc.allow_non_contiguous_dma(reason="the taps of a channel on its partition"):
                for tap in range(TAPS):
                    sp.dma_start(taps[:, tap], conv_w[tap].rearrange("(b p) -> p b", p=P)).then_inc(small, 16)
                sp.dma_start(gain[:], norm_g.rearrange("(p n) -> p n", n=1)).then_inc(small, 16)
            load(1)
            for it in range(H + 1):
                if it < H:
                    if it:
                        sp.wait_ge(eg_made, it)
                    rows = g_rows_dram.rearrange("(c h) t -> h c t", h=H)[it]
                    sp.dma_start(g_rows[:].rearrange("p (c t) -> p c t", c=NT),
                                 rows.partition_broadcast(P)).then_inc(g_loaded, 16)
                for b in range(4):
                    j = 4 * it + b + 2
                    if it < H and j < 4 * H:
                        load(j)

        @block.gpsimd
        def _(pool):
            step = Step(pool, pool_step)

            def low_part(j):
                pool.wait_ge(w_high, j + 1)
                step(pool.tensor_tensor(w_lo[:, j % 2], w_raw[:, j % 2], w_hi[:, j % 2].bitcast(F32),
                                        ALU.subtract), w_low)

            low_part(0)
            for it in range(H + 1):
                p = it - 1
                for s in range(STEPS):
                    if it < H and s % 16 == 4 and 4 * it + s // 16 + 1 < 4 * H:
                        low_part(4 * it + s // 16 + 1)
                    if 0 <= p < H and s == AT_QK:
                        pool.wait_ge(qk_made, p + 1)
                        pool.wait_ge(eg_made, p + 1)
                        q = qkvz[:, p % 2, 0]
                        step(pool.tensor_tensor(q, q, eg[:], ALU.mult), q_decayed)

        @block.tensor
        def _(pe):
            def project(it, s):
                u, k = s // KT, s % KT
                n, j, half = 8 * it + u, 4 * it + u // 2, u % 2
                if k == 0:
                    pe.wait_ge(w_low, j + 1)
                    if n >= 2:
                        pe.wait_ge(unit_taken, n - 1)
                out, ts = unit[n % 2][:], slice(half * HALF, (half + 1) * HALF)
                pe.matmul(out, w_hi[:, j % 2, k, :], xh[:, k, ts], start=(k == 0), stop=False)
                pe.matmul(out, w_hi[:, j % 2, k, :], xl[:, k, ts], start=False, stop=False)
                mm = pe.matmul(out, w_lo[:, j % 2, k, :], xh[:, k, ts], start=False, stop=(k == KT - 1))
                if k == KT - 1:
                    mm.then_inc(unit_made, 1)

            def column_sums(outs, src, signal):
                for half, out in enumerate(outs):
                    ts = slice(half * HALF, (half + 1) * HALF)
                    mm = pe.matmul(out, c["ones"][:], src[:, ts], start=True, stop=True)
                mm.then_inc(signal, 1)

            def turn(out, src, signal, chunks):
                for n in chunks:
                    mm = pe.transpose(out[:, chunk(n)], src[:, chunk(n)], c["ident"][:])
                mm.then_inc(signal, 1)

            def head_work(p, s):
                q, k, v = (qkvz[:, p % 2, n] for n in range(3))
                if s == AT_KK:
                    pe.wait_ge(normed, 2 * p + 2)
                    if p:
                        pe.wait_ge(s_made, 9 * p)
                    for n in range(NT):
                        mm = pe.matmul(w2[:, chunk(n)], k[:, chunk(n)], k[:, chunk(n)], start=True, stop=True)
                    mm.then_inc(kk_made, 1)
                if s == AT_QK:
                    for n in range(NT):
                        mm = pe.matmul(w1[:, chunk(n)], k[:, chunk(n)], q[:, chunk(n)], start=True, stop=True)
                    mm.then_inc(qk_made, 1)
                if s == AT_FIRST:
                    for g in range(2):
                        pe.wait_ge(inv2_made, 2 * p + g + 1)
                        turn(w2, inv, inv2_turned, range(4 * g, 4 * g + 4))
                if s == AT_KEYS:
                    if p:
                        pe.wait_ge(o_rms, p)
                    turn(w0, k, k_turned, range(NT))
                if s == AT_VALUES:
                    pe.wait_ge(v_ready, p + 1)
                    pe.wait_ge(att_made, p + 1)
                    turn(w1, v, v_turned, range(NT))
                if s == AT_O_SUMS:
                    if p + 1 < H:
                        pe.wait_ge(norms, 2 * p + 4)
                    pe.wait_ge(o_squared, p + 1)
                    column_sums((w0[:, 0:HALF], w0[:, HALF:T]), eg, o_summed)
                level, what = (s - AT_LEVELS) // 3, (s - AT_LEVELS) % 3
                if 0 <= level < LEVELS:
                    for g in range(2):
                        if what == 0:
                            if level == 0:
                                pe.wait_ge(inv2_copied, 2 * p + g + 1)
                            else:
                                pe.wait_ge(x_made, 12 * p + 2 * level - 1 + g)
                            for n in range(4):
                                mm = pe.matmul(as_blocks(w2[:, g * HALF + 64 * n:g * HALF + 64 * n + 64], level),
                                               lower[:, chunk(4 * g + n)],
                                               right_halves(inv_t[:, chunk(4 * g + n)], level), start=True, stop=True)
                            mm.then_inc(y_product, 1)
                        if what == 1:
                            pe.wait_ge(y_made, 12 * p + 2 * level + g + 1)
                            if level == 0:
                                pe.wait_ge(bv_made, p + 1)
                            else:
                                pe.wait_ge(t_copied, 10 * p + 2 * level - 1 + g)
                            for n in range(4):
                                mm = pe.matmul(w1[:, g * HALF + 64 * n:g * HALF + 64 * n + 64],
                                               inv[:, chunk(4 * g + n)], y[:, g, 64 * n:64 * n + 64],
                                               start=True, stop=True)
                            mm.then_inc(x_product, 1)
                        if what == 2 and level < LEVELS - 1:
                            pe.wait_ge(x_made, 12 * p + 2 * level + g + 1)
                            if level == 0:
                                pe.wait_ge(kd_made, p + 1)
                            turn(w0, inv_t, t_turned, range(4 * g, 4 * g + 4))
                n, what = (s - AT_CHUNKS) // 3, (s - AT_CHUNKS) % 3
                if 0 <= n < NT and s >= AT_CHUNKS:
                    if what == 0:
                        pe.wait_ge(s_made, 9 * p + n + 1)
                        pe.wait_ge(q_decayed, p + 1)
                        pe.matmul(w2[:, 0:P], k[:, chunk(n)], state[:, n % 2], start=True, stop=True).then_inc(ks_made, 1)
                        pe.matmul(w0[:, chunk(n)], state[:, n % 2], q[:, chunk(n)], start=True, stop=False)
                    if what == 1:
                        pe.wait_ge(x_made, 12 * p + 12)
                        pe.wait_ge(rest_made, NT * p + n + 1)
                        pe.matmul(w2[:, HALF:HALF + P], inv_t[:, chunk(n)], rest[:], start=True, stop=True
                                  ).then_inc(tr_made, 1)
                    if what == 2:
                        pe.wait_ge(vn_made, NT * p + n + 1)
                        pe.matmul(w1[:, 0:P], k_rows[:, chunk(n)], v_new[:], start=True, stop=True).then_inc(ds_made, 1)
                        pe.matmul(w0[:, chunk(n)], v_new[:], att_t[:, chunk(n)], start=False, stop=True
                                  ).then_inc(o_made, 1)

            for it in range(H + 1):
                for s in range(STEPS):
                    if it < H:
                        project(it, s)
                    if it >= 1:
                        head_work(it - 1, s)
                    if it < H and s in (AT_Q_SUMS, AT_K_SUMS):
                        kind = int(s == AT_K_SUMS)
                        pe.wait_ge(squared, 2 * it + kind + 1)
                        if kind:
                            pe.wait_ge(norms, 2 * it + 1)
                        elif it:
                            pe.wait_ge(o_taken, 2 * it - 1)
                        column_sums((w1[:, HALF:T], w0[:, 0:HALF]), squares, summed)

        @block.scalar
        def _(act):
            step = Step(act, act_step)

            def high_part(j):
                act.wait_ge(w_loaded[j % 2], 16 * (j // 2 + 1))
                if j >= 2:
                    act.wait_ge(unit_made, 2 * j - 2)
                step(act.activation(w_hi[:, j % 2], w_raw[:, j % 2], ACT.Copy), w_high)

            def take_unit(it, u):
                n, block_n, half = 8 * it + u, 3 * it + u // 2, u % 2
                act.wait_ge(unit_made, n + 1)
                if u >= 6:
                    if it >= 2:
                        act.wait_ge(o_done, it - 1)
                    step(act.activation(qkvz[:, it % 2, 3, half * HALF:(half + 1) * HALF], unit[n % 2][:], ACT.Copy),
                         unit_taken)
                    return
                if block_n >= 2:
                    act.wait_ge(conv_made, 2 * block_n - 2)
                at = TAPS - 1 + half * HALF
                step(act.activation(raw[:, block_n % 2, at:at + HALF], unit[n % 2][:], ACT.Copy), unit_taken)

            def root(out, sums, signal, scale):
                nc.scalar.preload_act_table_set("natural_log_exp_and_others")
                for half, part in enumerate(sums):
                    step(act.activation(out[:, half * HALF:(half + 1) * HALF], part, ACT.Ln, bias=eps[:, 0:1],
                                        scale=scale))
                step(act.activation(out[:], out[:], ACT.Exp, scale=-0.5), signal)

            def own_work(h, s):
                q, k = qkvz[:, h % 2, 0], qkvz[:, h % 2, 1]
                if s == AT_SILU:
                    act.wait_ge(conv_made, 6 * h + 4)
                    step(act.activation(q, q, ACT.Silu))
                    step(act.activation(k, k, ACT.Silu))
                    if h:
                        act.wait_ge(normed, 2 * h)
                    step(act.activation(squares[:], q, ACT.Square), squared)
                if s == AT_K_SQUARES:
                    act.wait_ge(normed, 2 * h + 1)
                    step(act.activation(squares[:], k, ACT.Square), squared)
                if s in (AT_Q_SUMS, AT_K_SUMS):
                    act.wait_ge(summed, 2 * h + int(s == AT_K_SUMS) + 1)
                    root(squares, (w1[:, HALF:T], w0[:, 0:HALF]), norms, 1.0)
                if s == AT_EXP:
                    act.wait_ge(exponents, 2 * h + 1)
                    step(act.activation(lower[:], lower[:], ACT.Exp, scale=-1.0), decays)
                    act.wait_ge(exponents, 2 * h + 2)
                    step(act.activation(att_t[:], att_t[:], ACT.Exp), decays)
                if s == AT_EG:
                    if h:
                        act.wait_ge(o_done, h)
                    step(act.activation(eg[:], g_rows[:], ACT.Exp), eg_made)

            high_part(0)
            act.wait_ge(small, 16 * (TAPS + 1))
            for it in range(H + 1):
                p = it - 1
                for s in range(STEPS):
                    if it < H and s % 16 == 4 and 4 * it + s // 16 + 1 < 4 * H:
                        high_part(4 * it + s // 16 + 1)
                    if it < H and s % 8 == 0 and s:
                        take_unit(it, s // 8 - 1)
                    if it < H:
                        own_work(it, s)
                    if p < 0:
                        continue
                    if s == AT_O_SUMS:
                        act.wait_ge(o_summed, p + 1)
                        root(eg, (w0[:, 0:HALF], w0[:, HALF:T]), o_rms, 1.0 / DK)
                    if s == AT_KEYS:
                        act.wait_ge(k_turned, p + 1)
                        for n in range(NT):
                            step(act.activation(k_rows[:, chunk(n)], w0[:, chunk(n)], ACT.Copy,
                                                scale=gates["k_decay"][:, n, p:p + 1]),
                                 kd_made if n == NT - 1 else None)
                    if s == AT_FIRST:
                        for g in range(2):
                            act.wait_ge(inv2_turned, 2 * p + g + 1)
                            step(act.activation(inv_t[:, g * HALF:(g + 1) * HALF], w2[:, g * HALF:(g + 1) * HALF],
                                                ACT.Copy), inv2_copied)
                    level, what = (s - AT_LEVELS) // 3, (s - AT_LEVELS) % 3
                    if 0 <= level < LEVELS - 1 and what == 2:
                        for g in range(2):
                            act.wait_ge(t_turned, 10 * p + 2 * level + g + 1)
                            step(act.activation(inv[:, g * HALF:(g + 1) * HALF], w0[:, g * HALF:(g + 1) * HALF],
                                                ACT.Copy), t_copied)
                    if s == AT_O_TAKE:
                        act.wait_ge(o_made, NT * p + NT // 2)
                        step(act.activation(o_t[:, p, 0:HALF], w0[:, 0:HALF], ACT.Copy), o_taken)
                    if s == AT_O_SQUARES:
                        act.wait_ge(o_made, NT * p + NT)
                        step(act.activation(o_t[:, p, HALF:T], w0[:, HALF:T], ACT.Copy), o_taken)
                        step(act.activation(eg[:], o_t[:, p], ACT.Square), o_squared)
                if it < H:
                    take_unit(it, 7)
                    v, z = qkvz[:, it % 2, 2], qkvz[:, it % 2, 3]
                    act.wait_ge(conv_made, 6 * it + 6)
                    step(act.activation(v, v, ACT.Silu), v_ready)
                    step(act.activation(z, z, ACT.Silu), z_ready)

        @block.vector
        def _(dve):
            step = Step(dve, dve_step)
            step(dve.memset(raw[:, :, 0:TAPS - 1], 0.0))
            step(dve.memset(eps[:], RMS_EPS))
            dve.wait_ge(small, 16 * (TAPS + 1))

            def convolve(it, u, part):
                kind, half = u // 2, u % 2
                if part == 0:
                    dve.wait_ge(unit_taken, 8 * it + u + 1)
                src = raw[:, (3 * it + kind) % 2]
                out = qkvz[:, it % 2, kind, half * HALF:(half + 1) * HALF]
                tap = TAPS - 1 - part
                shifted = src[:, half * HALF + tap:half * HALF + tap + HALF]
                weight = taps[:, tap, kind * H + it:kind * H + it + 1]
                if part == 0:
                    step(dve.tensor_scalar(out, shifted, weight, None, ALU.mult))
                else:
                    step(dve.scalar_tensor_tensor(out, shifted, weight, out, ALU.mult, ALU.add),
                         conv_made if part == TAPS - 1 else None)

            def own_work(h, s):
                q, k = qkvz[:, h % 2, 0], qkvz[:, h % 2, 1]
                if s == AT_Q_NORM:
                    dve.wait_ge(norms, 2 * h + 1)
                    step(dve.scalar_tensor_tensor(q, q, DK ** -0.5, squares[:], ALU.mult, ALU.mult), normed)
                if s == AT_K_NORM:
                    dve.wait_ge(norms, 2 * h + 2)
                    step(dve.tensor_tensor(k, k, squares[:], ALU.mult), normed)
                if s == AT_DECAYS:
                    dve.wait_ge(g_loaded, 16 * (h + 1))
                    for n in range(NT):
                        step(dve.scalar_tensor_tensor(lower[:, chunk(n)], g_rows[:, chunk(n)],
                                                      gates["g"][:, n, h:h + 1], c["above_big"][:],
                                                      ALU.subtract, ALU.max), exponents if n == NT - 1 else None)
                    if h:
                        dve.wait_ge(o_made, NT * h)
                    for n in range(NT):
                        step(dve.scalar_tensor_tensor(att_t[:, chunk(n)], g_rows[:, chunk(n)],
                                                      gates["g"][:, n, h:h + 1], c["below_neg"][:],
                                                      ALU.subtract, ALU.min), exponents if n == NT - 1 else None)

            def head_work(p, s):
                if s == AT_KK:
                    dve.wait_ge(kk_made, p + 1)
                    dve.wait_ge(decays, 2 * p + 1)
                    for g in range(2):
                        for n in range(4 * g, 4 * g + 4):
                            step(dve.scalar_tensor_tensor(lower[:, chunk(n)], w2[:, chunk(n)],
                                                          gates["beta"][:, n, p:p + 1], lower[:, chunk(n)],
                                                          ALU.mult, ALU.mult))
                        four = slice(g * HALF, (g + 1) * HALF)
                        view = lambda ap: ap[:, four].rearrange("p (n t) -> p n t", n=4)
                        step(dve.tensor_tensor(view(inv), view(lower), c["odd_below"][:].unsqueeze(1).to_broadcast(
                            [P, 4, P]), ALU.mult))
                        step(dve.tensor_tensor(view(inv), view(inv), c["ident"][:].unsqueeze(1).to_broadcast(
                            [P, 4, P]), ALU.add), inv2_made)
                if s == AT_VALUES:
                    dve.wait_ge(v_turned, p + 1)
                    for n in range(NT):
                        step(dve.tensor_scalar(v_rows[:, chunk(n)], w1[:, chunk(n)], gates["beta"][:, n, p:p + 1], None,
                                               ALU.mult), bv_made if n == NT - 1 else None)
                    step(dve.memset(state[:, 0], 0.0), s_made)
                if s == AT_O_NORM:
                    dve.wait_ge(o_rms, p + 1)
                    dve.wait_ge(z_ready, p + 1)
                    step(dve.scalar_tensor_tensor(o_t[:, p], o_t[:, p], gain[:, 0:1], eg[:], ALU.mult, ALU.mult))
                    step(dve.tensor_tensor(o_t[:, p], o_t[:, p], qkvz[:, p % 2, 3], ALU.mult), o_done)
                if s == AT_QK:
                    dve.wait_ge(qk_made, p + 1)
                    dve.wait_ge(decays, 2 * p + 2)
                    step(dve.tensor_tensor(att_t[:, 0:HALF], w1[:, 0:HALF], att_t[:, 0:HALF], ALU.mult))
                    step(dve.tensor_tensor(att_t[:, HALF:T], w1[:, HALF:T], att_t[:, HALF:T], ALU.mult), att_made)
                level, what = (s - AT_LEVELS) // 3, (s - AT_LEVELS) % 3
                if 0 <= level < LEVELS:
                    for g in range(2):
                        four = slice(g * HALF, g * HALF + 256)
                        if what == 0:
                            dve.wait_ge(y_product, 12 * p + 2 * level + g + 1)
                            mask = c["level_mask"][:, level].unsqueeze(1).to_broadcast([P, 4, P // 2])
                            step(dve.tensor_tensor(y[:, g].rearrange("p (n t) -> p n t", n=4),
                                                   w2[:, four].rearrange("p (n t) -> p n t", n=4), mask, ALU.mult),
                                 y_made)
                        if what == 1:
                            dve.wait_ge(x_product, 12 * p + 2 * level + g + 1)
                            x = right_halves(inv_t[:, g * HALF:(g + 1) * HALF], level)
                            step(dve.tensor_tensor(x, x, as_blocks(w1[:, four], level), ALU.add), x_made)
                n, what = (s - AT_CHUNKS) // 3, (s - AT_CHUNKS) % 3
                if 0 <= n < NT and s >= AT_CHUNKS:
                    if what == 0:
                        dve.wait_ge(ks_made, NT * p + n + 1)
                        step(dve.scalar_tensor_tensor(rest[:], w2[:, 0:P], gates["neg_beta_eg"][:, n, p:p + 1],
                                                      v_rows[:, chunk(n)], ALU.mult, ALU.add), rest_made)
                    if what == 1:
                        dve.wait_ge(tr_made, NT * p + n + 1)
                        step(dve.tensor_copy(v_new[:], w2[:, HALF:HALF + P]), vn_made)
                    if what == 2:
                        dve.wait_ge(ds_made, NT * p + n + 1)
                        step(dve.scalar_tensor_tensor(state[:, (n + 1) % 2], state[:, n % 2],
                                                      gates["last"][:, n, p:p + 1], w1[:, 0:P], ALU.mult, ALU.add),
                             s_made)

            for it in range(H + 1):
                for s in range(STEPS):
                    if it < H:
                        own_work(it, s)
                    if it >= 1:
                        head_work(it - 1, s)
                    u, part = s // 8 - 1, (s % 8 - 1) // 2
                    if it < H and 0 <= u < 6 and s % 2 == 1:
                        convolve(it, u, part)


def mixer_out(nc, c, o, turned, residual, w_out, ln_g, ln_b, w_hi, w_lo, x1, name):
    with Phase(nc, name) as ph:
        sb, ps, sem = ph.sb, ph.ps, ph.sem
        RAW = 3
        w_raw = sb("w_raw", [P, RAW, D])
        o_hi, o_lo = sb("o_hi", [P, 2, KT, P], F32R), sb("o_lo", [P, 2, KT, P], F32R)
        old = sb("old", [P, 2, D])
        mixed = sb("mixed", [P, 2, D])
        gain, shift = sb("gain", [P, D]), sb("shift", [P, D])
        stats, moments = sb("stats", [P, 2, 2, 6]), sb("moments", [P, 2, 2])
        rstd, eps = sb("rstd", [P, 2]), sb("eps", [P, 1])
        out = [ps(f"y{n}", [P, D]) for n in range(3)]
        flip = [ps(f"flip{n}", [P, HALF]) for n in range(2)]
        w_loaded = [sem(f"w_loaded{n}") for n in range(RAW)]
        x_loaded = [sem(f"x_loaded{n}") for n in range(2)]
        ln_loaded = sem("ln_loaded")
        act_step, dve_step, pool_step = sem("act_step"), sem("dve_step"), sem("pool_step")
        w_high, w_low, o_high, o_low = sem("w_high"), sem("w_low"), sem("o_high"), sem("o_low")
        flipped, y_made, mixed_made = sem("flipped"), sem("y_made"), sem("mixed_made")
        var_made, rstd_made, scaled, x_made = sem("var_made"), sem("rstd_made"), sem("scaled"), sem("x_made")
        eps_made = sem("eps_made")
        block = ph.enter_context(nc.Block())

        @block.sync
        def _(sp):
            def load_x(t):
                if t >= 2:
                    sp.wait_ge(mixed_made, t - 1)
                sp.dma_start(old[:, t % 2], residual[t * P:(t + 1) * P, :]).then_inc(x_loaded[t % 2], 16)

            for k in range(KT):
                if k >= RAW:
                    sp.wait_ge(w_low, k - RAW + 1)
                sp.dma_start(w_raw[:, k % RAW], w_out[k * P:(k + 1) * P, :]).then_inc(w_loaded[k % RAW], 16)
            load_x(0)
            load_x(1)
            sp.dma_start(gain[:], ln_g.partition_broadcast(P)).then_inc(ln_loaded, 16)
            sp.dma_start(shift[:], ln_b.partition_broadcast(P)).then_inc(ln_loaded, 16)
            for t in range(2, NT):
                load_x(t)

        @block.tensor
        def _(pe):
            def flip_tile(t):
                for half in range(2):
                    n = 2 * t + half
                    if n >= 2:
                        pe.wait_ge(o_low, n - 1)
                    for j in range(4):
                        k = 4 * half + j
                        mm = pe.transpose(flip[half][:, j * P:(j + 1) * P], o[:, t, k * P:(k + 1) * P], c["ident"][:])
                    mm.then_inc(flipped, 1)

            def multiply(t, k):
                if k == 0 and t >= 3:
                    pe.wait_ge(mixed_made, t - 2)
                y = out[t % 3]
                for half in range(2):
                    cols = slice(half * HALF, (half + 1) * HALF)
                    pe.matmul(y[:, cols], o_hi[:, t % 2, k, :], w_hi[:, k, cols], start=(k == 0), stop=False)
                    pe.matmul(y[:, cols], o_hi[:, t % 2, k, :], w_lo[:, k, cols], start=False, stop=False)
                    mm = pe.matmul(y[:, cols], o_lo[:, t % 2, k, :], w_hi[:, k, cols], start=False,
                                   stop=(k == KT - 1))
                if k == KT - 1:
                    mm.then_inc(y_made, 1)

            if turned:
                flip_tile(0)
                flip_tile(1)
            pe.wait_ge(o_low, 4)
            for k in range(KT):
                pe.wait_ge(w_low, k + 1)
                multiply(0, k)
                multiply(1, k)
                if turned and k == KT // 2:
                    flip_tile(2)
            for t in range(2, NT):
                pe.wait_ge(o_low, 2 * t + 2)
                for k in range(KT):
                    multiply(t, k)
                    if turned and k == KT // 2 and t + 1 < NT:
                        flip_tile(t + 1)

        def halves(t):
            for half in range(2):
                ks = slice(4 * half, 4 * half + 4)
                src = flip[half][:].rearrange("p (k t) -> p k t", k=4) if turned else o[:, ks, t * P:(t + 1) * P]
                yield 2 * t + half, ks, src

        @block.scalar
        def _(act):
            step = Step(act, act_step)

            def o_part(t):
                if t >= 2:
                    act.wait_ge(y_made, t - 1)
                for n, ks, src in halves(t):
                    if turned:
                        act.wait_ge(flipped, n + 1)
                    step(act.activation(o_hi[:, t % 2, ks], src, ACT.Copy), o_high)

            o_part(0)
            o_part(1)
            for k in range(KT):
                act.wait_ge(w_loaded[k % RAW], 16 * (k // RAW + 1))
                step(act.activation(w_hi[:, k], w_raw[:, k % RAW], ACT.Copy), w_high)
            act.wait_ge(eps_made, 1)
            nc.scalar.preload_act_table_set("natural_log_exp_and_others")
            for t in range(NT):
                if t + 2 < NT:
                    o_part(t + 2)
                act.wait_ge(var_made, t + 1)
                r = rstd[:, t % 2:t % 2 + 1]
                step(act.activation(r, moments[:, t % 2, 1:2], ACT.Ln, bias=eps[:, 0:1]))
                step(act.activation(r, r, ACT.Exp, scale=-0.5), rstd_made)

        @block.vector
        def _(dve):
            step = Step(dve, dve_step)
            step(dve.memset(eps[:], LN_EPS), eps_made)

            def o_part(t):
                for n, ks, src in halves(t):
                    dve.wait_ge(o_high, n + 1)
                    step(dve.tensor_tensor(o_lo[:, t % 2, ks], src, o_hi[:, t % 2, ks].bitcast(F32),
                                           ALU.subtract), o_low)

            o_part(0)
            o_part(1)
            for k in range(KT):
                dve.wait_ge(w_high, k + 1)
                step(dve.tensor_tensor(w_lo[:, k], w_raw[:, k % RAW], w_hi[:, k].bitcast(F32), ALU.subtract), w_low)
            for t in range(NT):
                b = t % 2
                dve.wait_ge(x_loaded[b], 16 * (t // 2 + 1))
                dve.wait_ge(y_made, t + 1)
                if t >= 2:
                    dve.wait_ge(x_made, t - 1)
                step(dve.scalar_tensor_tensor(mixed[:, b], old[:, b], ALPHA, out[t % 3][:], ALU.mult, ALU.add),
                     mixed_made)
                for half in range(2):
                    step(dve.bn_stats(stats[:, b, half], mixed[:, b, half * HALF:(half + 1) * HALF]))
                step(dve.bn_aggr(moments[:, b], stats[:, b]), var_made)
                if t + 2 < NT:
                    o_part(t + 2)
                dve.wait_ge(rstd_made, t + 1)
                step(dve.tensor_scalar(mixed[:, b], mixed[:, b], moments[:, b, 0:1], rstd[:, b:b + 1],
                                       ALU.subtract, ALU.mult))
                if t == 0:
                    dve.wait_ge(ln_loaded, 32)
                step(dve.tensor_tensor(mixed[:, b], mixed[:, b], gain[:], ALU.mult), scaled)

        @block.gpsimd
        def _(pool):
            step = Step(pool, pool_step)
            pool.wait_ge(ln_loaded, 32)
            for t in range(NT):
                pool.wait_ge(scaled, t + 1)
                step(pool.tensor_tensor(x1[:, t], mixed[:, t % 2], shift[:], ALU.add), x_made)


def gated_embedding(nc, c, x1, p_emb, w_gate, w_proj, out_dram, xh, xl, stored, name):
    KP = p_emb.shape[1] // P
    with Phase(nc, name) as ph:
        sb, ps, sem = ph.sb, ph.ps, ph.sem
        RAW, KW = 2, KP + KT
        w_raw = sb("w_raw", [P, RAW, D])
        w_hi, w_lo = sb("w_hi", [P, KW, D], F32R), sb("w_lo", [P, KW, D], F32R)
        p_hi, p_lo = sb("p_hi", [P, KP, P], F32R), sb("p_lo", [P, KP, P], F32R)
        a_hi, a_lo = sb("a_hi", [P, 2, KT, P], F32R), sb("a_lo", [P, 2, KT, P], F32R)
        p_tile = sb("p_tile", [P, 2, KP * P])
        tanh = sb("tanh", [P, HALF])
        flip = [ps(f"flip{n}", [P, HALF]) for n in range(2)]
        gate = [ps(f"gate{n}", [P, D]) for n in range(2)]
        proj = ps("proj", [P, D])
        w_loaded = [sem(f"w_loaded{n}") for n in range(RAW)]
        p_loaded = [sem(f"p_loaded{n}") for n in range(2)]
        act_step, dve_step = sem("act_step"), sem("dve_step")
        w_high, w_low = sem("w_high"), sem("w_low")
        flipped, high, low = sem("flipped"), sem("high"), sem("low")
        proj_made, gate_made, tanh_made, proj_used, half_used = (
            sem("proj_made"), sem("gate_made"), sem("tanh_made"), sem("proj_used"), sem("half_used"))
        block = ph.enter_context(nc.Block())
        last = xh is None

        def two(kind, t):
            return [(kind, t, 0), (kind, t, 1)]

        pieces = [("p", 0, 0)] + two("x1", 0) + two("x1", 1) + [("p", 1, 0)] + two("x1", 2)
        for t in range(2, NT):
            pieces += (two("x2", t - 2) if not last else []) + [("p", t, 0)]
            pieces += two("x1", t + 1) if t + 1 < NT else []
        if not last:
            pieces += two("x2", NT - 2) + two("x2", NT - 1)
        order = {piece: n for n, piece in enumerate(pieces)}

        def source(piece):
            kind, t, half = piece
            if kind == "p":
                return [p_tile[:, t % 2, k * P:(k + 1) * P] for k in range(KP)]
            return [x1[:, t, (4 * half + j) * P:(4 * half + j + 1) * P] for j in range(4)]

        def targets(piece):
            kind, t, half = piece
            if kind == "p":
                return [p_hi[:], p_lo[:]]
            if kind == "x1":
                return [a[:, t % 2, 4 * half:4 * half + 4] for a in (a_hi, a_lo)]
            return [a[:, 4 * half:4 * half + 4, t * P:(t + 1) * P] for a in (xh, xl)]

        @block.sync
        def _(sp):
            def load_w(k):
                if k >= RAW:
                    sp.wait_ge(w_low, k - RAW + 1)
                src = w_proj[k * P:(k + 1) * P, :] if k < KP else w_gate[(k - KP) * P:(k - KP + 1) * P, :]
                sp.dma_start(w_raw[:, k % RAW], src).then_inc(w_loaded[k % RAW], 16)

            def load_p(t):
                sp.dma_start(p_tile[:, t % 2], p_emb[t * P:(t + 1) * P, :]).then_inc(p_loaded[t % 2], 16)

            load_p(0)
            load_p(1)
            for k in range(KW):
                load_w(k)
            for t in range(NT):
                if t + 2 < NT:
                    sp.wait_ge(low, order[("p", t, 0)] + 1)
                    load_p(t + 2)
                sp.wait_ge(half_used, 2 * t + 2)
                sp.dma_start(out_dram[t * P:(t + 1) * P, :], x1[:, t]).then_inc(stored, 16)
            sp.wait_ge(stored, 16 * NT)

        @block.tensor
        def _(pe):
            def flip_piece(piece):
                n = order[piece]
                if n >= 2:
                    pe.wait_ge(low, n - 1)
                if piece[0] == "x2":
                    pe.wait_ge(half_used, 2 * piece[1] + 2)
                if piece[0] == "p":
                    pe.wait_ge(p_loaded[piece[1] % 2], 16 * (piece[1] // 2 + 1))
                for j, src in enumerate(source(piece)):
                    mm = pe.transpose(flip[n % 2][:, j * P:(j + 1) * P], src, c["ident"][:])
                mm.then_inc(flipped, 1)

            def flip_both(kind, t):
                if kind == "x1" or not last:
                    flip_piece((kind, t, 0))
                    flip_piece((kind, t, 1))

            def multiply(out, hi, lo, k, first, end):
                for half in range(2):
                    cols = slice(half * HALF, (half + 1) * HALF)
                    pe.matmul(out[:, cols], hi, w_hi[:, k, cols], start=first, stop=False)
                    pe.matmul(out[:, cols], hi, w_lo[:, k, cols], start=False, stop=False)
                    mm = pe.matmul(out[:, cols], lo, w_hi[:, k, cols], start=False, stop=end)
                return mm

            def project(t):
                pe.wait_ge(low, order[("p", t, 0)] + 1)
                if t >= 1:
                    pe.wait_ge(proj_used, 2 * t)
                for k in range(KP):
                    mm = multiply(proj, p_hi[:, k], p_lo[:, k], k, k == 0, k == KP - 1)
                mm.then_inc(proj_made, 1)

            def gates(t, k):
                if k == 0:
                    pe.wait_ge(low, order[("x1", t, 1)] + 1)
                    if t >= 2:
                        pe.wait_ge(tanh_made, 2 * t - 2)
                mm = multiply(gate[t % 2], a_hi[:, t % 2, k], a_lo[:, t % 2, k], KP + k, k == 0, k == KT - 1)
                if k == KT - 1:
                    mm.then_inc(gate_made, 1)

            flip_piece(("p", 0, 0))
            flip_both("x1", 0)
            flip_both("x1", 1)
            pe.wait_ge(w_low, KP)
            project(0)
            flip_piece(("p", 1, 0))
            for k in range(KT):
                pe.wait_ge(w_low, KP + k + 1)
                gates(0, k)
                gates(1, k)
            flip_both("x1", 2)
            for t in range(2, NT):
                for k in range(KT):
                    gates(t, k)
                    if k == 1:
                        flip_both("x2", t - 2)
                    if k == 2:
                        project(t - 1)
                    if k == 3:
                        flip_piece(("p", t, 0))
                    if k == 4 and t + 1 < NT:
                        flip_both("x1", t + 1)
            project(NT - 1)
            flip_both("x2", NT - 2)
            flip_both("x2", NT - 1)

        @block.scalar
        def _(act):
            step = Step(act, act_step)

            def high_part(piece):
                n = order[piece]
                if piece[0] == "x1" and piece[1] >= 2:
                    act.wait_ge(gate_made, piece[1] - 1)
                if piece[0] == "p" and piece[1] >= 1:
                    act.wait_ge(proj_made, piece[1])
                act.wait_ge(flipped, n + 1)
                width = len(source(piece))
                step(act.activation(targets(piece)[0], flip[n % 2][:, 0:width * P].rearrange("p (k t) -> p k t", t=P),
                                    ACT.Copy), high)

            def high_parts(kind, t):
                if kind == "x1" or not last:
                    high_part((kind, t, 0))
                    high_part((kind, t, 1))

            def sigmoid(t, half):
                act.wait_ge(gate_made, t + 1)
                if 2 * t + half:
                    act.wait_ge(half_used, 2 * t + half)
                step(act.activation(tanh[:], gate[t % 2][:, half * HALF:(half + 1) * HALF], ACT.Tanh, scale=0.5),
                     tanh_made)

            def high_weights(k):
                act.wait_ge(w_loaded[k % RAW], 16 * (k // RAW + 1))
                step(act.activation(w_hi[:, k], w_raw[:, k % RAW], ACT.Copy), w_high)

            high_part(("p", 0, 0))
            high_parts("x1", 0)
            high_parts("x1", 1)
            for k in range(KP):
                high_weights(k)
            high_weights(KP)
            high_part(("p", 1, 0))
            for k in range(KP + 1, KW):
                high_weights(k)
            sigmoid(0, 0)
            high_parts("x1", 2)
            sigmoid(0, 1)
            for t in range(2, NT):
                high_parts("x2", t - 2)
                sigmoid(t - 1, 0)
                high_part(("p", t, 0))
                if t + 1 < NT:
                    high_part(("x1", t + 1, 0))
                sigmoid(t - 1, 1)
                if t + 1 < NT:
                    high_part(("x1", t + 1, 1))
            sigmoid(NT - 1, 0)
            high_parts("x2", NT - 2)
            sigmoid(NT - 1, 1)
            high_parts("x2", NT - 1)

        @block.vector
        def _(dve):
            step = Step(dve, dve_step)

            def low_part(piece):
                n = order[piece]
                dve.wait_ge(high, n + 1)
                hi, lo = targets(piece)
                width = len(source(piece))
                step(dve.tensor_tensor(lo, flip[n % 2][:, 0:width * P].rearrange("p (k t) -> p k t", t=P),
                                       hi.bitcast(F32), ALU.subtract), low)

            def low_parts(kind, t):
                if kind == "x1" or not last:
                    low_part((kind, t, 0))
                    low_part((kind, t, 1))

            def add(t, half):
                dve.wait_ge(proj_made, t + 1)
                cols = slice(half * HALF, (half + 1) * HALF)
                dve.wait_ge(tanh_made, 2 * t + half + 1)
                step(dve.scalar_tensor_tensor(tanh[:], tanh[:], 1.0, proj[:, cols], ALU.add, ALU.mult), proj_used)
                step(dve.scalar_tensor_tensor(x1[:, t, cols], tanh[:], 0.5, x1[:, t, cols], ALU.mult, ALU.add),
                     half_used)

            def low_weights(k):
                dve.wait_ge(w_high, k + 1)
                step(dve.tensor_tensor(w_lo[:, k], w_raw[:, k % RAW], w_hi[:, k].bitcast(F32), ALU.subtract), w_low)

            low_part(("p", 0, 0))
            low_parts("x1", 0)
            low_parts("x1", 1)
            for k in range(KP + 1):
                low_weights(k)
            low_part(("p", 1, 0))
            for k in range(KP + 1, KW):
                low_weights(k)
            add(0, 0)
            low_parts("x1", 2)
            add(0, 1)
            for t in range(2, NT):
                low_parts("x2", t - 2)
                add(t - 1, 0)
                low_part(("p", t, 0))
                if t + 1 < NT:
                    low_part(("x1", t + 1, 0))
                add(t - 1, 1)
                if t + 1 < NT:
                    low_part(("x1", t + 1, 1))
            add(NT - 1, 0)
            low_parts("x2", NT - 2)
            add(NT - 1, 1)
            low_parts("x2", NT - 1)


BF16 = mybir.dt.bfloat16
FH = 16
DH = 64
PAIRS = FH // 2
WIDTH = FH * DH


def fox_values(nc, c, xh, xl, w_in, b_f, c_rows, values, gate_z):
    with Phase(nc, "fv") as ph:
        sb, ps, sem = ph.sb, ph.ps, ph.sem
        RAW, PANELS = 3, 4
        w_raw = sb("w_raw", [P, RAW, HALF])
        w_hi, w_lo = sb("w_hi", [P, 2, KT, HALF], F32R), sb("w_lo", [P, 2, KT, HALF], F32R)
        f_raw, f_hi, f_lo = (sb("f_raw", [P, KT, FH]), sb("f_hi", [P, KT, FH], F32R), sb("f_lo", [P, KT, FH], F32R))
        bias = sb("bias", [P, FH])
        work = [sb(f"work{n}", [P, NT, FH]) for n in range(5)]
        rows = sb("rows", [P, P])
        f_rows = gate_z[0:FH, NT - 1]
        bank = [ps(f"bank{n}", [P, HALF]) for n in range(8)]
        w_loaded = [sem(f"w_loaded{n}") for n in range(RAW)]
        small = sem("small")
        act_step, dve_step = sem("act_step"), sem("dve_step")
        w_high, w_low, f_high, f_low = sem("w_high"), sem("w_low"), sem("f_high"), sem("f_low")
        made, taken, f_made, f_log, c_summed, c_ready, c_turned = (
            sem("made"), sem("taken"), sem("f_made"), sem("f_log"), sem("c_summed"), sem("c_ready"), sem("c_turned"))
        f_product, f_copied = sem("f_product"), sem("f_copied")
        abs_made, exp_made, rows_made, stored = sem("abs_made"), sem("exp_made"), sem("rows_made"), sem("stored")
        block = ph.enter_context(nc.Block())
        F = NT * FH

        @block.sync
        def _(sp):
            sp.dma_start(f_raw[:], w_in[:, 4 * WIDTH:4 * WIDTH + FH].rearrange("(k p) n -> p k n", p=P)
                         ).then_inc(small, 16)
            sp.dma_start(bias[:], b_f.partition_broadcast(P)).then_inc(small, 16)
            for n in range(PANELS):
                for k in range(KT):
                    m = n * KT + k
                    if m >= RAW:
                        sp.wait_ge(w_low, m - RAW + 1)
                    sp.dma_start(w_raw[:, m % RAW], w_in[k * P:(k + 1) * P, 2 * WIDTH + n * HALF:2 * WIDTH + (n + 1) * HALF]
                                 ).then_inc(w_loaded[m % RAW], 16)
            sp.wait_ge(rows_made, 1)
            sp.dma_start(c_rows, rows[:]).then_inc(stored, 16)
            sp.wait_ge(stored, 16)

        @block.tensor
        def _(pe):
            def multiply(n, t, k):
                ts, b = slice(t * P, (t + 1) * P), n % 2
                if k == 0 and n >= 1:
                    pe.wait_ge(taken, (n - 1) * NT + t + 1)
                pe.matmul(bank[t][:], xh[:, k, ts], w_hi[:, b, k], start=(k == 0), stop=False)
                pe.matmul(bank[t][:], xh[:, k, ts], w_lo[:, b, k], start=False, stop=False)
                mm = pe.matmul(bank[t][:], xl[:, k, ts], w_hi[:, b, k], start=False, stop=(k == KT - 1))
                if k == KT - 1:
                    mm.then_inc(made, 1)

            pe.wait_ge(f_low, 1)
            for k in range(KT):
                for half in range(2):
                    out, ts = bank[NT - 2 + half][0:FH], slice(half * HALF, (half + 1) * HALF)
                    pe.matmul(out, f_hi[:, k], xh[:, k, ts], start=(k == 0), stop=False)
                    pe.matmul(out, f_hi[:, k], xl[:, k, ts], start=False, stop=False)
                    mm = pe.matmul(out, f_lo[:, k], xh[:, k, ts], start=False, stop=(k == KT - 1))
            mm.then_inc(f_product, 1)
            for k in range(KT):
                pe.wait_ge(w_low, k + 1)
                for t in range(NT):
                    if k == 0 and t == NT - 2:
                        pe.wait_ge(f_copied, 2)
                    multiply(0, t, k)
            small_bank = bank[NT - 1]
            for n in range(1, PANELS):
                pe.wait_ge(w_low, (n + 1) * KT)
                for t in range(NT):
                    if n == 1 and t == 1:
                        pe.wait_ge(taken, NT)
                        for i in range(NT):
                            mm = pe.transpose(small_bank[:, i * FH:(i + 1) * FH], f_rows[:, i * P:(i + 1) * P],
                                              c["ident"][0:FH, 0:FH])
                        mm.then_inc(f_made, 1)
                    if n == 1 and t == NT - 1:
                        pe.wait_ge(abs_made, 1)
                    if n == 2 and t == 1:
                        pe.wait_ge(f_log, 1)
                        pe.wait_ge(taken, 2 * NT)
                        for i in range(NT):
                            out = small_bank[:, i * FH:(i + 1) * FH]
                            for before in range(i):
                                pe.matmul(out, c["ones"][:], work[3][:, before], start=(before == 0), stop=False)
                            mm = pe.matmul(out, c["tri"][:], work[3][:, i], start=(i == 0), stop=True)
                        mm.then_inc(c_summed, 1)
                    if n == 2 and t == 3:
                        pe.wait_ge(c_ready, 1)
                        pe.transpose(small_bank[:, 0:P], work[4][:].rearrange("p t h -> p (t h)"), c["ident"][:]
                                     ).then_inc(c_turned, 1)
                    if n == 2 and t == NT - 1:
                        pe.wait_ge(rows_made, 1)
                    for k in range(KT):
                        multiply(n, t, k)

        @block.scalar
        def _(act):
            step = Step(act, act_step)

            def high(m):
                n, k = m // KT, m % KT
                act.wait_ge(w_loaded[m % RAW], 16 * (m // RAW + 1))
                if n >= 2:
                    act.wait_ge(made, (n - 1) * NT)
                step(act.activation(w_hi[:, n % 2, k], w_raw[:, m % RAW], ACT.Copy), w_high)

            act.wait_ge(small, 32)
            step(act.activation(f_hi[:], f_raw[:], ACT.Copy), f_high)
            for m in range(2):
                high(m)
            act.wait_ge(f_product, 1)
            for half in range(2):
                step(act.activation(f_rows[:, half * HALF:(half + 1) * HALF], bank[NT - 2 + half][0:FH], ACT.Copy),
                     f_copied)
            for m in range(2, 2 * KT):
                high(m)
            for n in range(PANELS):
                for t in range(NT):
                    act.wait_ge(made, n * NT + t + 1)
                    half = n % 2
                    cols = slice(half * HALF, (half + 1) * HALF)
                    if n < 2:
                        step(act.activation(values[:, t, cols], bank[t][:], ACT.Copy), taken)
                    else:
                        step(act.activation(gate_z[:, t, cols], bank[t][:], ACT.Silu), taken)
                    if n == 2 and t == 4:
                        act.wait_ge(c_turned, 1)
                        step(act.activation(rows[:], bank[NT - 1][:, 0:P], ACT.Copy), rows_made)
                if n == 0:
                    act.wait_ge(abs_made, 1)
                    step(act.activation(work[1][:], work[1][:], ACT.Exp), exp_made)
                if n + 2 < PANELS:
                    for k in range(KT):
                        high((n + 2) * KT + k)

        @block.vector
        def _(dve):
            step = Step(dve, dve_step)

            def low(m):
                n, k = m // KT, m % KT
                dve.wait_ge(w_high, m + 1)
                step(dve.tensor_tensor(w_lo[:, n % 2, k], w_raw[:, m % RAW], w_hi[:, n % 2, k].bitcast(F32),
                                       ALU.subtract), w_low)

            dve.wait_ge(f_high, 1)
            step(dve.tensor_tensor(f_lo[:], f_raw[:], f_hi[:].bitcast(F32), ALU.subtract), f_low)
            for m in range(2 * KT):
                low(m)
            dve.wait_ge(f_made, 1)
            small_bank = bank[NT - 1][:, 0:F].rearrange("p (t h) -> p t h", h=FH)
            step(dve.tensor_tensor(work[0][:], small_bank, bias[:].unsqueeze(1).to_broadcast([P, NT, FH]), ALU.add))
            step(dve.scalar_tensor_tensor(work[1][:], work[0][:], -1.0, work[0][:], ALU.mult, ALU.min), abs_made)
            dve.wait_ge(exp_made, 1)
            log_one_plus(dve, step, work[1], work[2], work[4], work[3])
            step(dve.scalar_tensor_tensor(work[3][:], work[0][:], 0.0, work[2][:], ALU.min, ALU.subtract), f_log)
            for m in range(2 * KT, 3 * KT):
                low(m)
            dve.wait_ge(c_summed, 1)
            step(dve.tensor_scalar(work[4][:], small_bank, -1.0, None, ALU.mult), c_ready)
            for m in range(3 * KT, PANELS * KT):
                low(m)


F_STEPS = 32
AT_SUMS = 1
AT_ITEMS = 7
ITEMS = 2 * NT
LAG_TURN, LAG_OUT = 2, 3


def fox_attention(nc, c, xh, xl, w_in, q_gain, k_gain, c_rows, values, gate_z):
    with Phase(nc, "fa") as ph:
        sb, ps, sem = ph.sb, ph.ps, ph.sem
        w_raw = sb("w_raw", [P, 2, KT, P])
        w_hi, w_lo = sb("w_hi", [P, 2, KT, P], F32R), sb("w_lo", [P, 2, KT, P], F32R)
        qk = sb("qk", [P, 2, 2, T])
        root = sb("root", [P, 2, T])
        decay = sb("decay", [P, 2, T])
        probs = sb("probs", [P, 3, T])
        probs_t = sb("probs_t", [P, 2, T])
        halves = sb("halves", [P, P])
        ident_b, mask_b = sb("ident_b", [P, P], BF16), sb("mask_b", [P, P], BF16)
        gains = sb("gains", [P, 2])
        top, total, share = sb("top", [P, 4]), sb("total", [P, 4]), sb("share", [P, 4])
        eps = sb("eps", [P, 1])
        unit = [ps(f"unit{n}", [P, HALF]) for n in range(2)]
        scores, turned = ps("scores", [P, T]), ps("turned", [P, T])
        result, spare = ps("result", [P, HALF]), ps("spare", [P, HALF])
        w_loaded = [sem(f"w_loaded{n}") for n in range(2)]
        d_loaded = [sem(f"d_loaded{n}") for n in range(2)]
        small = sem("small")
        act_step, dve_step, pool_step = sem("act_step"), sem("dve_step"), sem("pool_step")
        ready = sem("constants")
        w_high, w_low, unit_made, unit_taken = sem("w_high"), sem("w_low"), sem("unit_made"), sem("unit_taken")
        squared, summed, normed = sem("squared"), sem("summed"), sem("normed")
        rooted, roots = sem("rooted"), sem("roots")
        scored, biased, topped, exped = sem("scored"), sem("biased"), sem("topped"), sem("exped")
        flipped, flip_a, flip_d, result_made, result_used = (
            sem("flipped"), sem("flip_a"), sem("flip_d"), sem("result_made"), sem("result_used"))
        block = ph.enter_context(nc.Block())

        def items_of(step):
            lo, hi = step - AT_ITEMS, step - AT_ITEMS + 1
            span, n = F_STEPS - AT_ITEMS, ITEMS + LAG_OUT
            if lo < 0:
                return range(0)
            return range(lo * n // span, hi * n // span)

        def by_scalar(m):
            return m // NT * (NT // 2) + max(0, m % NT - NT // 2)

        def columns(j):
            pair, kind = j // 2, j % 2
            return slice(kind * WIDTH + pair * P, kind * WIDTH + (pair + 1) * P)

        def blocks(i):
            return slice(0, (i + 1) * P)

        @block.sync
        def _(sp):
            def load(j):
                if j >= 2:
                    sp.wait_ge(w_low, j - 1)
                sp.dma_start(w_raw[:, j % 2], w_in[:, columns(j)].rearrange("(k p) n -> p k n", p=P)
                             ).then_inc(w_loaded[j % 2], 16)

            load(0)
            for n, g in enumerate((q_gain, k_gain)):
                for head in range(2):
                    sp.dma_start(gains[head * DH:(head + 1) * DH, n:n + 1], g.rearrange("(p n) -> p n", n=1)
                                 ).then_inc(small, 16)
            load(1)
            for it in range(PAIRS + 1):
                if it >= 1:
                    for head in range(2):
                        p = it - 1
                        if p:
                            sp.wait_ge(biased, ITEMS * (p - 1) + NT * (head + 1))
                        rows = c_rows.rearrange("(t h) s -> h t s", h=FH)[2 * p + head]
                        sp.dma_start(decay[:, head].rearrange("p (t s) -> p t s", t=NT), rows.partition_broadcast(P)
                                     ).then_inc(d_loaded[head], 16)
                        if it < PAIRS and 2 * it + head + 2 < 2 * PAIRS:
                            load(2 * it + head + 2)
                else:
                    load(2)
                    load(3)

        @block.gpsimd
        def _(pool):
            step = Step(pool, pool_step)
            step(pool.memset(eps[:], RMS_EPS))
            step(pool.memset(halves[:], 0.0))
            step(pool.memset(halves[0:DH, 0:DH], 1.0))
            step(pool.memset(halves[DH:P, DH:P], 1.0))
            step(pool.memset(mask_b[:], 0.0))
            step(pool.affine_select(out=mask_b[:], in_=mask_b[:], compare_op=ALU.is_ge, fill=-BIG, base=0,
                                    pattern=[[-1, P]], channel_multiplier=1))
            step(pool.tensor_copy(ident_b[:], c["ident"][:]), ready)
            for j in range(2 * PAIRS):
                pool.wait_ge(w_high, j + 1)
                step(pool.tensor_tensor(w_lo[:, j % 2], w_raw[:, j % 2], w_hi[:, j % 2].bitcast(F32),
                                        ALU.subtract), w_low)

        @block.tensor
        def _(pe):
            def project(it, s):
                u, k = s // KT, s % KT
                n, j, half = 4 * it + u, 2 * it + u // 2, u % 2
                if k == 0:
                    pe.wait_ge(w_low, j + 1)
                    if n >= 2:
                        pe.wait_ge(unit_taken, n - 1)
                out, ts = unit[n % 2][:], slice(half * HALF, (half + 1) * HALF)
                pe.matmul(out, w_hi[:, j % 2, k, :], xh[:, k, ts], start=(k == 0), stop=False)
                pe.matmul(out, w_hi[:, j % 2, k, :], xl[:, k, ts], start=False, stop=False)
                mm = pe.matmul(out, w_lo[:, j % 2, k, :], xh[:, k, ts], start=False, stop=(k == KT - 1))
                if k == KT - 1:
                    mm.then_inc(unit_made, 1)

            def score(p, n):
                head, i = n // NT, n % NT
                m = ITEMS * p + n
                if n == 0:
                    pe.wait_ge(normed, p + 1)
                if m:
                    pe.wait_ge(biased, m)
                rows = slice(head * DH, (head + 1) * DH)
                q, k = qk[rows, p % 2, 0, i * P:(i + 1) * P], qk[rows, p % 2, 1]
                width = (i + 1) * P
                for at in range(0, width, HALF):
                    end = min(width, at + HALF)
                    pe.matmul(scores[:, at:end], q, k[:, at:end], start=True, stop=(end < width))
                pe.matmul(scores[:, width - P:width], ident_b[:], mask_b[:], start=False, stop=True
                          ).then_inc(scored, 1)

            def turn(p, n):
                i, m = n % NT, ITEMS * p + n
                pe.wait_ge(exped, m + 1)
                if m:
                    pe.wait_ge(flip_d, m)
                if by_scalar(m):
                    pe.wait_ge(flip_a, by_scalar(m))
                for b in range(i + 1):
                    mm = pe.transpose(turned[:, b * P:(b + 1) * P], probs[:, m % 3, b * P:(b + 1) * P], c["ident"][:])
                mm.then_inc(flipped, 1)

            def weigh(p, n):
                head, i, m = n // NT, n % NT, ITEMS * p + n
                pe.wait_ge(flip_d, m + 1)
                if by_scalar(m + 1):
                    pe.wait_ge(flip_a, by_scalar(m + 1))
                if m:
                    pe.wait_ge(result_used, m)
                col = (2 * p + head) * DH
                for b in range(i + 1):
                    mm = pe.matmul(result[:, 0:DH], probs_t[:, m % 2, b * P:(b + 1) * P], values[:, b, col:col + DH],
                                   start=(b == 0), stop=(b == i))
                mm.then_inc(result_made, 1)

            pe.wait_ge(ready, 1)
            for it in range(PAIRS + 1):
                p = it - 1
                for s in range(F_STEPS):
                    if it < PAIRS:
                        project(it, s)
                    if p < 0:
                        continue
                    if s == AT_SUMS:
                        for kind in range(2):
                            pe.wait_ge(squared, 2 * p + kind + 1)
                            if kind == 0 and p:
                                pe.wait_ge(biased, ITEMS * p)
                            if kind == 1:
                                pe.wait_ge(rooted, 2 * p + 1)
                            for half in range(2):
                                ts = slice(half * HALF, (half + 1) * HALF)
                                mm = pe.matmul(scores[:, ts], halves[:], root[:, kind, ts], start=True, stop=True)
                            mm.then_inc(summed, 1)
                    for e in items_of(s):
                        if e < ITEMS:
                            score(p, e)
                        if 0 <= e - LAG_TURN < ITEMS:
                            turn(p, e - LAG_TURN)
                        if 0 <= e - LAG_OUT < ITEMS:
                            weigh(p, e - LAG_OUT)

        @block.scalar
        def _(act):
            step = Step(act, act_step)

            def high_part(j):
                act.wait_ge(w_loaded[j % 2], 16 * (j // 2 + 1))
                if j >= 2:
                    act.wait_ge(unit_made, 2 * j - 2)
                step(act.activation(w_hi[:, j % 2], w_raw[:, j % 2], ACT.Copy), w_high)

            def take_unit(it, u):
                n = 4 * it + u
                act.wait_ge(unit_made, n + 1)
                step(act.activation(qk[:, it % 2, u // 2, u % 2 * HALF:(u % 2 + 1) * HALF], unit[n % 2][:], ACT.Copy),
                     unit_taken)

            high_part(0)
            act.wait_ge(ready, 1)
            for it in range(PAIRS + 1):
                p = it - 1
                for s in range(F_STEPS):
                    if it < PAIRS and s % 16 == 4 and 2 * it + s // 16 + 1 < 2 * PAIRS:
                        high_part(2 * it + s // 16 + 1)
                    if it < PAIRS and s % 8 == 0 and s:
                        take_unit(it, s // 8 - 1)
                    if p < 0:
                        continue
                    if s == AT_SUMS:
                        nc.scalar.preload_act_table_set("natural_log_exp_and_others")
                        for kind in range(2):
                            act.wait_ge(summed, 2 * p + kind + 1)
                            step(act.activation(root[:, kind], scores[:], ACT.Ln, bias=eps[:, 0:1], scale=1.0 / DH),
                                 rooted)
                        for kind in range(2):
                            step(act.activation(root[:, kind], root[:, kind], ACT.Exp, scale=-0.5), roots)
                    for e in items_of(s):
                        if e < ITEMS:
                            m, i = ITEMS * p + e, e % NT
                            act.wait_ge(topped, m + 1)
                            row = probs[:, m % 3, blocks(i)]
                            step(act.activation(row, row, ACT.Exp, bias=top[:, m % 4:m % 4 + 1],
                                                accum_out=total[:, m % 4:m % 4 + 1]), exped)
                        n = e - LAG_TURN
                        if 0 <= n < ITEMS:
                            m, i = ITEMS * p + n, n % NT
                            act.wait_ge(flipped, m + 1)
                            if m >= 2:
                                act.wait_ge(result_made, m - 1)
                            if i >= NT // 2:
                                step(act.activation(probs_t[:, m % 2, 0:HALF], turned[:, 0:HALF], ACT.Copy), flip_a)
                if it < PAIRS:
                    take_unit(it, 3)
                    for kind in range(2):
                        step(act.activation(root[:, kind], qk[:, it % 2, kind], ACT.Square), squared)

        @block.vector
        def _(dve):
            step = Step(dve, dve_step)
            dve.wait_ge(small, 64)
            step(dve.tensor_scalar(gains[:, 0:1], gains[:, 0:1], DH ** -0.5, None, ALU.mult))
            for it in range(1, PAIRS + 1):
                p = it - 1
                for s in range(F_STEPS):
                    if s == AT_SUMS:
                        for kind in range(2):
                            dve.wait_ge(roots, 2 * p + kind + 1)
                            step(dve.scalar_tensor_tensor(qk[:, p % 2, kind], qk[:, p % 2, kind], gains[:, kind:kind + 1],
                                                          root[:, kind], ALU.mult, ALU.mult), normed if kind else None)
                    for e in items_of(s):
                        if e < ITEMS:
                            head, i, m = e // NT, e % NT, ITEMS * p + e
                            if i == 0:
                                dve.wait_ge(d_loaded[head], 16 * (p + 1))
                            dve.wait_ge(scored, m + 1)
                            if m >= 3:
                                dve.wait_ge(flipped, m - 2)
                            peak = top[:, m % 4:m % 4 + 1]
                            step(dve.tensor_tensor_reduce(probs[:, m % 3, blocks(i)], scores[:, blocks(i)],
                                                          decay[:, head, blocks(i)], 1.0, -3e38, ALU.add, ALU.max,
                                                          peak), biased)
                            step(dve.tensor_scalar(peak, peak, -1.0, None, ALU.mult), topped)
                        n = e - LAG_TURN
                        if 0 <= n < ITEMS:
                            m, i = ITEMS * p + n, n % NT
                            dve.wait_ge(flipped, m + 1)
                            if m >= 2:
                                dve.wait_ge(result_made, m - 1)
                            at = HALF if i >= NT // 2 else 0
                            there = slice(at, (i + 1) * P)
                            step(dve.tensor_copy(probs_t[:, m % 2, there], turned[:, there]), flip_d)
                        n = e - LAG_OUT
                        if 0 <= n < ITEMS:
                            head, i, m = n // NT, n % NT, ITEMS * p + n
                            sums, inverse = total[:, m % 4:m % 4 + 1], share[:, m % 4:m % 4 + 1]
                            dve.wait_ge(exped, m + 1)
                            step(dve.reciprocal(inverse, sums))
                            dve.wait_ge(result_made, m + 1)
                            col = (2 * p + head) * DH
                            z = gate_z[:, i, col:col + DH]
                            step(dve.scalar_tensor_tensor(z, result[:, 0:DH], inverse, z, ALU.mult, ALU.mult),
                                 result_used)


def build_program(nc, a, out):
    g_rows = nc.dram_tensor("g_rows_scratch", (NT * H, P), F32, kind="Internal").ap()
    c_rows = nc.dram_tensor("c_rows_scratch", (NT * FH, P), F32, kind="Internal").ap()
    x2 = nc.dram_tensor("x2_scratch", (T, D), F32, kind="Internal").ap()
    with ExitStack() as ctx:
        x2_stored = ctx.enter_context(nc.semaphore("x2_stored"))
        output_stored = ctx.enter_context(nc.semaphore("output_stored"))
        sb = lambda n, s, d=F32: ctx.enter_context(nc.sbuf_tensor(n, s, d))
        c = {n: sb(n, [P, P]) for n in ("ident", "tri", "ones")}
        part_hi, part_lo = sb("part_hi", [P, KT, T], F32R), sb("part_lo", [P, KT, T], F32R)
        x1 = sb("x1", [P, NT, D])
        with ExitStack() as gdn:
            sb1 = lambda n, s, d=F32: gdn.enter_context(nc.sbuf_tensor(n, s, d))
            o_t = sb1("o_t", [P, H, T])
            with ExitStack() as masks:
                sb2 = lambda n, s, d=F32: masks.enter_context(nc.sbuf_tensor(n, s, d))
                for n in ("odd_below", "above_big", "below_neg"):
                    c[n] = sb2(n, [P, P])
                c["level_mask"] = sb2("level_mask", [P, LEVELS, P // 2])
                gates = {n: sb2(f"gates_{n}", [P, NT, H]) for n in ("beta", "g", "neg_beta_eg", "k_decay", "last")}
                w_in = a["gdn_w_in"][0]
                small = {"ab": w_in[:, 4 * H * DK:4 * H * DK + 2 * H], "dt_bias": a["gdn_dt_bias"][0],
                         "a_log": a["gdn_a_log"][0]}
                transpose_input(nc, a["x"], c, part_hi, part_lo, small, gates, g_rows)
                delta_net(nc, c, part_hi, part_lo, gates, w_in, a["gdn_conv_w"][0], a["gdn_norm_g"][0], g_rows,
                          x1, o_t)
            mixer_out(nc, c, o_t, False, a["x"][0], a["gdn_w_out"][0], a["ln_g"][0], a["ln_b"][0],
                      part_hi, part_lo, x1, "m0")
        gated_embedding(nc, c, x1, a["p"][0, 0], a["ple_w_gate"][0], a["ple_w_proj"][0], x2, part_hi, part_lo,
                        x2_stored, "e0")
        with ExitStack() as fox:
            gate_z = fox.enter_context(nc.sbuf_tensor("gate_z", [P, NT, WIDTH], F32))
            w_in = a["fox_w_in"][0]
            fox_values(nc, c, part_hi, part_lo, w_in, a["fox_b_f"][0], c_rows, x1, gate_z)
            fox_attention(nc, c, part_hi, part_lo, w_in, a["fox_q_norm_g"][0], a["fox_k_norm_g"][0], c_rows, x1,
                          gate_z)
            mixer_out(nc, c, gate_z, True, x2, a["fox_w_out"][0], a["ln_g"][1], a["ln_b"][1],
                      part_hi, part_lo, x1, "m1")
        gated_embedding(nc, c, x1, a["p"][1, 0], a["ple_w_gate"][1], a["ple_w_proj"][1], out[0], None, None,
                        output_stored, "e1")


_INS = ["x", "p", "ln_g", "ln_b", "ple_w_gate", "ple_w_proj", "gdn_w_in", "gdn_conv_w", "gdn_a_log", "gdn_dt_bias",
        "gdn_norm_g", "gdn_w_out", "fox_w_in", "fox_b_f", "fox_q_norm_g", "fox_k_norm_g", "fox_w_out"]


def kernel(**inputs):
    import numpy as _np
    import concourse.bacc as _bacc
    from concourse import mybir as _mybir
    from concourse.bass_utils import run_bass_kernel_spmd as _run

    nc = _bacc.Bacc("TRN2", target_bir_lowering=False, num_devices=1)
    arrays, args = {}, {}
    for name in _INS:
        a = _np.ascontiguousarray(inputs[name])
        arrays[f"in_{name}_dram"] = a
        args[name] = nc.dram_tensor(f"in_{name}_dram", a.shape, _mybir.dt.from_np(a.dtype), kind="ExternalInput").ap()
    out = nc.dram_tensor("out_0_dram", (1, T, D), F32, kind="ExternalOutput").ap()
    build_program(nc, args, out)
    r = _run(nc, [arrays], core_ids=[0])
    return r.results[0]["out_0_dram"]
```

```python
import numpy as np
from contextlib import ExitStack

import concourse.bass as bass
from concourse import mybir

F32 = mybir.dt.float32
F32R = mybir.dt.float32r
ALU = mybir.AluOpType
ACT = mybir.ActivationFunctionType

P = 128
D = 1024
T = 1024
KT = D // P
NT = T // P
HALF = 512
H = 8
DK = 128
TAPS = 4
BIG = 1e30
RMS_EPS = 1e-6
LN_EPS = 1e-5
ALPHA = float((2 * 2) ** 0.25)
LEVELS = 6


class Phase(ExitStack):

    def __init__(self, nc, name):
        super().__init__()
        self.nc, self.name, self.semaphores = nc, name, []
        self.callback(self.clear)

    def sb(self, name, shape, dtype=F32):
        return self.enter_context(self.nc.sbuf_tensor(f"{self.name}_{name}", shape, dtype))

    def ps(self, name, shape):
        return self.enter_context(self.nc.psum_tensor(f"{self.name}_{name}", shape, F32))

    def sem(self, name):
        self.semaphores.append(self.nc.alloc_semaphore(f"{self.name}_{name}"))
        return self.semaphores[-1]

    def clear(self):
        self.nc.clear_and_free_semaphores(self.semaphores)
        self.nc.all_engine_barrier()


class Ahead:

    def __init__(self, semaphore, loads):
        self.semaphore, self.loads = semaphore, loads

    def start(self, sp):
        for to, source in self.loads:
            sp.dma_start(to, source).then_inc(self.semaphore, 16)

    def arrive(self, engine):
        engine.wait_ge(self.semaphore, 16 * len(self.loads))


class Step:

    def __init__(self, engine, own):
        self.engine, self.own, self.value = engine, own, {}

    def __call__(self, instruction, signal=None, ends=True):
        if not ends:
            return
        sem = self.own if signal is None else signal
        self.value[sem] = self.value.get(sem, 0) + 1
        instruction.then_inc(sem, 1)
        self.engine.wait_ge(sem, self.value[sem])


def constants_program(pool, step, c, ident_made):
    def select(ap, compare, fill, base, pattern, multiplier):
        step(pool.affine_select(out=ap, in_=ap, compare_op=compare, fill=fill, base=base,
                                pattern=pattern, channel_multiplier=multiplier))

    step(pool.memset(c["ident"][:], 0.0))
    step(pool.affine_select(out=c["ident"][:], in_=c["ident"][:], compare_op=ALU.not_equal, fill=1.0, base=0,
                            pattern=[[-1, P]], channel_multiplier=1), ident_made)
    step(pool.memset(c["tri"][:], 1.0))
    select(c["tri"][:], ALU.is_ge, 0.0, 0, [[1, P]], -1)
    step(pool.memset(c["ones"][:], 1.0))
    step(pool.memset(c["above_big"][:], 0.0))
    select(c["above_big"][:], ALU.is_ge, BIG, 0, [[-1, P]], 1)
    step(pool.memset(c["below_neg"][:], 0.0))
    select(c["below_neg"][:], ALU.is_ge, -BIG, 0, [[1, P]], -1)
    step(pool.memset(c["odd_below"][:], 0.0))
    view = c["odd_below"][:].rearrange("p (n two) -> p n two", two=2)[:, :, 0]
    step(pool.affine_select(out=view, in_=view, compare_op=ALU.not_equal, fill=-1.0, base=-1,
                            pattern=[[-2, P // 2]], channel_multiplier=1))
    for level in range(LEVELS):
        s = 2 << level
        nb = P // (2 * s)
        m = c["level_mask"][:, level, :]
        step(pool.memset(m, -1.0))
        select(m, ALU.is_ge, 0.0, 0, [[-2 * s, nb], [0, s]], 1)
        select(m, ALU.is_ge, 0.0, s - 1, [[2 * s, nb], [0, s]], -1)


def warm_up(pe, c, bank, rounds=9):
    for _ in range(rounds):
        pe.matmul(bank[:, 0:P], c["ident"][:], c["tri"][:], start=True, stop=True)


def right_halves(ap, level):
    return ap.rearrange("p (n two s) -> p n two s", two=2, s=2 << level)[:, :, 1, :]


def as_blocks(ap, level):
    return ap.rearrange("p (n s) -> p n s", s=2 << level)


def transpose_input(nc, x, c, xh, xl, after):
    with Phase(nc, "in") as ph:
        sb, ps, sem = ph.sb, ph.ps, ph.sem
        TILES, BANKS = 4, 4
        x_tile = sb("x_tile", [P, TILES, D])
        turned = [ps(f"turned{n}", [P, HALF]) for n in range(BANKS)]
        x_loaded = [sem(f"x_loaded{n}") for n in range(TILES)]
        pool_step, act_step, dve_step = sem("in_pool_step"), sem("in_act_step"), sem("in_dve_step")
        ident_made = sem("ident_made")
        x_turned, high_made, low_made = sem("x_turned"), sem("high_made"), sem("low_made")
        block = ph.enter_context(nc.Block())

        @block.sync
        def _(sp):
            for t in range(NT):
                if t >= TILES:
                    sp.wait_ge(x_turned, 2 * (t - TILES + 1))
                sp.dma_start(x_tile[:, t % TILES, :], x[0, t * P:(t + 1) * P, :]).then_inc(x_loaded[t % TILES], 16)
                if t == TILES - 1:
                    after.start(sp)

        @block.gpsimd
        def _(pool):
            constants_program(pool, Step(pool, pool_step), c, ident_made)

        @block.tensor
        def _(pe):
            pe.wait_ge(ident_made, 1)
            for n in range(2 * NT):
                t, half = n // 2, n % 2
                if half == 0:
                    pe.wait_ge(x_loaded[t % TILES], 16 * (t // TILES + 1))
                if n >= BANKS:
                    pe.wait_ge(low_made, n - BANKS + 1)
                for j in range(4):
                    k = 4 * half + j
                    mm = pe.transpose(turned[n % BANKS][:, j * P:(j + 1) * P],
                                      x_tile[:, t % TILES, k * P:(k + 1) * P], c["ident"][:])
                mm.then_inc(x_turned, 1)

        def piece(n):
            t, half = n // 2, n % 2
            where = (slice(None), slice(4 * half, 4 * half + 4), slice(t * P, (t + 1) * P))
            return where, turned[n % BANKS][:].rearrange("p (j t) -> p j t", j=4)

        @block.scalar
        def _(act):
            step = Step(act, act_step)
            for n in range(2 * NT):
                where, src = piece(n)
                act.wait_ge(x_turned, n + 1)
                step(act.activation(xh[where], src, ACT.Copy), high_made)

        @block.vector
        def _(dve):
            step = Step(dve, dve_step)
            for n in range(2 * NT):
                where, src = piece(n)
                dve.wait_ge(high_made, n + 1)
                step(dve.tensor_tensor(xl[where], src, xh[where].bitcast(F32), ALU.subtract), low_made)


def log_one_plus(dve, step, y, out, z2, series):
    step(dve.tensor_scalar(z2[:], y[:], 2.0, None, ALU.add))
    step(dve.reciprocal(out[:], z2[:]))
    step(dve.tensor_tensor(y[:], y[:], out[:], ALU.mult))
    step(dve.tensor_tensor(z2[:], y[:], y[:], ALU.mult))
    step(dve.tensor_scalar(series[:], z2[:], 2.0 / 17, None, ALU.mult))
    for odd in (15, 13, 11, 9, 7, 5, 3):
        step(dve.scalar_tensor_tensor(series[:], series[:], 2.0 / odd, z2[:], ALU.add, ALU.mult))
    step(dve.scalar_tensor_tensor(out[:], series[:], 2.0, y[:], ALU.add, ALU.mult))


def column_blocks(ring):
    return ring[:].rearrange("p b (k n) -> p b k n", k=KT)


def half_rows(ring):
    return ring[:].rearrange("p b (half n) -> p (b half) n", half=2)


STEPS = 8 * KT
AT_KK = 1
AT_QK = 2
AT_KEYS = 3
AT_FIRST = 8
AT_VALUES = 9
AT_LEVELS = 11
AT_CHUNKS = 29
AT_O_TAKE = 41
AT_SILU = 41
AT_K_SUMS = 45
AT_K_NORM = 49
AT_Q_SQUARES = 51
AT_O_SQUARES = 53
AT_DECAYS = 55
AT_O_SUMS = 59
AT_EXP = 60
AT_O_NORM = 62
AT_EG = 63
AT_GATES = 2
AT_GATES_TURNED = 6
AT_G_SUMS = 24
AT_G_ROWS = 28


def delta_net(nc, c, ring, ahead, after, xh, xl, gates, w_in, gate_bias, a_log_dram, conv_w, norm_g, g_rows_dram, qkvz_space, o_t):
    with Phase(nc, "gdn") as ph:
        sb, ps, sem = ph.sb, ph.ps, ph.sem
        w_raw = column_blocks(ring)
        w_hi = sb("w_hi", [P, 2, KT, P], F32R)
        w_lo = sb("w_lo", [P, 2, KT, P], F32R)
        raw = sb("raw", [P, 2, TAPS - 1 + T])
        qkvz = qkvz_space[:].rearrange("p (b n) t -> p b n t", b=2)
        g_rows = sb("g_bc", [P, T])
        lower = sb("lower", [P, T])
        inv = sb("inv", [P, T])
        inv_t = sb("inv_t", [P, T])
        att_t = sb("att_t", [P, T])
        y = sb("y", [P, 2, T // 4])
        k_rows = sb("k_rows", [P, T])
        v_rows = sb("v_rows", [P, T])
        eg = sb("eg", [P, T])
        squares = sb("squares", [P, T])
        rest = sb("rest", [P, P])
        v_new = sb("v_new", [P, P])
        state = sb("state", [P, 2, P])
        taps = sb("taps", [P, TAPS, 3 * H])
        gain = sb("gain", [P, 1])
        eps, o_eps = sb("gdn_eps", [P, 1]), sb("o_eps", [P, 1])
        by_head = lambda ap: ap.rearrange("p (c h) -> p c h", h=H)
        ab_rows = o_t[0:2 * H, 0]
        ab_raw = o_t[:, 1, 0:KT * 2 * H].rearrange("p (k h) -> p k h", k=KT)
        ab_hi, ab_lo = sb("ab_hi", [P, KT, 2 * H], F32R)[:], sb("ab_lo", [P, KT, 2 * H], F32R)[:]
        work = [by_head(o_t[:, 2, n * NT * H:(n + 1) * NT * H]) for n in range(6)]
        dt_bias, a_log = o_t[:, 3, 0:H], o_t[:, 3, H:2 * H]
        own_rows = o_t[0:NT * H, 4, 0:P]
        unit = [ps(f"unit{n}", [P, HALF]) for n in range(2)]
        w0, w1, w2 = ps("w0", [P, T]), ps("w1", [P, T]), ps("w2", [P, T])

        w_loaded = [sem(f"w_loaded{n}") for n in range(2)]
        g_loaded = sem("g_loaded")
        small = sem("taps_loaded")
        pool_step, act_step, dve_step = sem("gdn_pool_step"), sem("gdn_act_step"), sem("gdn_dve_step")
        w_high, w_low = sem("w_high"), sem("w_low")
        unit_made, unit_taken, conv_made = sem("unit_made"), sem("unit_taken"), sem("conv_made")
        z_ready, v_ready, squared = sem("z_ready"), sem("v_ready"), sem("squared")
        v_turned, bv_made = sem("v_turned"), sem("bv_made")
        o_added = sem("o_added")
        o_squared, o_summed, o_rms, o_done = sem("o_squared"), sem("o_summed"), sem("o_rms"), sem("o_done")
        summed, norms, normed = sem("summed"), sem("norms"), sem("normed")
        exponents, decays, eg_made = sem("exponents"), sem("decays"), sem("eg_made")
        k_turned, kd_made = sem("k_turned"), sem("kd_made")
        kk_made, qk_made, att_made = sem("kk_made"), sem("qk_made"), sem("att_made")
        q_decayed, inv2_made, inv2_turned, inv2_copied = sem("q_decayed"), sem("inv2_made"), sem("inv2_turned"), sem("inv2_copied")
        y_product, y_made, x_product, x_made = sem("y_product"), sem("y_made"), sem("x_product"), sem("x_made")
        t_turned, t_copied = sem("t_turned"), sem("t_copied")
        ks_made, rest_made, tr_made, vn_made = sem("ks_made"), sem("rest_made"), sem("tr_made"), sem("vn_made")
        ds_made, s_made, o_made, o_taken = sem("ds_made"), sem("s_made"), sem("o_made"), sem("o_taken")
        gate_loaded, gate_high, gate_low = sem("gate_loaded"), sem("gate_high"), sem("gate_low")
        ab_product, ab_copied, ab_turned = sem("ab_product"), sem("ab_copied"), sem("ab_turned")
        exp_beta, exp_alpha, abs_made, g_made = sem("exp_beta"), sem("exp_alpha"), sem("abs_made"), sem("g_made")
        g_summed, g_copied, g_turned, g_exps = sem("g_summed"), sem("g_copied"), sem("g_turned"), sem("g_exps")
        rows_made, g_out = sem("rows_made"), sem("g_out")
        block = ph.enter_context(nc.Block())

        def q_squares(h):
            return o_t[:, h + 1] if h + 1 < H else squares[:]

        def columns(j):
            head, kind = j // 4, j % 4
            return slice(kind * H * DK + head * DK, kind * H * DK + (head + 1) * DK)

        def chunk(n):
            return slice(n * P, (n + 1) * P)

        @block.sync
        def _(sp):
            def load(j):
                if j >= 2:
                    sp.wait_ge(w_low, j - 1)
                sp.dma_start(w_raw[:, j % 2], w_in[:, columns(j)].rearrange("(k p) n -> p k n", p=P)
                             ).then_inc(w_loaded[j % 2], 16)

            sp.dma_start(ab_raw, w_in[:, 4 * H * DK:4 * H * DK + 2 * H].rearrange("(k p) n -> p k n", p=P)
                         ).then_inc(gate_loaded, 16)
            sp.dma_start(dt_bias, gate_bias.partition_broadcast(P)).then_inc(gate_loaded, 16)
            sp.dma_start(a_log, a_log_dram.partition_broadcast(P)).then_inc(gate_loaded, 16)
            with nc.allow_non_contiguous_dma(reason="the taps of a channel on its partition"):
                for tap in range(TAPS):
                    sp.dma_start(taps[:, tap], conv_w[tap].rearrange("(b p) -> p b", p=P)).then_inc(small, 16)
                sp.dma_start(gain[:], norm_g.rearrange("(p n) -> p n", n=1)).then_inc(small, 16)
            for it in range(H + 1):
                def load_decays():
                    rows = g_rows_dram.rearrange("(c h) t -> h c t", h=H)[it]
                    sp.dma_start(g_rows[:].rearrange("p (c t) -> p c t", c=NT),
                                 rows.partition_broadcast(P)).then_inc(g_loaded, 16)

                if 1 <= it < H:
                    sp.wait_ge(eg_made, it)
                    load_decays()
                for b in range(4):
                    j = 4 * it + b + 2
                    if it < H and j < 4 * H:
                        load(j)
                if it == 0:
                    sp.wait_ge(rows_made, 1)
                    sp.dma_start(g_rows_dram, own_rows).then_inc(g_out, 16)
                    sp.wait_ge(g_out, 16)
                    load_decays()
            sp.wait_ge(w_low, 4 * H)
            after.start(sp)

        @block.gpsimd
        def _(pool):
            step = Step(pool, pool_step)

            def low_part(j):
                pool.wait_ge(w_low, 1)
                pool.wait_ge(w_high, j + 1)
                step(pool.tensor_tensor(w_lo[:, j % 2], w_raw[:, j % 2], w_hi[:, j % 2].bitcast(F32),
                                        ALU.subtract), w_low)

            for it in range(H + 1):
                p = it - 1
                for s in range(STEPS):
                    if it < H and s % 16 == 4 and 4 * it + s // 16 + 1 < 4 * H:
                        low_part(4 * it + s // 16 + 1)
                    if it < H and s == AT_K_NORM:
                        k = qkvz[:, it % 2, 1]
                        pool.wait_ge(norms, it + 1)
                        step(pool.tensor_tensor(k, k, squares[:], ALU.mult), normed)
                    if 0 <= p < H and s == AT_O_SQUARES:
                        pool.wait_ge(o_squared, p + 1)
                        step(pool.tensor_tensor(eg[:], eg[:], q_squares(p), ALU.add), o_added)
                    if 0 <= p < H and s == AT_QK:
                        pool.wait_ge(qk_made, p + 1)
                        pool.wait_ge(eg_made, p + 1)
                        q = qkvz[:, p % 2, 0]
                        step(pool.tensor_tensor(q, q, eg[:], ALU.mult), q_decayed)

        @block.tensor
        def _(pe):
            def project(it, s):
                u, k = s // KT, s % KT
                n, j, half = 8 * it + u, 4 * it + u // 2, u % 2
                if k == 0:
                    pe.wait_ge(w_low, j + 1)
                    if n >= 2:
                        pe.wait_ge(unit_taken, n - 1)
                out, ts = unit[n % 2][:], slice(half * HALF, (half + 1) * HALF)
                pe.matmul(out, w_hi[:, j % 2, k, :], xh[:, k, ts], start=(k == 0), stop=False)
                pe.matmul(out, w_hi[:, j % 2, k, :], xl[:, k, ts], start=False, stop=False)
                mm = pe.matmul(out, w_lo[:, j % 2, k, :], xh[:, k, ts], start=False, stop=(k == KT - 1))
                if k == KT - 1:
                    mm.then_inc(unit_made, 1)

            def gate_work(s):
                if s == AT_GATES:
                    pe.wait_ge(gate_low, 1)
                    for half in range(2):
                        out, ts = w2[0:2 * H, half * HALF:(half + 1) * HALF], slice(half * HALF, (half + 1) * HALF)
                        for k in range(KT):
                            pe.matmul(out, ab_hi[:, k], xh[:, k, ts], start=(k == 0), stop=False)
                            pe.matmul(out, ab_hi[:, k], xl[:, k, ts], start=False, stop=False)
                            mm = pe.matmul(out, ab_lo[:, k], xh[:, k, ts], start=False, stop=(k == KT - 1))
                    mm.then_inc(ab_product, 1)
                if s == AT_GATES_TURNED:
                    pe.wait_ge(ab_copied, 1)
                    for n in range(NT):
                        mm = pe.transpose(w0[:, n * 2 * H:(n + 1) * 2 * H], ab_rows[:, chunk(n)],
                                          c["ident"][0:2 * H, 0:2 * H])
                    mm.then_inc(ab_turned, 1)
                if s == AT_G_SUMS:
                    pe.wait_ge(g_made, 1)
                    g = work[5].rearrange("p c h -> p (c h)")
                    pe.matmul(w1[:, 0:NT * H], c["tri"][:], g, start=True, stop=True)
                    pe.matmul(w1[:, HALF:HALF + NT * H], c["ones"][:], g, start=True, stop=True).then_inc(g_summed, 1)
                if s == AT_G_ROWS:
                    pe.wait_ge(g_copied, 1)
                    pe.transpose(w2[0:NT * H, 0:P], gates["g"][:].rearrange("p c h -> p (c h)"),
                                 c["ident"][:]).then_inc(g_turned, 1)

            def keep_warm(s):
                if s == AT_FIRST - 1:
                    pe.wait_ge(unit_taken, 8 * H)
                    rounds = 20
                else:
                    rounds = int(s >= AT_CHUNKS)
                for n in range(rounds):
                    pe.matmul(unit[n % 2][:], w_hi[:, 0, 0, :], xh[:, 0, 0:HALF], start=True, stop=True)

            def column_sums(outs, src, signal):
                for half, out in enumerate(outs):
                    ts = slice(half * HALF, (half + 1) * HALF)
                    mm = pe.matmul(out, c["ones"][:], src[:, ts], start=True, stop=True)
                mm.then_inc(signal, 1)

            def turn(out, src, signal, chunks):
                for n in chunks:
                    mm = pe.transpose(out[:, chunk(n)], src[:, chunk(n)], c["ident"][:])
                mm.then_inc(signal, 1)

            def head_work(p, s):
                q, k, v = (qkvz[:, p % 2, n] for n in range(3))
                if s == AT_KK:
                    pe.wait_ge(normed, p + 1)
                    if p:
                        pe.wait_ge(s_made, 9 * p)
                    for n in range(NT):
                        mm = pe.matmul(w2[:, chunk(n)], k[:, chunk(n)], k[:, chunk(n)], start=True, stop=True)
                    mm.then_inc(kk_made, 1)
                if s == AT_QK:
                    for n in range(NT):
                        mm = pe.matmul(w1[:, chunk(n)], k[:, chunk(n)], q[:, chunk(n)], start=True, stop=True)
                    mm.then_inc(qk_made, 1)
                if s == AT_FIRST:
                    for g in range(2):
                        pe.wait_ge(inv2_made, 2 * p + g + 1)
                        turn(w2, inv, inv2_turned, range(4 * g, 4 * g + 4))
                if s == AT_KEYS:
                    if p:
                        pe.wait_ge(o_rms, p)
                    turn(w0, k, k_turned, range(NT))
                if s == AT_VALUES:
                    pe.wait_ge(v_ready, p + 1)
                    pe.wait_ge(att_made, p + 1)
                    turn(w1, v, v_turned, range(NT))
                if s == AT_O_SUMS:
                    if p + 1 < H:
                        pe.wait_ge(norms, p + 2)
                    pe.wait_ge(o_added, p + 1)
                    column_sums((w0[:, 0:HALF], w0[:, HALF:T]), eg, o_summed)
                level, what = (s - AT_LEVELS) // 3, (s - AT_LEVELS) % 3
                if 0 <= level < LEVELS:
                    for g in range(2):
                        if what == 0:
                            if level == 0:
                                pe.wait_ge(inv2_copied, 2 * p + g + 1)
                            else:
                                pe.wait_ge(x_made, 12 * p + 2 * level - 1 + g)
                            for n in range(4):
                                mm = pe.matmul(as_blocks(w2[:, g * HALF + 64 * n:g * HALF + 64 * n + 64], level),
                                               lower[:, chunk(4 * g + n)],
                                               right_halves(inv_t[:, chunk(4 * g + n)], level), start=True, stop=True)
                            mm.then_inc(y_product, 1)
                        if what == 1:
                            pe.wait_ge(y_made, 12 * p + 2 * level + g + 1)
                            if level == 0:
                                pe.wait_ge(bv_made, p + 1)
                            else:
                                pe.wait_ge(t_copied, 10 * p + 2 * level - 1 + g)
                            for n in range(4):
                                mm = pe.matmul(w1[:, g * HALF + 64 * n:g * HALF + 64 * n + 64],
                                               inv[:, chunk(4 * g + n)], y[:, g, 64 * n:64 * n + 64],
                                               start=True, stop=True)
                            mm.then_inc(x_product, 1)
                        if what == 2 and level < LEVELS - 1:
                            pe.wait_ge(x_made, 12 * p + 2 * level + g + 1)
                            if level == 0:
                                pe.wait_ge(kd_made, p + 1)
                            turn(w0, inv_t, t_turned, range(4 * g, 4 * g + 4))
                n, what = (s - AT_CHUNKS) // 3, (s - AT_CHUNKS) % 3
                if 0 <= n < NT and s >= AT_CHUNKS:
                    if what == 0:
                        pe.wait_ge(s_made, 9 * p + n + 1)
                        pe.wait_ge(q_decayed, p + 1)
                        pe.matmul(w2[:, 0:P], k[:, chunk(n)], state[:, n % 2], start=True, stop=True).then_inc(ks_made, 1)
                        pe.matmul(w0[:, chunk(n)], state[:, n % 2], q[:, chunk(n)], start=True, stop=False)
                    if what == 1:
                        pe.wait_ge(x_made, 12 * p + 12)
                        pe.wait_ge(rest_made, NT * p + n + 1)
                        pe.matmul(w2[:, HALF:HALF + P], inv_t[:, chunk(n)], rest[:], start=True, stop=True
                                  ).then_inc(tr_made, 1)
                    if what == 2:
                        pe.wait_ge(vn_made, NT * p + n + 1)
                        pe.matmul(w1[:, 0:P], k_rows[:, chunk(n)], v_new[:], start=True, stop=True).then_inc(ds_made, 1)
                        pe.matmul(w0[:, chunk(n)], v_new[:], att_t[:, chunk(n)], start=False, stop=True
                                  ).then_inc(o_made, 1)

            warm_up(pe, c, w0)
            for it in range(H + 1):
                for s in range(STEPS):
                    if it == 0:
                        gate_work(s)
                    if it < H:
                        project(it, s)
                    else:
                        keep_warm(s)
                    if it >= 1:
                        head_work(it - 1, s)
                    if it < H and s == AT_K_SUMS:
                        pe.wait_ge(squared, it + 1)
                        if it:
                            pe.wait_ge(o_taken, 2 * it - 1)
                        column_sums((w1[:, HALF:T], w0[:, 0:HALF]), squares, summed)

        @block.scalar
        def _(act):
            step = Step(act, act_step)

            def high_part(j):
                if j < 2:
                    ahead.arrive(act)
                else:
                    act.wait_ge(w_loaded[j % 2], 16 * (j // 2))
                if j >= 2:
                    act.wait_ge(unit_made, 2 * j - 2)
                step(act.activation(w_hi[:, j % 2], w_raw[:, j % 2], ACT.Copy), w_high)

            def take_unit(it, u):
                n, block_n, half = 8 * it + u, 3 * it + u // 2, u % 2
                act.wait_ge(unit_made, n + 1)
                if u >= 6:
                    if it >= 2:
                        act.wait_ge(o_done, it - 1)
                    step(act.activation(qkvz[:, it % 2, 3, half * HALF:(half + 1) * HALF], unit[n % 2][:], ACT.Copy),
                         unit_taken)
                    return
                if block_n >= 2:
                    act.wait_ge(conv_made, 2 * block_n - 2)
                at = TAPS - 1 + half * HALF
                step(act.activation(raw[:, block_n % 2, at:at + HALF], unit[n % 2][:], ACT.Copy), unit_taken)

            def gate_work(s):
                if s == AT_GATES:
                    act.wait_ge(ab_product, 1)
                    step(act.activation(ab_rows, w2[0:2 * H], ACT.Copy), ab_copied)
                if s == AT_GATES_TURNED:
                    nc.scalar.preload_act_table_set("natural_log_exp_and_others")
                    act.wait_ge(ab_turned, 1)
                    turned = w0[:, 0:2 * NT * H].rearrange("p (c h) -> p c h", h=2 * H)
                    step(act.activation(work[0], turned[:, :, 0:H], ACT.Exp, scale=-1.0), exp_beta)
                    act.wait_ge(abs_made, 1)
                    step(act.activation(work[2], work[1], ACT.Exp))
                    step(act.activation(a_log, a_log, ACT.Exp), exp_alpha)
                if s == AT_G_SUMS:
                    act.wait_ge(g_copied, 2)
                    step(act.activation(gates["neg_beta_eg"][:], gates["g"][:], ACT.Exp))
                    step(act.activation(gates["k_decay"][:], work[0], ACT.Exp))
                    step(act.activation(gates["last"][:], by_head(w1[:, HALF:HALF + NT * H]), ACT.Exp), g_exps)
                if s == AT_G_ROWS:
                    act.wait_ge(g_turned, 1)
                    step(act.activation(own_rows, w2[0:NT * H, 0:P], ACT.Copy), rows_made)

            def root(out, sums, signal, scale, bias):
                nc.scalar.preload_act_table_set("natural_log_exp_and_others")
                for half, part in enumerate(sums):
                    step(act.activation(out[:, half * HALF:(half + 1) * HALF], part, ACT.Ln, bias=bias,
                                        scale=scale))
                step(act.activation(out[:], out[:], ACT.Exp, scale=-0.5), signal)

            def own_work(h, s):
                q, k = qkvz[:, h % 2, 0], qkvz[:, h % 2, 1]
                if s == AT_SILU:
                    act.wait_ge(conv_made, 6 * h + 4)
                    step(act.activation(q, q, ACT.Silu))
                    step(act.activation(k, k, ACT.Silu))
                    if h:
                        act.wait_ge(normed, h)
                    step(act.activation(squares[:], k, ACT.Square), squared)
                if s == AT_K_SUMS:
                    act.wait_ge(summed, h + 1)
                    root(squares, (w1[:, HALF:T], w0[:, 0:HALF]), norms, 1.0, eps[:, 0:1])
                if s == AT_Q_SQUARES:
                    if h == H - 1:
                        act.wait_ge(normed, H)
                    step(act.activation(q_squares(h), q, ACT.Square, scale=DK * RMS_EPS ** 0.5))
                if s == AT_EXP:
                    act.wait_ge(exponents, 2 * h + 1)
                    step(act.activation(lower[:], lower[:], ACT.Exp, scale=-1.0), decays)
                    act.wait_ge(exponents, 2 * h + 2)
                    step(act.activation(att_t[:], att_t[:], ACT.Exp), decays)
                if s == AT_EG:
                    if h:
                        act.wait_ge(o_done, h)
                    step(act.activation(eg[:], g_rows[:], ACT.Exp), eg_made)

            high_part(0)
            act.wait_ge(gate_loaded, 48)
            step(act.activation(ab_hi, ab_raw, ACT.Copy), gate_high)
            act.wait_ge(small, 16 * (TAPS + 1))
            for it in range(H + 1):
                p = it - 1
                for s in range(STEPS):
                    if it < H and s % 16 == 4 and 4 * it + s // 16 + 1 < 4 * H:
                        high_part(4 * it + s // 16 + 1)
                    if it < H and s % 8 == 0 and s:
                        take_unit(it, s // 8 - 1)
                    if it == 0:
                        gate_work(s)
                    if it < H:
                        own_work(it, s)
                    if p < 0:
                        continue
                    if s == AT_O_SUMS:
                        act.wait_ge(o_summed, p + 1)
                        root(eg, (w0[:, 0:HALF], w0[:, HALF:T]), o_rms, 1.0 / DK, o_eps[:, 0:1])
                    if s == AT_KEYS:
                        act.wait_ge(k_turned, p + 1)
                        for n in range(NT):
                            step(act.activation(k_rows[:, chunk(n)], w0[:, chunk(n)], ACT.Copy,
                                                scale=gates["k_decay"][:, n, p:p + 1]),
                                 kd_made, n == NT - 1)
                    if s == AT_FIRST:
                        for g in range(2):
                            act.wait_ge(inv2_turned, 2 * p + g + 1)
                            step(act.activation(inv_t[:, g * HALF:(g + 1) * HALF], w2[:, g * HALF:(g + 1) * HALF],
                                                ACT.Copy), inv2_copied)
                    if s == AT_VALUES:
                        act.wait_ge(v_turned, p + 1)
                        for n in range(NT):
                            step(act.activation(v_rows[:, chunk(n)], w1[:, chunk(n)], ACT.Copy,
                                                scale=gates["beta"][:, n, p:p + 1]),
                                 bv_made, n == NT - 1)
                    level, what = (s - AT_LEVELS) // 3, (s - AT_LEVELS) % 3
                    if 0 <= level < LEVELS - 1 and what == 2:
                        for g in range(2):
                            act.wait_ge(t_turned, 10 * p + 2 * level + g + 1)
                            step(act.activation(inv[:, g * HALF:(g + 1) * HALF], w0[:, g * HALF:(g + 1) * HALF],
                                                ACT.Copy), t_copied)
                    if s == AT_O_TAKE:
                        act.wait_ge(o_made, NT * p + NT // 2)
                        step(act.activation(o_t[:, p, 0:HALF], w0[:, 0:HALF], ACT.Copy), o_taken)
                    if s == AT_O_SQUARES:
                        act.wait_ge(o_made, NT * p + NT)
                        step(act.activation(o_t[:, p, HALF:T], w0[:, HALF:T], ACT.Copy), o_taken)
                        step(act.activation(eg[:], o_t[:, p], ACT.Square), o_squared)
                if it < H:
                    take_unit(it, 7)
                    v, z = qkvz[:, it % 2, 2], qkvz[:, it % 2, 3]
                    act.wait_ge(conv_made, 6 * it + 6)
                    step(act.activation(v, v, ACT.Silu), v_ready)
                    step(act.activation(z, z, ACT.Silu), z_ready)

        @block.vector
        def _(dve):
            step = Step(dve, dve_step)
            step(dve.memset(raw[:, :, 0:TAPS - 1], 0.0))
            step(dve.memset(eps[:], RMS_EPS))
            step(dve.memset(o_eps[:], RMS_EPS * RMS_EPS * DK))
            dve.wait_ge(w_high, 1)
            step(dve.tensor_tensor(w_lo[:, 0], w_raw[:, 0], w_hi[:, 0].bitcast(F32), ALU.subtract), w_low)
            dve.wait_ge(gate_high, 1)
            step(dve.tensor_tensor(ab_lo, ab_raw, ab_hi.bitcast(F32), ALU.subtract), gate_low)
            dve.wait_ge(small, 16 * (TAPS + 1))

            def gate_work(s):
                if s == AT_GATES_TURNED:
                    dve.wait_ge(exp_beta, 1)
                    step(dve.tensor_scalar(work[0], work[0], 1.0, None, ALU.add))
                    step(dve.reciprocal(gates["beta"][:], work[0]))
                    turned = w0[:, 0:2 * NT * H].rearrange("p (c h) -> p c h", h=2 * H)
                    step(dve.tensor_tensor(work[3], turned[:, :, H:2 * H],
                                           dt_bias.unsqueeze(1).to_broadcast([P, NT, H]), ALU.add))
                    step(dve.scalar_tensor_tensor(work[1], work[3], -1.0, work[3], ALU.mult, ALU.min), abs_made)
                    dve.wait_ge(exp_alpha, 1)
                    log_one_plus(dve, step, work[2], work[1], work[4], work[0])
                    step(dve.scalar_tensor_tensor(work[0], work[3], 0.0, work[1], ALU.max, ALU.add))
                    step(dve.scalar_tensor_tensor(work[5], work[0], -1.0,
                                                  a_log.unsqueeze(1).to_broadcast([P, NT, H]),
                                                  ALU.mult, ALU.mult), g_made)
                if s == AT_G_SUMS:
                    dve.wait_ge(g_summed, 1)
                    step(dve.tensor_copy(gates["g"][:], by_head(w1[:, 0:NT * H])), g_copied)
                    step(dve.tensor_tensor(work[0], by_head(w1[:, HALF:HALF + NT * H]), gates["g"][:], ALU.subtract),
                         g_copied)
                    dve.wait_ge(g_exps, 1)
                    step(dve.scalar_tensor_tensor(gates["neg_beta_eg"][:], gates["neg_beta_eg"][:], -1.0,
                                                  gates["beta"][:], ALU.mult, ALU.mult))

            def convolve(it, u, part):
                kind, half = u // 2, u % 2
                if part == 0:
                    dve.wait_ge(unit_taken, 8 * it + u + 1)
                src = raw[:, (3 * it + kind) % 2]
                out = qkvz[:, it % 2, kind, half * HALF:(half + 1) * HALF]
                tap = TAPS - 1 - part
                shifted = src[:, half * HALF + tap:half * HALF + tap + HALF]
                weight = taps[:, tap, kind * H + it:kind * H + it + 1]
                if part == 0:
                    step(dve.tensor_scalar(out, shifted, weight, None, ALU.mult))
                else:
                    step(dve.scalar_tensor_tensor(out, shifted, weight, out, ALU.mult, ALU.add),
                         conv_made if part == TAPS - 1 else None)

            def own_work(h, s):
                if s == AT_DECAYS:
                    dve.wait_ge(g_loaded, 16 * (h + 1))
                    for n in range(NT):
                        step(dve.scalar_tensor_tensor(lower[:, chunk(n)], g_rows[:, chunk(n)],
                                                      gates["g"][:, n, h:h + 1], c["above_big"][:],
                                                      ALU.subtract, ALU.max), exponents, n == NT - 1)
                    if h:
                        dve.wait_ge(o_made, NT * h)
                    for n in range(NT):
                        step(dve.scalar_tensor_tensor(att_t[:, chunk(n)], g_rows[:, chunk(n)],
                                                      gates["g"][:, n, h:h + 1], c["below_neg"][:],
                                                      ALU.subtract, ALU.min), exponents, n == NT - 1)

            def head_work(p, s):
                if s == AT_KK:
                    dve.wait_ge(kk_made, p + 1)
                    dve.wait_ge(decays, 2 * p + 1)
                    for g in range(2):
                        for n in range(4 * g, 4 * g + 4):
                            step(dve.scalar_tensor_tensor(lower[:, chunk(n)], w2[:, chunk(n)],
                                                          gates["beta"][:, n, p:p + 1], lower[:, chunk(n)],
                                                          ALU.mult, ALU.mult), None, n % 4 == 3)
                        four = slice(g * HALF, (g + 1) * HALF)
                        view = lambda ap: ap[:, four].rearrange("p (n t) -> p n t", n=4)
                        step(dve.tensor_tensor(view(inv), view(lower), c["odd_below"][:].unsqueeze(1).to_broadcast(
                            [P, 4, P]), ALU.mult))
                        step(dve.tensor_tensor(view(inv), view(inv), c["ident"][:].unsqueeze(1).to_broadcast(
                            [P, 4, P]), ALU.add), inv2_made)
                if s == AT_VALUES:
                    step(dve.memset(state[:, 0], 0.0), s_made)
                if s == AT_O_NORM:
                    dve.wait_ge(o_rms, p + 1)
                    dve.wait_ge(z_ready, p + 1)
                    step(dve.scalar_tensor_tensor(o_t[:, p], o_t[:, p], gain[:, 0:1], eg[:], ALU.mult, ALU.mult))
                    step(dve.tensor_tensor(o_t[:, p], o_t[:, p], qkvz[:, p % 2, 3], ALU.mult), o_done)
                if s == AT_QK:
                    dve.wait_ge(qk_made, p + 1)
                    dve.wait_ge(decays, 2 * p + 2)
                    step(dve.tensor_tensor(att_t[:, 0:HALF], w1[:, 0:HALF], att_t[:, 0:HALF], ALU.mult))
                    step(dve.tensor_tensor(att_t[:, HALF:T], w1[:, HALF:T], att_t[:, HALF:T], ALU.mult), att_made)
                level, what = (s - AT_LEVELS) // 3, (s - AT_LEVELS) % 3
                if 0 <= level < LEVELS:
                    for g in range(2):
                        four = slice(g * HALF, g * HALF + 256)
                        if what == 0:
                            dve.wait_ge(y_product, 12 * p + 2 * level + g + 1)
                            mask = c["level_mask"][:, level].unsqueeze(1).to_broadcast([P, 4, P // 2])
                            step(dve.tensor_tensor(y[:, g].rearrange("p (n t) -> p n t", n=4),
                                                   w2[:, four].rearrange("p (n t) -> p n t", n=4), mask, ALU.mult),
                                 y_made)
                        if what == 1:
                            dve.wait_ge(x_product, 12 * p + 2 * level + g + 1)
                            x = right_halves(inv_t[:, g * HALF:(g + 1) * HALF], level)
                            step(dve.tensor_tensor(x, x, as_blocks(w1[:, four], level), ALU.add), x_made)
                n, what = (s - AT_CHUNKS) // 3, (s - AT_CHUNKS) % 3
                if 0 <= n < NT and s >= AT_CHUNKS:
                    if what == 0:
                        dve.wait_ge(ks_made, NT * p + n + 1)
                        step(dve.scalar_tensor_tensor(rest[:], w2[:, 0:P], gates["neg_beta_eg"][:, n, p:p + 1],
                                                      v_rows[:, chunk(n)], ALU.mult, ALU.add), rest_made)
                    if what == 1:
                        dve.wait_ge(tr_made, NT * p + n + 1)
                        step(dve.tensor_copy(v_new[:], w2[:, HALF:HALF + P]), vn_made)
                    if what == 2:
                        dve.wait_ge(ds_made, NT * p + n + 1)
                        step(dve.scalar_tensor_tensor(state[:, (n + 1) % 2], state[:, n % 2],
                                                      gates["last"][:, n, p:p + 1], w1[:, 0:P], ALU.mult, ALU.add),
                             s_made)

            for it in range(H + 1):
                for s in range(STEPS):
                    if it == 0:
                        gate_work(s)
                    if it < H:
                        own_work(it, s)
                    if it >= 1:
                        head_work(it - 1, s)
                    u, part = s // 8 - 1, (s % 8 - 1) // 2
                    if it < H and 0 <= u < 6 and s % 2 == 1:
                        convolve(it, u, part)


def mixer_out(nc, c, ring, ahead, after, o, turned, residual, w_out, ln_g, ln_b, w_hi, w_lo, x1, name):
    with Phase(nc, name) as ph:
        sb, ps, sem = ph.sb, ph.ps, ph.sem
        RAW, w_raw = 4, half_rows(ring)
        OB = 3
        o_hi, o_lo = sb("o_hi", [P, OB, KT, P], F32R), sb("o_lo", [P, OB, KT, P], F32R)
        old = sb("old", [P, 2, D])
        mixed = sb("mixed", [P, 2, D])
        gain, shift = sb("gain", [P, D]), sb("shift", [P, D])
        stats, moments = sb("stats", [P, 2, 2, 6]), sb("moments", [P, 2, 2])
        rstd, eps = sb("rstd", [P, 2]), sb("eps", [P, 1])
        out = [ps(f"y{n}", [P, D]) for n in range(3)]
        flip = [ps(f"flip{n}", [P, HALF]) for n in range(2)]
        w_loaded = [sem(f"w_loaded{n}") for n in range(RAW)]
        x_loaded = [sem(f"x_loaded{n}") for n in range(2)]
        ln_loaded = sem("ln_loaded")
        act_step, dve_step, pool_step = sem("act_step"), sem("dve_step"), sem("pool_step")
        w_high, w_low, o_high, o_low = sem("w_high"), sem("w_low"), sem("o_high"), sem("o_low")
        flipped, y_made, mixed_made = sem("flipped"), sem("y_made"), sem("mixed_made")
        var_made, rstd_made, scaled, x_made = sem("var_made"), sem("rstd_made"), sem("scaled"), sem("x_made")
        eps_made, half_made = sem("eps_made"), sem("half_made")
        block = ph.enter_context(nc.Block())

        @block.sync
        def _(sp):
            def load_x(t):
                if t >= 2:
                    sp.wait_ge(mixed_made, t - 1)
                sp.dma_start(old[:, t % 2], residual[t * P:(t + 1) * P, :]).then_inc(x_loaded[t % 2], 16)

            for n in range(RAW, 2 * KT):
                k, cols = n // 2, slice(n % 2 * HALF, (n % 2 + 1) * HALF)
                sp.wait_ge(w_low, n - RAW + 1)
                sp.dma_start(w_raw[:, n % RAW], w_out[k * P:(k + 1) * P, cols]).then_inc(w_loaded[n % RAW], 16)
            load_x(0)
            load_x(1)
            sp.dma_start(gain[:], ln_g.partition_broadcast(P)).then_inc(ln_loaded, 16)
            sp.dma_start(shift[:], ln_b.partition_broadcast(P)).then_inc(ln_loaded, 16)
            sp.wait_ge(w_low, 2 * KT)
            after.start(sp)
            for t in range(2, NT):
                load_x(t)

        @block.tensor
        def _(pe):
            def flip_tile(t):
                for half in range(2):
                    n = 2 * t + half
                    if n >= 2:
                        pe.wait_ge(o_low, n - 1)
                    for j in range(4):
                        k = 4 * half + j
                        mm = pe.transpose(flip[half][:, j * P:(j + 1) * P], o[:, t, k * P:(k + 1) * P], c["ident"][:])
                    mm.then_inc(flipped, 1)

            def multiply(t, k, halves=(0, 1)):
                if k == 0 and t >= 3:
                    pe.wait_ge(mixed_made, t - 2)
                y = out[t % 3]
                for half in halves:
                    cols = slice(half * HALF, (half + 1) * HALF)
                    pe.matmul(y[:, cols], o_hi[:, t % OB, k, :], w_hi[:, k, cols], start=(k == 0), stop=False)
                    pe.matmul(y[:, cols], o_hi[:, t % OB, k, :], w_lo[:, k, cols], start=False, stop=False)
                    mm = pe.matmul(y[:, cols], o_lo[:, t % OB, k, :], w_hi[:, k, cols], start=False,
                                   stop=(k == KT - 1))
                if k == KT - 1:
                    mm.then_inc(y_made if half else half_made, 1)

            if turned:
                flip_tile(0)
                flip_tile(1)
            else:
                warm_up(pe, c, out[2])
            pe.wait_ge(o_low, 2)
            for k in range(KT):
                pe.wait_ge(w_low, 2 * k + 2)
                multiply(0, k)
                if k == 0:
                    pe.wait_ge(o_low, 4)
                multiply(1, k)
                if turned and k == KT // 2:
                    flip_tile(2)
            for t in range(2, NT):
                pe.wait_ge(o_low, 2 * t + 2)
                if t == NT - 1:
                    for half in range(2):
                        for k in range(KT):
                            multiply(t, k, (half,))
                    break
                for k in range(KT):
                    multiply(t, k)
                    if turned and k == KT // 2 and t + 1 < NT:
                        flip_tile(t + 1)

        def halves(t):
            for half in range(2):
                ks = slice(4 * half, 4 * half + 4)
                src = flip[half][:].rearrange("p (k t) -> p k t", k=4) if turned else o[:, ks, t * P:(t + 1) * P]
                yield 2 * t + half, ks, src

        @block.scalar
        def _(act):
            step = Step(act, act_step)

            def o_part(t):
                if t >= OB:
                    act.wait_ge(y_made, t - OB + 1)
                for n, ks, src in halves(t):
                    if turned:
                        act.wait_ge(flipped, n + 1)
                    step(act.activation(o_hi[:, t % OB, ks], src, ACT.Copy), o_high)

            for k in range(KT):
                if k < 2:
                    o_part(k)
                    ahead.arrive(act)
                for n in (2 * k, 2 * k + 1):
                    if n >= RAW:
                        act.wait_ge(w_loaded[n % RAW], 16 * (n // RAW))
                    cols = slice(n % 2 * HALF, (n % 2 + 1) * HALF)
                    step(act.activation(w_hi[:, k, cols], w_raw[:, n % RAW], ACT.Copy), w_high)
            o_part(2)
            act.wait_ge(eps_made, 1)
            nc.scalar.preload_act_table_set("natural_log_exp_and_others")
            for t in range(NT):
                if t and t + 2 < NT:
                    o_part(t + 2)
                act.wait_ge(var_made, t + 1)
                r = rstd[:, t % 2:t % 2 + 1]
                step(act.activation(r, moments[:, t % 2, 1:2], ACT.Ln, bias=eps[:, 0:1]))
                step(act.activation(r, r, ACT.Exp, scale=-0.5), rstd_made)

        @block.vector
        def _(dve):
            step = Step(dve, dve_step)
            step(dve.memset(eps[:], LN_EPS), eps_made)

            def o_part(t):
                for n, ks, src in halves(t):
                    dve.wait_ge(o_high, n + 1)
                    step(dve.tensor_tensor(o_lo[:, t % OB, ks], src, o_hi[:, t % OB, ks].bitcast(F32),
                                           ALU.subtract), o_low)

            for k in range(KT):
                if k < 2:
                    o_part(k)
                for n in (2 * k, 2 * k + 1):
                    cols = slice(n % 2 * HALF, (n % 2 + 1) * HALF)
                    dve.wait_ge(w_high, n + 1)
                    step(dve.tensor_tensor(w_lo[:, k, cols], w_raw[:, n % RAW], w_hi[:, k, cols].bitcast(F32),
                                           ALU.subtract), w_low)
            o_part(2)
            for t in range(NT):
                b = t % 2
                dve.wait_ge(x_loaded[b], 16 * (t // 2 + 1))
                if t >= 2:
                    dve.wait_ge(x_made, t - 1)
                for half in range(2):
                    cols = slice(half * HALF, (half + 1) * HALF)
                    if half == 0 and t == NT - 1:
                        dve.wait_ge(half_made, 1)
                    else:
                        dve.wait_ge(y_made, t + 1)
                    step(dve.scalar_tensor_tensor(mixed[:, b, cols], old[:, b, cols], ALPHA, out[t % 3][:, cols],
                                                  ALU.mult, ALU.add), mixed_made if half else None)
                    step(dve.bn_stats(stats[:, b, half], mixed[:, b, cols]))
                step(dve.bn_aggr(moments[:, b], stats[:, b]), var_made)
                if t and t + 2 < NT:
                    o_part(t + 2)
                dve.wait_ge(rstd_made, t + 1)
                step(dve.tensor_scalar(mixed[:, b], mixed[:, b], moments[:, b, 0:1], rstd[:, b:b + 1],
                                       ALU.subtract, ALU.mult))
                if t == 0:
                    dve.wait_ge(ln_loaded, 32)
                step(dve.tensor_tensor(mixed[:, b], mixed[:, b], gain[:], ALU.mult), scaled)
            step(dve.tensor_tensor(x1[:, NT - 1], mixed[:, b], shift[:], ALU.add))

        @block.gpsimd
        def _(pool):
            step = Step(pool, pool_step)
            pool.wait_ge(ln_loaded, 32)
            for t in range(NT - 1):
                pool.wait_ge(scaled, t + 1)
                step(pool.tensor_tensor(x1[:, t], mixed[:, t % 2], shift[:], ALU.add), x_made)


def gated_embedding(nc, c, ring, ahead, after, x1, p_emb, w_gate, w_proj, out_dram, xh, xl, stored, name):
    KP = p_emb.shape[1] // P
    with Phase(nc, name) as ph:
        sb, ps, sem = ph.sb, ph.ps, ph.sem
        RAW, KW = 4, KP + KT
        w_raw = half_rows(ring)
        w_hi, w_lo = sb("w_hi", [P, KW, D], F32R), sb("w_lo", [P, KW, D], F32R)
        p_hi, p_lo = sb("p_hi", [P, KP, P], F32R), sb("p_lo", [P, KP, P], F32R)
        a_hi, a_lo = sb("a_hi", [P, 2, KT, P], F32R), sb("a_lo", [P, 2, KT, P], F32R)
        p_tile = sb("p_tile", [P, 2, KP * P])
        tanh = sb("tanh", [P, HALF])
        flip = [ps(f"flip{n}", [P, HALF]) for n in range(2)]
        gate = [ps(f"gate{n}", [P, D]) for n in range(2)]
        proj = ps("proj", [P, D])
        w_loaded = [sem(f"w_loaded{n}") for n in range(RAW)]
        p_loaded = [sem(f"p_loaded{n}") for n in range(2)]
        act_step, dve_step = sem("act_step"), sem("dve_step")
        w_high, w_low = sem("w_high"), sem("w_low")
        flipped, high, low = sem("flipped"), sem("high"), sem("low")
        half_made = sem("half_made")
        proj_made, gate_made, tanh_made, proj_used, half_used = (
            sem("proj_made"), sem("gate_made"), sem("tanh_made"), sem("proj_used"), sem("half_used"))
        block = ph.enter_context(nc.Block())
        last = xh is None

        def two(kind, t):
            return [(kind, t, 0), (kind, t, 1)]

        pieces = two("x1", 0) + two("x1", 1) + [("p", 0, 0)] + [("p", 1, 0)] + two("x1", 2)
        for t in range(2, NT):
            pieces += (two("x2", t - 2) if not last else []) + [("p", t, 0)]
            pieces += two("x1", t + 1) if t + 1 < NT else []
        if not last:
            pieces += two("x2", NT - 2) + two("x2", NT - 1)
        order = {piece: n for n, piece in enumerate(pieces)}

        def source(piece):
            kind, t, half = piece
            if kind == "p":
                return [p_tile[:, t % 2, k * P:(k + 1) * P] for k in range(KP)]
            return [x1[:, t, (4 * half + j) * P:(4 * half + j + 1) * P] for j in range(4)]

        def targets(piece):
            kind, t, half = piece
            if kind == "p":
                return [p_hi[:], p_lo[:]]
            if kind == "x1":
                return [a[:, t % 2, 4 * half:4 * half + 4] for a in (a_hi, a_lo)]
            return [a[:, 4 * half:4 * half + 4, t * P:(t + 1) * P] for a in (xh, xl)]

        @block.sync
        def _(sp):
            def load_w(n):
                k, cols = n // 2, slice(n % 2 * HALF, (n % 2 + 1) * HALF)
                sp.wait_ge(w_low, n - RAW + 1)
                w, row = (w_proj, k * P) if k < KP else (w_gate, (k - KP) * P)
                sp.dma_start(w_raw[:, n % RAW], w[row:row + P, cols]).then_inc(w_loaded[n % RAW], 16)

            def load_p(t):
                sp.dma_start(p_tile[:, t % 2], p_emb[t * P:(t + 1) * P, :]).then_inc(p_loaded[t % 2], 16)

            load_p(0)
            load_p(1)
            for n in range(RAW, 2 * KW):
                load_w(n)
            if after:
                sp.wait_ge(w_low, 2 * KW)
                after.start(sp)
            for t in range(NT):
                if t + 2 < NT:
                    sp.wait_ge(low, order[("p", t, 0)] + 1)
                    load_p(t + 2)
                sp.wait_ge(half_used, 2 * t + 2)
                sp.dma_start(out_dram[t * P:(t + 1) * P, :], x1[:, t]).then_inc(stored, 16)
            sp.wait_ge(stored, 16 * NT)

        @block.tensor
        def _(pe):
            def flip_piece(piece):
                n = order[piece]
                if n >= 2:
                    pe.wait_ge(low, n - 1)
                if piece[0] == "x2":
                    pe.wait_ge(half_used, 2 * piece[1] + 2)
                if piece[0] == "p":
                    pe.wait_ge(p_loaded[piece[1] % 2], 16 * (piece[1] // 2 + 1))
                for j, src in enumerate(source(piece)):
                    mm = pe.transpose(flip[n % 2][:, j * P:(j + 1) * P], src, c["ident"][:])
                mm.then_inc(flipped, 1)

            def flip_both(kind, t):
                if kind == "x1" or not last:
                    flip_piece((kind, t, 0))
                    flip_piece((kind, t, 1))

            def multiply(out, hi, lo, k, first, end, halves=(0, 1)):
                for half in halves:
                    cols = slice(half * HALF, (half + 1) * HALF)
                    pe.matmul(out[:, cols], hi, w_hi[:, k, cols], start=first, stop=False)
                    pe.matmul(out[:, cols], hi, w_lo[:, k, cols], start=False, stop=False)
                    mm = pe.matmul(out[:, cols], lo, w_hi[:, k, cols], start=False, stop=end)
                return mm

            def project(t):
                pe.wait_ge(low, order[("p", t, 0)] + 1)
                if t >= 1:
                    pe.wait_ge(proj_used, 2 * t)
                for k in range(KP):
                    mm = multiply(proj, p_hi[:, k], p_lo[:, k], k, k == 0, k == KP - 1)
                mm.then_inc(proj_made, 1)

            def gates(t, k, halves=(0, 1)):
                if k == 0:
                    pe.wait_ge(low, order[("x1", t, 1)] + 1)
                    if t >= 2:
                        pe.wait_ge(tanh_made, 2 * t - 2)
                mm = multiply(gate[t % 2], a_hi[:, t % 2, k], a_lo[:, t % 2, k], KP + k, k == 0, k == KT - 1, halves)
                if k == KT - 1:
                    mm.then_inc(gate_made if 1 in halves else half_made, 1)

            flip_both("x1", 0)
            flip_both("x1", 1)
            flip_piece(("p", 0, 0))
            pe.wait_ge(w_low, 2 * KP)
            project(0)
            flip_piece(("p", 1, 0))
            for k in range(KT):
                pe.wait_ge(w_low, 2 * (KP + k + 1))
                gates(0, k)
                if k < KT - 2:
                    gates(1, k)
            flip_both("x1", 2)
            gates(1, KT - 2)
            gates(1, KT - 1)
            for t in range(2, NT):
                ends = t == NT - 1
                for k in range(KT):
                    gates(t, k, (0,) if ends else (0, 1))
                    if k == 1:
                        flip_both("x2", t - 2)
                    if k == 2:
                        project(t - 1)
                    if k == 3:
                        flip_piece(("p", t, 0))
                    if k == 4 and not ends:
                        flip_both("x1", t + 1)
                    if k == 6 and ends:
                        project(t)
                if ends:
                    for k in range(KT):
                        gates(t, k, (1,))
            flip_both("x2", NT - 2)
            flip_both("x2", NT - 1)

        @block.scalar
        def _(act):
            step = Step(act, act_step)

            def high_part(piece):
                n = order[piece]
                if piece[0] == "x1" and piece[1] >= 2:
                    act.wait_ge(gate_made, piece[1] - 1)
                if piece[0] == "p" and piece[1] >= 1:
                    act.wait_ge(proj_made, piece[1])
                act.wait_ge(flipped, n + 1)
                width = len(source(piece))
                step(act.activation(targets(piece)[0], flip[n % 2][:, 0:width * P].rearrange("p (k t) -> p k t", t=P),
                                    ACT.Copy), high)

            def high_parts(kind, t):
                if kind == "x1" or not last:
                    high_part((kind, t, 0))
                    high_part((kind, t, 1))

            def sigmoid(t, half):
                if t == NT - 1 and half == 0:
                    act.wait_ge(half_made, 1)
                else:
                    act.wait_ge(gate_made, t + 1)
                if 2 * t + half:
                    act.wait_ge(half_used, 2 * t + half)
                step(act.activation(tanh[:], gate[t % 2][:, half * HALF:(half + 1) * HALF], ACT.Tanh, scale=0.5),
                     tanh_made)

            def high_weights(k):
                for n in (2 * k, 2 * k + 1):
                    if n < RAW:
                        ahead.arrive(act)
                    else:
                        act.wait_ge(w_loaded[n % RAW], 16 * (n // RAW))
                    cols = slice(n % 2 * HALF, (n % 2 + 1) * HALF)
                    step(act.activation(w_hi[:, k, cols], w_raw[:, n % RAW], ACT.Copy), w_high)

            high_weights(0)
            high_parts("x1", 0)
            high_weights(1)
            high_parts("x1", 1)
            high_part(("p", 0, 0))
            for k in range(2, KP):
                high_weights(k)
            high_weights(KP)
            high_part(("p", 1, 0))
            for k in range(KP + 1, KW):
                high_weights(k)
            sigmoid(0, 0)
            high_parts("x1", 2)
            sigmoid(0, 1)
            for t in range(2, NT):
                high_parts("x2", t - 2)
                sigmoid(t - 1, 0)
                high_part(("p", t, 0))
                if t + 1 < NT:
                    high_part(("x1", t + 1, 0))
                sigmoid(t - 1, 1)
                if t + 1 < NT:
                    high_part(("x1", t + 1, 1))
            sigmoid(NT - 1, 0)
            high_parts("x2", NT - 2)
            sigmoid(NT - 1, 1)
            high_parts("x2", NT - 1)

        @block.vector
        def _(dve):
            step = Step(dve, dve_step)

            def low_part(piece):
                n = order[piece]
                dve.wait_ge(high, n + 1)
                hi, lo = targets(piece)
                width = len(source(piece))
                step(dve.tensor_tensor(lo, flip[n % 2][:, 0:width * P].rearrange("p (k t) -> p k t", t=P),
                                       hi.bitcast(F32), ALU.subtract), low)

            def low_parts(kind, t):
                if kind == "x1" or not last:
                    low_part((kind, t, 0))
                    low_part((kind, t, 1))

            def add(t, half):
                dve.wait_ge(proj_made, t + 1)
                cols = slice(half * HALF, (half + 1) * HALF)
                dve.wait_ge(tanh_made, 2 * t + half + 1)
                step(dve.scalar_tensor_tensor(tanh[:], tanh[:], 1.0, proj[:, cols], ALU.add, ALU.mult), proj_used)
                step(dve.scalar_tensor_tensor(x1[:, t, cols], tanh[:], 0.5, x1[:, t, cols], ALU.mult, ALU.add),
                     half_used)

            def low_weights(k):
                for n in (2 * k, 2 * k + 1):
                    cols = slice(n % 2 * HALF, (n % 2 + 1) * HALF)
                    dve.wait_ge(w_high, n + 1)
                    step(dve.tensor_tensor(w_lo[:, k, cols], w_raw[:, n % RAW], w_hi[:, k, cols].bitcast(F32),
                                           ALU.subtract), w_low)

            low_weights(0)
            low_parts("x1", 0)
            low_weights(1)
            low_parts("x1", 1)
            low_part(("p", 0, 0))
            for k in range(2, KP + 1):
                low_weights(k)
            low_part(("p", 1, 0))
            for k in range(KP + 1, KW):
                low_weights(k)
            add(0, 0)
            low_parts("x1", 2)
            add(0, 1)
            for t in range(2, NT):
                low_parts("x2", t - 2)
                add(t - 1, 0)
                low_part(("p", t, 0))
                if t + 1 < NT:
                    low_part(("x1", t + 1, 0))
                add(t - 1, 1)
                if t + 1 < NT:
                    low_part(("x1", t + 1, 1))
            add(NT - 1, 0)
            low_parts("x2", NT - 2)
            add(NT - 1, 1)
            low_parts("x2", NT - 1)


BF16 = mybir.dt.bfloat16
FH = 16
DH = 64
PAIRS = FH // 2
WIDTH = FH * DH


def fox_values(nc, c, ring, ahead, after, xh, xl, w_in, b_f, c_rows, values, gate_z):
    with Phase(nc, "fv") as ph:
        sb, ps, sem = ph.sb, ph.ps, ph.sem
        RAW, PANELS = 4, 4
        w_raw = half_rows(ring)
        w_hi, w_lo = sb("w_hi", [P, 2, KT, HALF], F32R), sb("w_lo", [P, 2, KT, HALF], F32R)
        f_raw, f_hi, f_lo = (sb("f_raw", [P, KT, FH]), sb("f_hi", [P, KT, FH], F32R), sb("f_lo", [P, KT, FH], F32R))
        bias = sb("bias", [P, FH])
        work = [sb(f"work{n}", [P, NT, FH]) for n in range(5)]
        rows = sb("rows", [P, P])
        f_rows = gate_z[0:FH, NT - 1]
        bank = [ps(f"bank{n}", [P, HALF]) for n in range(8)]
        w_loaded = [sem(f"w_loaded{n}") for n in range(RAW)]
        small = sem("small")
        act_step, dve_step = sem("act_step"), sem("dve_step")
        w_high, w_low, f_high, f_low = sem("w_high"), sem("w_low"), sem("f_high"), sem("f_low")
        made, taken, f_made, f_log, c_summed, c_ready, c_turned = (
            sem("made"), sem("taken"), sem("f_made"), sem("f_log"), sem("c_summed"), sem("c_ready"), sem("c_turned"))
        f_product, f_copied = sem("f_product"), sem("f_copied")
        abs_made, exp_made, rows_made, stored = sem("abs_made"), sem("exp_made"), sem("rows_made"), sem("stored")
        block = ph.enter_context(nc.Block())
        F = NT * FH

        @block.sync
        def _(sp):
            sp.dma_start(f_raw[:], w_in[:, 4 * WIDTH:4 * WIDTH + FH].rearrange("(k p) n -> p k n", p=P)
                         ).then_inc(small, 16)
            sp.dma_start(bias[:], b_f.partition_broadcast(P)).then_inc(small, 16)
            for n in range(PANELS):
                for k in range(KT):
                    m = n * KT + k
                    if m < RAW:
                        continue
                    sp.wait_ge(w_low, m - RAW + 1)
                    sp.dma_start(w_raw[:, m % RAW], w_in[k * P:(k + 1) * P, 2 * WIDTH + n * HALF:2 * WIDTH + (n + 1) * HALF]
                                 ).then_inc(w_loaded[m % RAW], 16)
            sp.wait_ge(w_low, PANELS * KT)
            after.start(sp)
            sp.wait_ge(rows_made, 1)
            sp.dma_start(c_rows, rows[:]).then_inc(stored, 16)
            sp.wait_ge(stored, 16)

        @block.tensor
        def _(pe):
            def multiply(n, t, k):
                ts, b = slice(t * P, (t + 1) * P), n % 2
                if k == 0 and n >= 1:
                    pe.wait_ge(taken, (n - 1) * NT + t + 1)
                pe.matmul(bank[t][:], xh[:, k, ts], w_hi[:, b, k], start=(k == 0), stop=False)
                pe.matmul(bank[t][:], xh[:, k, ts], w_lo[:, b, k], start=False, stop=False)
                mm = pe.matmul(bank[t][:], xl[:, k, ts], w_hi[:, b, k], start=False, stop=(k == KT - 1))
                if k == KT - 1:
                    mm.then_inc(made, 1)

            warm_up(pe, c, bank[NT - 1])
            for k in range(KT):
                pe.wait_ge(w_low, k + 1)
                for t in range(NT):
                    multiply(0, t, k)
            small_bank = bank[NT - 1]
            for n in range(1, PANELS):
                pe.wait_ge(w_low, (n + 1) * KT)
                for t in range(NT):
                    if n == 1 and t == 1:
                        pe.wait_ge(taken, NT)
                        pe.wait_ge(f_low, 1)
                        for k in range(KT):
                            for half in range(2):
                                out, ts = bank[NT - 2 + half][0:FH], slice(half * HALF, (half + 1) * HALF)
                                pe.matmul(out, f_hi[:, k], xh[:, k, ts], start=(k == 0), stop=False)
                                pe.matmul(out, f_hi[:, k], xl[:, k, ts], start=False, stop=False)
                                mm = pe.matmul(out, f_lo[:, k], xh[:, k, ts], start=False, stop=(k == KT - 1))
                        mm.then_inc(f_product, 1)
                    if n == 1 and t == 2:
                        pe.wait_ge(f_copied, 2)
                        for i in range(NT):
                            mm = pe.transpose(small_bank[:, i * FH:(i + 1) * FH], f_rows[:, i * P:(i + 1) * P],
                                              c["ident"][0:FH, 0:FH])
                        mm.then_inc(f_made, 1)
                    if n == 1 and t == NT - 1:
                        pe.wait_ge(abs_made, 1)
                    if n == 2 and t == 1:
                        pe.wait_ge(f_log, 1)
                        pe.wait_ge(taken, 2 * NT)
                        log_f = work[3][:].rearrange("p t h -> p (t h)")
                        pe.matmul(small_bank[:, 0:F], c["tri"][:], log_f, start=True, stop=True)
                        mm = pe.matmul(small_bank[:, F:2 * F], c["ones"][:], log_f, start=True, stop=True)
                        mm.then_inc(c_summed, 1)
                    if n == 2 and t == 3:
                        pe.wait_ge(c_ready, 1)
                        pe.transpose(small_bank[:, 0:P], work[4][:].rearrange("p t h -> p (t h)"), c["ident"][:]
                                     ).then_inc(c_turned, 1)
                    if n == 2 and t == NT - 1:
                        pe.wait_ge(rows_made, 1)
                    for k in range(KT):
                        multiply(n, t, k)

        @block.scalar
        def _(act):
            step = Step(act, act_step)

            def high(m):
                n, k = m // KT, m % KT
                if m < RAW:
                    ahead.arrive(act)
                else:
                    act.wait_ge(w_loaded[m % RAW], 16 * (m // RAW))
                if n >= 2:
                    act.wait_ge(made, (n - 1) * NT)
                step(act.activation(w_hi[:, n % 2, k], w_raw[:, m % RAW], ACT.Copy), w_high)

            for m in range(2 * KT):
                high(m)
            act.wait_ge(small, 32)
            step(act.activation(f_hi[:], f_raw[:], ACT.Copy), f_high)
            for n in range(PANELS):
                for t in range(NT):
                    act.wait_ge(made, n * NT + t + 1)
                    half = n % 2
                    cols = slice(half * HALF, (half + 1) * HALF)
                    if n < 2:
                        step(act.activation(values[:, t, cols], bank[t][:], ACT.Copy), taken)
                    else:
                        step(act.activation(gate_z[:, t, cols], bank[t][:], ACT.Silu), taken)
                    if n == 2 and t == 4:
                        act.wait_ge(c_turned, 1)
                        step(act.activation(rows[:], bank[NT - 1][:, 0:P], ACT.Copy), rows_made)
                if n == 0:
                    act.wait_ge(f_product, 1)
                    for half in range(2):
                        step(act.activation(f_rows[:, half * HALF:(half + 1) * HALF], bank[NT - 2 + half][0:FH],
                                            ACT.Copy), f_copied)
                    act.wait_ge(abs_made, 1)
                    step(act.activation(work[1][:], work[1][:], ACT.Exp), exp_made)
                if n + 2 < PANELS:
                    for k in range(KT):
                        high((n + 2) * KT + k)

        @block.vector
        def _(dve):
            step = Step(dve, dve_step)

            def low(m):
                n, k = m // KT, m % KT
                dve.wait_ge(w_high, m + 1)
                step(dve.tensor_tensor(w_lo[:, n % 2, k], w_raw[:, m % RAW], w_hi[:, n % 2, k].bitcast(F32),
                                       ALU.subtract), w_low)

            for m in range(2 * KT):
                low(m)
            dve.wait_ge(f_high, 1)
            step(dve.tensor_tensor(f_lo[:], f_raw[:], f_hi[:].bitcast(F32), ALU.subtract), f_low)
            dve.wait_ge(f_made, 1)
            small_bank = bank[NT - 1][:, 0:F].rearrange("p (t h) -> p t h", h=FH)
            step(dve.tensor_tensor(work[0][:], small_bank, bias[:].unsqueeze(1).to_broadcast([P, NT, FH]), ALU.add))
            step(dve.scalar_tensor_tensor(work[1][:], work[0][:], -1.0, work[0][:], ALU.mult, ALU.min), abs_made)
            dve.wait_ge(exp_made, 1)
            log_one_plus(dve, step, work[1], work[2], work[4], work[3])
            step(dve.scalar_tensor_tensor(work[3][:], work[0][:], 0.0, work[2][:], ALU.min, ALU.subtract), f_log)
            for m in range(2 * KT, 3 * KT):
                low(m)
            dve.wait_ge(c_summed, 1)
            totals = bank[NT - 1][:, F:2 * F].rearrange("p (t h) -> p t h", h=FH)
            step(dve.tensor_copy(work[1][:], totals))
            for t in range(1, NT - 1):
                step(dve.tensor_tensor(work[1][:, t], work[1][:, t], work[1][:, t - 1], ALU.add))
            step(dve.tensor_scalar(work[4][:], small_bank, -1.0, None, ALU.mult))
            step(dve.tensor_tensor(work[4][:, 1:NT], work[4][:, 1:NT], work[1][:, 0:NT - 1], ALU.subtract), c_ready)
            for m in range(3 * KT, PANELS * KT):
                low(m)


F_STEPS = 32
AT_SUMS = 1
AT_QUERY_SQUARES = 20
AT_ITEMS = 7
ITEMS = 2 * NT
LAG_TURN, LAG_OUT = 2, 3


def fox_attention(nc, c, ring, ahead, after, xh, xl, w_in, q_gain, k_gain, c_rows, values, gate_z):
    with Phase(nc, "fa") as ph:
        sb, ps, sem = ph.sb, ph.ps, ph.sem
        w_raw = column_blocks(ring)
        w_hi, w_lo = sb("w_hi", [P, 2, KT, P], F32R), sb("w_lo", [P, 2, KT, P], F32R)
        qk = sb("qk", [P, 2, 2, T])
        root = sb("root", [P, 2, T])
        decay = sb("decay", [P, 2, T])
        probs = sb("probs", [P, 3, T])
        probs_t = sb("probs_t", [P, 2, T])
        halves = sb("halves", [P, P])
        ident_b, mask_b = sb("ident_b", [P, P], BF16), sb("mask_b", [P, P], BF16)
        gains = sb("gains", [P, 2])
        top, total, share = sb("top", [P, 4]), sb("total", [P, 4]), sb("share", [P, 4])
        eps = sb("eps", [P, 1])
        unit = [ps(f"unit{n}", [P, HALF]) for n in range(2)]
        scores, turned = ps("scores", [P, T]), ps("turned", [P, T])
        result, short_scores = ps("result", [P, HALF]), ps("short_scores", [P, HALF])
        w_loaded = [sem(f"w_loaded{n}") for n in range(2)]
        d_loaded = [sem(f"d_loaded{n}") for n in range(2)]
        small = sem("small")
        act_step, dve_step, pool_step = sem("act_step"), sem("dve_step"), sem("pool_step")
        ready = sem("constants")
        w_high, w_low, unit_made, unit_taken = sem("w_high"), sem("w_low"), sem("unit_made"), sem("unit_taken")
        squared, summed, normed = sem("squared"), sem("summed"), sem("normed")
        roots = sem("roots")
        scored, biased, topped, exped = sem("scored"), sem("biased"), sem("topped"), sem("exped")
        flipped, flip_a, flip_d, result_made, result_used = (
            sem("flipped"), sem("flip_a"), sem("flip_d"), sem("result_made"), sem("result_used"))
        block = ph.enter_context(nc.Block())

        def items_of(step):
            lo, hi = step - AT_ITEMS, step - AT_ITEMS + 1
            span, n = F_STEPS - AT_ITEMS, ITEMS + LAG_OUT
            if lo < 0:
                return range(0)
            return range(lo * n // span, hi * n // span)

        def place(n):
            return scores if item(n % ITEMS)[1] >= NT // 2 else short_scores

        def by_scalar(m):
            return m // ITEMS * NT + sum(item(n)[1] >= NT // 2 for n in range(m % ITEMS))

        def item(n):
            return n % 2, (n // 2, NT - 1 - n // 2)[n % 2]

        def columns(j):
            pair, kind = j // 2, j % 2
            return slice(kind * WIDTH + pair * P, kind * WIDTH + (pair + 1) * P)

        def blocks(i):
            return slice(0, (i + 1) * P)

        @block.sync
        def _(sp):
            def load(j):
                sp.wait_ge(w_low, j - 1)
                sp.dma_start(w_raw[:, j % 2], w_in[:, columns(j)].rearrange("(k p) n -> p k n", p=P)
                             ).then_inc(w_loaded[j % 2], 16)

            for n, g in enumerate((q_gain, k_gain)):
                for head in range(2):
                    sp.dma_start(gains[head * DH:(head + 1) * DH, n:n + 1], g.rearrange("(p n) -> p n", n=1)
                                 ).then_inc(small, 16)
            for it in range(PAIRS + 1):
                if it >= 1:
                    for head in range(2):
                        p = it - 1
                        if p:
                            sp.wait_ge(biased, ITEMS * p)
                        rows = c_rows.rearrange("(t h) s -> h t s", h=FH)[2 * p + head]
                        sp.dma_start(decay[:, head].rearrange("p (t s) -> p t s", t=NT), rows.partition_broadcast(P)
                                     ).then_inc(d_loaded[head], 16)
                        if it < PAIRS and 2 * it + head + 2 < 2 * PAIRS:
                            load(2 * it + head + 2)
                else:
                    load(2)
                    load(3)
            sp.wait_ge(w_low, 2 * PAIRS)
            after.start(sp)

        @block.gpsimd
        def _(pool):
            step = Step(pool, pool_step)
            step(pool.memset(eps[:], RMS_EPS))
            step(pool.memset(halves[:], 0.0))
            step(pool.memset(halves[0:DH, 0:DH], 1.0))
            step(pool.memset(halves[DH:P, DH:P], 1.0))
            step(pool.memset(mask_b[:], 0.0))
            step(pool.affine_select(out=mask_b[:], in_=mask_b[:], compare_op=ALU.is_ge, fill=-BIG, base=0,
                                    pattern=[[-1, P]], channel_multiplier=1))
            step(pool.tensor_copy(ident_b[:], c["ident"][:]), ready)
            pool.wait_ge(w_low, 1)
            for j in range(1, 2 * PAIRS):
                pool.wait_ge(w_high, j + 1)
                step(pool.tensor_tensor(w_lo[:, j % 2], w_raw[:, j % 2], w_hi[:, j % 2].bitcast(F32),
                                        ALU.subtract), w_low)

        @block.tensor
        def _(pe):
            def project(it, s):
                u, k = s // KT, s % KT
                n, j, half = 4 * it + u, 2 * it + u // 2, u % 2
                if k == 0:
                    pe.wait_ge(w_low, j + 1)
                    if n >= 2:
                        pe.wait_ge(unit_taken, n - 1)
                out, ts = unit[n % 2][:], slice(half * HALF, (half + 1) * HALF)
                pe.matmul(out, w_hi[:, j % 2, k, :], xh[:, k, ts], start=(k == 0), stop=False)
                pe.matmul(out, w_hi[:, j % 2, k, :], xl[:, k, ts], start=False, stop=False)
                mm = pe.matmul(out, w_lo[:, j % 2, k, :], xh[:, k, ts], start=False, stop=(k == KT - 1))
                if k == KT - 1:
                    mm.then_inc(unit_made, 1)

            def score(p, n):
                head, i = item(n)
                m = ITEMS * p + n
                if n == 0:
                    pe.wait_ge(normed, p + 1)
                if m >= 2:
                    pe.wait_ge(biased, m - int(place(n) is not place(n - 1)))
                rows = slice(head * DH, (head + 1) * DH)
                q, k = qk[rows, p % 2, 0, i * P:(i + 1) * P], qk[rows, p % 2, 1]
                width = (i + 1) * P
                for at in range(0, width, HALF):
                    end = min(width, at + HALF)
                    pe.matmul(place(n)[:, at:end], q, k[:, at:end], start=True, stop=(end < width))
                pe.matmul(place(n)[:, width - P:width], ident_b[:], mask_b[:], start=False, stop=True
                          ).then_inc(scored, 1)

            def turn(p, n):
                i, m = item(n)[1], ITEMS * p + n
                pe.wait_ge(exped, m + 1)
                if m:
                    pe.wait_ge(flip_d, m)
                if by_scalar(m):
                    pe.wait_ge(flip_a, by_scalar(m))
                for b in range(i + 1):
                    mm = pe.transpose(turned[:, b * P:(b + 1) * P], probs[:, m % 3, b * P:(b + 1) * P], c["ident"][:])
                mm.then_inc(flipped, 1)

            def weigh(p, n):
                (head, i), m = item(n), ITEMS * p + n
                pe.wait_ge(flip_d, m + 1)
                if by_scalar(m + 1):
                    pe.wait_ge(flip_a, by_scalar(m + 1))
                if m:
                    pe.wait_ge(result_used, m)
                col = (2 * p + head) * DH
                for b in range(i + 1):
                    mm = pe.matmul(result[:, 0:DH], probs_t[:, m % 2, b * P:(b + 1) * P], values[:, b, col:col + DH],
                                   start=(b == 0), stop=(b == i))
                mm.then_inc(result_made, 1)

            def keep_warm(rounds):
                for n in range(rounds):
                    pe.matmul(unit[n % 2][:], w_hi[:, 0, 0, :], xh[:, 0, 0:HALF], start=True, stop=True)

            warm_up(pe, c, scores)
            pe.wait_ge(ready, 1)
            for it in range(PAIRS + 1):
                p = it - 1
                for s in range(F_STEPS):
                    if it < PAIRS:
                        project(it, s)
                    if p < 0:
                        continue
                    if s == AT_SUMS:
                        for kind in range(2):
                            pe.wait_ge(squared, 2 * p + kind + 1)
                            if kind == 0 and p:
                                pe.wait_ge(biased, ITEMS * p)
                            if kind == 1 and p:
                                pe.wait_ge(flip_d, ITEMS * p)
                                pe.wait_ge(flip_a, by_scalar(ITEMS * p))
                            out = (scores, turned)[kind]
                            for half in range(2):
                                ts = slice(half * HALF, (half + 1) * HALF)
                                mm = pe.matmul(out[:, ts], halves[:], root[:, kind, ts], start=True, stop=True)
                            mm.then_inc(summed, 1)
                        if it == PAIRS:
                            pe.wait_ge(unit_taken, 4 * PAIRS)
                            keep_warm(24)
                    for e in items_of(s):
                        if e < ITEMS:
                            score(p, e)
                        if it == PAIRS:
                            keep_warm(1)
                        if 0 <= e - LAG_TURN < ITEMS:
                            turn(p, e - LAG_TURN)
                        if 0 <= e - LAG_OUT < ITEMS:
                            weigh(p, e - LAG_OUT)

        @block.scalar
        def _(act):
            step = Step(act, act_step)

            def high_part(j):
                if j < 2:
                    ahead.arrive(act)
                else:
                    act.wait_ge(w_loaded[j % 2], 16 * (j // 2))
                if j >= 2:
                    act.wait_ge(unit_made, 2 * j - 2)
                step(act.activation(w_hi[:, j % 2], w_raw[:, j % 2], ACT.Copy), w_high)

            def take_unit(it, u):
                n = 4 * it + u
                act.wait_ge(unit_made, n + 1)
                step(act.activation(qk[:, it % 2, u // 2, u % 2 * HALF:(u % 2 + 1) * HALF], unit[n % 2][:], ACT.Copy),
                     unit_taken)

            high_part(0)
            act.wait_ge(ready, 1)
            for it in range(PAIRS + 1):
                p = it - 1
                for s in range(F_STEPS):
                    if it < PAIRS and s % 16 == 4 and 2 * it + s // 16 + 1 < 2 * PAIRS:
                        high_part(2 * it + s // 16 + 1)
                    if it < PAIRS and s % 8 == 0 and s:
                        take_unit(it, s // 8 - 1)
                    if it < PAIRS and s == AT_QUERY_SQUARES:
                        if it:
                            act.wait_ge(normed, it)
                        step(act.activation(root[:, 0], qk[:, it % 2, 0], ACT.Square), squared)
                    if p < 0:
                        continue
                    if s == AT_SUMS:
                        nc.scalar.preload_act_table_set("natural_log_exp_and_others")
                        for kind in range(2):
                            act.wait_ge(summed, 2 * p + kind + 1)
                            step(act.activation(root[:, kind], (scores, turned)[kind][:], ACT.Ln, bias=eps[:, 0:1],
                                                scale=1.0 / DH))
                            step(act.activation(root[:, kind], root[:, kind], ACT.Exp, scale=-0.5), roots)
                    for e in items_of(s):
                        if e < ITEMS:
                            m, i = ITEMS * p + e, item(e)[1]
                            act.wait_ge(topped, m + 1)
                            row = probs[:, m % 3, blocks(i)]
                            step(act.activation(row, row, ACT.Exp, bias=top[:, m % 4:m % 4 + 1],
                                                accum_out=total[:, m % 4:m % 4 + 1]), exped)
                        n = e - LAG_TURN
                        if 0 <= n < ITEMS:
                            m, i = ITEMS * p + n, item(n)[1]
                            act.wait_ge(flipped, m + 1)
                            if m >= 2:
                                act.wait_ge(result_made, m - 1)
                            if i >= NT // 2:
                                step(act.activation(probs_t[:, m % 2, 0:HALF], turned[:, 0:HALF], ACT.Copy), flip_a)
                if it < PAIRS:
                    take_unit(it, 3)
                    step(act.activation(root[:, 1], qk[:, it % 2, 1], ACT.Square), squared)

        @block.vector
        def _(dve):
            step = Step(dve, dve_step)
            dve.wait_ge(w_high, 1)
            step(dve.tensor_tensor(w_lo[:, 0], w_raw[:, 0], w_hi[:, 0].bitcast(F32), ALU.subtract), w_low)
            dve.wait_ge(small, 64)
            step(dve.tensor_scalar(gains[:, 0:1], gains[:, 0:1], DH ** -0.5, None, ALU.mult))
            for it in range(1, PAIRS + 1):
                p = it - 1
                for s in range(F_STEPS):
                    if s == AT_SUMS:
                        for kind in range(2):
                            dve.wait_ge(roots, 2 * p + kind + 1)
                            step(dve.scalar_tensor_tensor(qk[:, p % 2, kind], qk[:, p % 2, kind], gains[:, kind:kind + 1],
                                                          root[:, kind], ALU.mult, ALU.mult), normed if kind else None)
                    for e in items_of(s):
                        if e < ITEMS:
                            (head, i), m = item(e), ITEMS * p + e
                            if e < 2:
                                dve.wait_ge(d_loaded[head], 16 * (p + 1))
                            dve.wait_ge(scored, m + 1)
                            if m >= 3:
                                dve.wait_ge(flipped, m - 2)
                            peak = top[:, m % 4:m % 4 + 1]
                            step(dve.tensor_tensor_reduce(probs[:, m % 3, blocks(i)], place(e)[:, blocks(i)],
                                                          decay[:, head, blocks(i)], 1.0, -3e38, ALU.add, ALU.max,
                                                          peak), biased)
                            step(dve.tensor_scalar(peak, peak, -1.0, None, ALU.mult), topped)
                        n = e - LAG_TURN
                        if 0 <= n < ITEMS:
                            m, i = ITEMS * p + n, item(n)[1]
                            dve.wait_ge(flipped, m + 1)
                            if m >= 2:
                                dve.wait_ge(result_made, m - 1)
                            at = HALF if i >= NT // 2 else 0
                            there = slice(at, (i + 1) * P)
                            step(dve.tensor_copy(probs_t[:, m % 2, there], turned[:, there]), flip_d)
                        n = e - LAG_OUT
                        if 0 <= n < ITEMS:
                            (head, i), m = item(n), ITEMS * p + n
                            sums, inverse = total[:, m % 4:m % 4 + 1], share[:, m % 4:m % 4 + 1]
                            dve.wait_ge(exped, m + 1)
                            step(dve.reciprocal(inverse, sums))
                            dve.wait_ge(result_made, m + 1)
                            col = (2 * p + head) * DH
                            z = gate_z[:, i, col:col + DH]
                            step(dve.scalar_tensor_tensor(z, result[:, 0:DH], inverse, z, ALU.mult, ALU.mult),
                                 result_used)


def build_program(nc, a, out):
    g_rows = nc.dram_tensor("g_rows_scratch", (NT * H, P), F32, kind="Internal").ap()
    c_rows = nc.dram_tensor("c_rows_scratch", (NT * FH, P), F32, kind="Internal").ap()
    x2 = nc.dram_tensor("x2_scratch", (T, D), F32, kind="Internal").ap()
    with ExitStack() as ctx:
        x2_stored = ctx.enter_context(nc.semaphore("x2_stored"))
        output_stored = ctx.enter_context(nc.semaphore("output_stored"))
        sb = lambda n, s, d=F32: ctx.enter_context(nc.sbuf_tensor(n, s, d))
        c = {n: sb(n, [P, P]) for n in ("ident", "tri", "ones")}
        part_hi, part_lo = sb("part_hi", [P, KT, T], F32R), sb("part_lo", [P, KT, T], F32R)
        x1 = sb("x1", [P, NT, D])
        ring = sb("ring", [P, 2, D])
        gdn_in, fox_in = a["gdn_w_in"][0], a["fox_w_in"][0]

        def ahead(name, loads):
            return Ahead(ctx.enter_context(nc.semaphore(f"{name}_ahead")), loads)

        def columns(w, starts):
            return [(column_blocks(ring)[:, n], w[:, at:at + P].rearrange("(k p) n -> p k n", p=P))
                    for n, at in enumerate(starts)]

        def rows(w):
            return [(ring[:, n], w[n * P:(n + 1) * P, :]) for n in range(2)]

        to_gdn = ahead("gdn", columns(gdn_in, (0, H * DK)))
        to_mix = [ahead(f"m{n}", rows(w)) for n, w in enumerate((a["gdn_w_out"][0], a["fox_w_out"][0]))]
        to_ple = [ahead(f"e{n}", rows(a["ple_w_proj"][n])) for n in range(2)]
        to_values = ahead("fv", [(half_rows(ring)[:, n], fox_in[n * P:(n + 1) * P, 2 * WIDTH:2 * WIDTH + HALF])
                                 for n in range(4)])
        to_attention = ahead("fa", columns(fox_in, (0, WIDTH)))
        with ExitStack() as gdn:
            sb1 = lambda n, s, d=F32: gdn.enter_context(nc.sbuf_tensor(n, s, d))
            o_t = sb1("o_t", [P, H, T])
            with ExitStack() as masks:
                sb2 = lambda n, s, d=F32: masks.enter_context(nc.sbuf_tensor(n, s, d))
                for n in ("odd_below", "above_big", "below_neg"):
                    c[n] = sb2(n, [P, P])
                c["level_mask"] = sb2("level_mask", [P, LEVELS, P // 2])
                gates = {n: sb2(f"gates_{n}", [P, NT, H]) for n in ("beta", "g", "neg_beta_eg", "k_decay", "last")}
                transpose_input(nc, a["x"], c, part_hi, part_lo, to_gdn)
                delta_net(nc, c, ring, to_gdn, to_mix[0], part_hi, part_lo, gates, gdn_in, a["gdn_dt_bias"][0],
                          a["gdn_a_log"][0], a["gdn_conv_w"][0], a["gdn_norm_g"][0], g_rows,
                          x1, o_t)
            mixer_out(nc, c, ring, to_mix[0], to_ple[0], o_t, False, a["x"][0], a["gdn_w_out"][0], a["ln_g"][0], a["ln_b"][0],
                      part_hi, part_lo, x1, "m0")
        gated_embedding(nc, c, ring, to_ple[0], to_values, x1, a["p"][0, 0], a["ple_w_gate"][0], a["ple_w_proj"][0],
                        x2, part_hi, part_lo, x2_stored, "e0")
        with ExitStack() as fox:
            gate_z = fox.enter_context(nc.sbuf_tensor("gate_z", [P, NT, WIDTH], F32))
            fox_values(nc, c, ring, to_values, to_attention, part_hi, part_lo, fox_in, a["fox_b_f"][0], c_rows, x1, gate_z)
            fox_attention(nc, c, ring, to_attention, to_mix[1], part_hi, part_lo, fox_in, a["fox_q_norm_g"][0],
                          a["fox_k_norm_g"][0], c_rows, x1, gate_z)
            mixer_out(nc, c, ring, to_mix[1], to_ple[1], gate_z, True, x2, a["fox_w_out"][0], a["ln_g"][1], a["ln_b"][1],
                      part_hi, part_lo, x1, "m1")
        gated_embedding(nc, c, ring, to_ple[1], None, x1, a["p"][1, 0], a["ple_w_gate"][1], a["ple_w_proj"][1], out[0], None, None,
                        output_stored, "e1")


_INS = ["x", "p", "ln_g", "ln_b", "ple_w_gate", "ple_w_proj", "gdn_w_in", "gdn_conv_w", "gdn_a_log", "gdn_dt_bias",
        "gdn_norm_g", "gdn_w_out", "fox_w_in", "fox_b_f", "fox_q_norm_g", "fox_k_norm_g", "fox_w_out"]


def kernel(**inputs):
    import numpy as _np
    import concourse.bacc as _bacc
    from concourse import mybir as _mybir
    from concourse.bass_utils import run_bass_kernel_spmd as _run

    nc = _bacc.Bacc("TRN2", target_bir_lowering=False, num_devices=1)
    arrays, args = {}, {}
    for name in _INS:
        a = _np.ascontiguousarray(inputs[name])
        arrays[f"in_{name}_dram"] = a
        args[name] = nc.dram_tensor(f"in_{name}_dram", a.shape, _mybir.dt.from_np(a.dtype), kind="ExternalInput").ap()
    out = nc.dram_tensor("out_0_dram", (1, T, D), F32, kind="ExternalOutput").ap()
    build_program(nc, args, out)
    r = _run(nc, [arrays], core_ids=[0])
    return r.results[0]["out_0_dram"]
```
